# Optimizing a Trainium2 kernel written in Bass

```python
import jax, jax.numpy as jnp
from jax import lax
import numpy as np

D_MODEL = 1024
BATCH = 1
SEQ = 512
DEPTH = 1

HEAD_DIM = 64
RET_HEADS = 8
SWA_Q_HEADS = 8
SWA_KV_HEADS = 2
SWA_GROUP = SWA_Q_HEADS // SWA_KV_HEADS
RET_WIDTH = RET_HEADS * HEAD_DIM
SWA_Q_WIDTH = SWA_Q_HEADS * HEAD_DIM
SWA_KV_WIDTH = SWA_KV_HEADS * HEAD_DIM
MIX_WIDTH = RET_WIDTH + SWA_Q_WIDTH
IN_SPLITS = (RET_WIDTH, RET_WIDTH, RET_WIDTH, RET_WIDTH, SWA_Q_WIDTH, SWA_KV_WIDTH, SWA_KV_WIDTH)
IN_WIDTH = sum(IN_SPLITS)
RET_CHUNK = 128
ROPE_BASE = 10000.0
WINDOW = 128
SWA_BLOCK = 128
PEER_HEADS = 8
PEER_KEYS = 128
PEER_EXPERTS = PEER_KEYS * PEER_KEYS
PEER_QDIM = 256
PEER_HALF = PEER_QDIM // 2
PEER_TOPK = 16
PEER_TOKEN_BLOCK = 128
PLE_DIM = 256
EPS = 1e-6

kernel_name = "hybrid_retention_swa_peer_block"

def rmsnorm(x, g):
    xf = x.astype(jnp.float32)
    y = xf * lax.rsqrt(jnp.mean(xf * xf, axis=-1, keepdims=True) + EPS)
    return (y * g.astype(jnp.float32)).astype(x.dtype)

def head_layernorm(x):
    xf = x.astype(jnp.float32)
    mu = jnp.mean(xf, axis=-1, keepdims=True)
    xc = xf - mu
    var = jnp.mean(xc * xc, axis=-1, keepdims=True)
    return (xc * lax.rsqrt(var + EPS)).astype(x.dtype)

def rotary(x, pos):
    d = x.shape[-1]
    half = d // 2
    freqs = ROPE_BASE ** (-jnp.arange(half, dtype=jnp.float32) / half)
    ang = pos[:, None] * freqs[None, :]
    c = jnp.cos(ang)[None, :, None, :]
    s = jnp.sin(ang)[None, :, None, :]
    x1, x2 = x[..., :half], x[..., half:]
    out = jnp.concatenate([x1 * c - x2 * s, x1 * s + x2 * c], axis=-1)
    return out.astype(x.dtype)

def retention_chunkwise(q, k, v):
    B, S, H, d = q.shape
    C = RET_CHUNK
    NC = S // C
    gamma = 1.0 - jnp.exp2(-5.0 - jnp.arange(H, dtype=jnp.float32))
    log_g = jnp.log(gamma)
    k = k * (d ** -0.5)
    qc = q.reshape(B, NC, C, H, d)
    kc = k.reshape(B, NC, C, H, d)
    vc = v.reshape(B, NC, C, H, d)
    idx = jnp.arange(C)
    rel = idx[:, None] - idx[None, :]
    dec = jnp.where(rel[None] >= 0,
                    jnp.exp(log_g[:, None, None] * jnp.maximum(rel, 0)[None].astype(jnp.float32)),
                    0.0)
    att = jnp.einsum('bnihd,bnjhd->bnhij', qc, kc) * dec[None, None]
    o_intra = jnp.einsum('bnhij,bnjhe->bnihe', att, vc)
    w_k = jnp.exp(log_g[None, :] * (C - 1 - idx)[:, None].astype(jnp.float32))
    kv = jnp.einsum('bnjhd,jh,bnjhe->bnhde', kc, w_k, vc)
    chunk_decay = jnp.exp(log_g * C)

    def step(state, kv_n):
        return state * chunk_decay[None, :, None, None] + kv_n, state

    init = jnp.zeros((B, H, d, d), dtype=kv.dtype)
    _, prev = lax.scan(step, init, jnp.moveaxis(kv, 1, 0))
    prev = jnp.moveaxis(prev, 0, 1)
    w_q = jnp.exp(log_g[None, :] * (idx + 1)[:, None].astype(jnp.float32))
    o_cross = jnp.einsum('bnihd,bnhde->bnihe', qc, prev) * w_q[None, None, :, :, None]
    return (o_intra + o_cross).reshape(B, S, H, d)

def sliding_window_sink_attention(q, k, v, sinks):
    B, S, Hq, d = q.shape
    L = SWA_BLOCK
    NB = S // L
    qb = q.reshape(B, NB, L, SWA_KV_HEADS, SWA_GROUP, d)
    kb = k.reshape(B, NB, L, SWA_KV_HEADS, d)
    vb = v.reshape(B, NB, L, SWA_KV_HEADS, d)
    pad = ((0, 0), (1, 0), (0, 0), (0, 0), (0, 0))
    kcat = jnp.concatenate([jnp.pad(kb, pad)[:, :-1], kb], axis=2)
    vcat = jnp.concatenate([jnp.pad(vb, pad)[:, :-1], vb], axis=2)
    s = jnp.einsum('bnqhgd,bnkhd->bnhgqk', qb, kcat).astype(jnp.float32) * (d ** -0.5)
    qi = jnp.arange(L)[:, None]
    ki = jnp.arange(2 * L)[None, :]
    rel = qi + L - ki
    band = (rel >= 0) & (rel < WINDOW)
    mask = band[None] & ((jnp.arange(NB) > 0)[:, None, None] | (ki >= L)[None])
    s = jnp.where(mask[None, :, None, None], s, -jnp.inf)
    sink = sinks.astype(jnp.float32).reshape(SWA_KV_HEADS, SWA_GROUP)[None, None, :, :, None, None]
    m = jnp.maximum(jnp.max(s, axis=-1, keepdims=True), sink)
    e = jnp.exp(s - m)
    pr = e / (jnp.sum(e, axis=-1, keepdims=True) + jnp.exp(sink - m))
    o = jnp.einsum('bnhgqk,bnkhd->bnqhgd', pr.astype(v.dtype), vcat)
    return o.reshape(B, S, Hq * d)

def peer_ffn(h, w_query, sub_keys, emb_u, emb_v):
    B, S, D = h.shape
    q = (h @ w_query).reshape(B, S, PEER_HEADS, 2, PEER_HALF)
    sc = jnp.einsum('bshpc,pkc->bshpk', q, sub_keys).astype(jnp.float32)
    top_s, top_i = lax.top_k(sc, PEER_TOPK)
    cand_s = top_s[..., 0, :, None] + top_s[..., 1, None, :]
    cand_i = top_i[..., 0, :, None] * PEER_KEYS + top_i[..., 1, None, :]
    cand_s = cand_s.reshape(B, S, PEER_HEADS, PEER_TOPK * PEER_TOPK)
    cand_i = cand_i.reshape(B, S, PEER_HEADS, PEER_TOPK * PEER_TOPK)
    best_s, pos = lax.top_k(cand_s, PEER_TOPK)
    expert = jnp.take_along_axis(cand_i, pos, axis=-1)
    gate = jax.nn.softmax(best_s, axis=-1).astype(h.dtype)
    T = B * S
    nblk = T // PEER_TOKEN_BLOCK
    hb = h.reshape(nblk, PEER_TOKEN_BLOCK, D)
    eb = expert.reshape(nblk, PEER_TOKEN_BLOCK, PEER_HEADS, PEER_TOPK)
    gb = gate.reshape(nblk, PEER_TOKEN_BLOCK, PEER_HEADS, PEER_TOPK)

    def block(args):
        hx, ex, gx = args
        u = emb_u[ex]
        a = jnp.einsum('td,thkd->thk', hx, u)
        act = jax.nn.gelu(a, approximate=False) * gx
        vv = emb_v[ex]
        return jnp.einsum('thk,thkd->td', act, vv)

    y = lax.map(block, (hb, eb, gb))
    return y.reshape(B, S, D)

def setup_inputs(seed: int = 0) -> dict:
    key = jax.random.key(seed)
    ks = jax.random.split(key, 16)
    f32 = jnp.float32
    nrm = lambda k, shape, scale: jax.random.normal(k, shape, f32) * scale
    return {
        "x": nrm(ks[0], (BATCH, SEQ, D_MODEL), 1.0),
        "p": nrm(ks[1], (DEPTH, BATCH, SEQ, PLE_DIM), 1.0),
        "g_mix": 1.0 + nrm(ks[2], (DEPTH, D_MODEL), 0.02),
        "w_in": nrm(ks[3], (DEPTH, D_MODEL, IN_WIDTH), D_MODEL ** -0.5),
        "q_norm": 1.0 + nrm(ks[4], (DEPTH, HEAD_DIM), 0.02),
        "k_norm": 1.0 + nrm(ks[5], (DEPTH, HEAD_DIM), 0.02),
        "sinks": nrm(ks[6], (DEPTH, SWA_Q_HEADS), 0.5),
        "w_out": nrm(ks[7], (DEPTH, MIX_WIDTH, D_MODEL), MIX_WIDTH ** -0.5),
        "g_ffn": 1.0 + nrm(ks[8], (DEPTH, D_MODEL), 0.02),
        "peer_w_query": nrm(ks[9], (DEPTH, D_MODEL, PEER_HEADS * PEER_QDIM), D_MODEL ** -0.5),
        "peer_sub_keys": nrm(ks[10], (DEPTH, 2, PEER_KEYS, PEER_HALF), PEER_HALF ** -0.5),
        "peer_u": nrm(ks[11], (DEPTH, PEER_EXPERTS, D_MODEL), D_MODEL ** -0.5),
        "peer_v": nrm(ks[12], (DEPTH, PEER_EXPERTS, D_MODEL), 0.3),
        "g_ple": 1.0 + nrm(ks[13], (DEPTH, D_MODEL), 0.02),
        "w_ple_gate": nrm(ks[14], (DEPTH, D_MODEL, D_MODEL), D_MODEL ** -0.5),
        "w_ple_proj": nrm(ks[15], (DEPTH, PLE_DIM, D_MODEL), PLE_DIM ** -0.5),
    }

def reference(x, p, g_mix, w_in, q_norm, k_norm, sinks, w_out, g_ffn,
              peer_w_query, peer_sub_keys, peer_u, peer_v, g_ple, w_ple_gate, w_ple_proj):
    B, S, _ = x.shape
    pos = jnp.arange(S, dtype=jnp.float32)
    split_pts = list(np.cumsum(IN_SPLITS)[:-1])
    for i in range(DEPTH):
        h = rmsnorm(x, g_mix[i])
        proj = h @ w_in[i]
        rq, rk, rv, rg, sq, sk, sv = jnp.split(proj, split_pts, axis=-1)
        rq = rotary(rq.reshape(B, S, RET_HEADS, HEAD_DIM), pos)
        rk = rotary(rk.reshape(B, S, RET_HEADS, HEAD_DIM), pos)
        rv = rv.reshape(B, S, RET_HEADS, HEAD_DIM)
        ro = head_layernorm(retention_chunkwise(rq, rk, rv)).reshape(B, S, RET_WIDTH)
        ro = jax.nn.silu(rg) * ro.astype(rg.dtype)
        sq = rmsnorm(sq.reshape(B, S, SWA_Q_HEADS, HEAD_DIM), q_norm[i])
        sk = rmsnorm(sk.reshape(B, S, SWA_KV_HEADS, HEAD_DIM), k_norm[i])
        sv = sv.reshape(B, S, SWA_KV_HEADS, HEAD_DIM)
        so = sliding_window_sink_attention(sq, sk, sv, sinks[i])
        mixed = jnp.concatenate([ro, so.astype(ro.dtype)], axis=-1)
        x = x + mixed @ w_out[i]
        h = rmsnorm(x, g_ffn[i])
        x = x + peer_ffn(h, peer_w_query[i], peer_sub_keys[i], peer_u[i], peer_v[i]).astype(x.dtype)
        gate = jax.nn.sigmoid(rmsnorm(x, g_ple[i]) @ w_ple_gate[i])
        x = x + gate * (p[i] @ w_ple_proj[i])
    return x


_drawn_inputs = setup_inputs


def setup_inputs(seed=0):
    import zlib

    import numpy as np

    out = dict(_drawn_inputs(seed))
    spreads = {}
    factors = {'q_norm': 8.0, 'k_norm': 7.856, 'sinks': 64.0, 'g_ffn': 3.023, 'g_ple': 49.04}
    for name, (base, spread) in spreads.items():
        noise = np.random.default_rng([zlib.crc32(name.encode()), seed]).standard_normal(out[name].shape)
        drawn = base * np.exp(spread * noise) if base else spread * noise
        out[name] = __import__('jax').numpy.asarray(drawn.astype(out[name].dtype))
    for name, factor in factors.items():
        out[name] = (out[name] * factor).astype(out[name].dtype)
    return out
```

```python
from contextlib import ExitStack

import concourse.bass as bass
from concourse import mybir

F32 = mybir.dt.float32
F32R = mybir.dt.float32r
F16 = mybir.dt.float16
U32 = mybir.dt.uint32
I32 = mybir.dt.int32
ALU = mybir.AluOpType
ACT = mybir.ActivationFunctionType
AX = mybir.AxisListType

P = 128
D = 1024
SEQ = 512
TB = SEQ // P
KC = D // P
HD = 64
RH = 8
QH = 8
KVH = 2
RW = RH * HD
IN_W = 4 * RW + QH * HD + 2 * KVH * HD
RQ, RK, RV, RG, SQ, SK, SV = 0, RW, 2 * RW, 3 * RW, 4 * RW, 4 * RW + QH * HD, 4 * RW + (QH + KVH) * HD
IN_PANELS = 8
IN_PW = IN_W // IN_PANELS
BANK = 512
PH = 8
KEYS = 128
TOPK = 16
HALVES = 2 * PH
PICKS = PH * TOPK
TILES = KEYS
GROUP = 4
PLE = 256
EPS = 1e-6
NEG = -3.0e38
GATE_SCALE = 4096.0
TCH = 32
GST = 64


class Chain:

    def __init__(self, eng, sem, settled=None):
        self.eng, self.sem, self.settled, self.n, self.off = eng, sem, settled, 0, 0

    def step(self, ins):
        ins.then_inc(self.sem, 1)
        self.n += 1

    def settle(self):
        self.eng.wait_ge(self.sem, self.off + self.n)
        if self.settled is not None:
            self.eng.sem_inc(self.settled, 1)


def split_product(pe, out, pairs):
    last = None
    for n, ((ah, al), (bh, bl)) in enumerate(pairs):
        pe.matmul(out, ah, bh, start=(n == 0), stop=False)
        pe.matmul(out, ah, bl, start=False, stop=False)
        last = pe.matmul(out, al, bh, start=False, stop=(n == len(pairs) - 1))
    return last


def to_transposed_parts(nc, sem, psum, tag, src, gain, hT_hi, hT_lo, ident, normalize):
    with ExitStack() as ctx:
        sumsq = ctx.enter_context(nc.sbuf_tensor(f"{tag}_sumsq", [P, TB], F32))
        mean = ctx.enter_context(nc.sbuf_tensor(f"{tag}_mean", [P, TB], F32))
        inv = ctx.enter_context(nc.sbuf_tensor(f"{tag}_inv", [P, TB], F32))
        rstd = ctx.enter_context(nc.sbuf_tensor(f"{tag}_rstd", [P, TB], F32))
        square = ctx.enter_context(nc.sbuf_tensor(f"{tag}_square", [P, D], F32))
        xn = ctx.enter_context(nc.sbuf_tensor(f"{tag}_xn", [P, TB, D], F32)) if normalize else src
        sq_done, inv_done, rstd_done = sem(f"{tag}_sq_done"), sem(f"{tag}_inv_done"), sem(f"{tag}_rstd_done")
        dve_steps, xn_done = sem(f"{tag}_dve_steps"), sem(f"{tag}_xn_done")
        transposed, hi_done = sem(f"{tag}_transposed"), sem(f"{tag}_hi_done")
        block = ctx.enter_context(nc.Block())

        @block.scalar
        def _(act):
            if normalize:
                for tb in range(TB):
                    if tb:
                        act.wait_ge(sq_done, tb)
                    act.activation(square[:, :], src[:, tb, :], ACT.Square,
                                   accum_out=sumsq[:, tb:tb + 1]).then_inc(sq_done, 1)
                act.wait_ge(inv_done, 1)
                act.activation(rstd[:, :], inv[:, :], ACT.Sqrt).then_inc(rstd_done, 1)
            for kc in range(KC):
                act.wait_ge(transposed, kc + 1)
                act.activation(hT_hi[:, kc, :], psum[kc][:, :], ACT.Copy,
                               scale=gain[:, kc:kc + 1] if normalize else 1.0).then_inc(hi_done, 1)

        @block.vector
        def _(dve):
            if normalize:
                chain = Chain(dve, dve_steps)
                dve.wait_ge(sq_done, TB)
                chain.step(dve.tensor_scalar(mean[:, :], sumsq[:, :], 1.0 / D, EPS, ALU.mult, ALU.add))
                chain.settle()
                dve.reciprocal(inv[:, :], mean[:, :]).then_inc(inv_done, 1)
                dve.wait_ge(rstd_done, 1)
                for tb in range(TB):
                    dve.tensor_scalar(xn[:, tb, :], src[:, tb, :], rstd[:, tb:tb + 1], None,
                                      ALU.mult).then_inc(xn_done, 1)
            for kc in range(KC):
                dve.wait_ge(hi_done, kc + 1)
                dve.scalar_tensor_tensor(out=hT_lo[:, kc, :], in0=psum[kc][:, :],
                                         scalar=gain[:, kc:kc + 1] if normalize else 1.0,
                                         in1=hT_hi[:, kc, :].bitcast(F32), op0=ALU.mult, op1=ALU.subtract)\
                   .then_inc(dve_steps, 1)

        @block.tensor
        def _(pe):
            if normalize:
                pe.wait_ge(xn_done, TB)
            for kc in range(KC):
                for tb in range(TB):
                    last = pe.transpose(psum[kc][:, tb * P:(tb + 1) * P], xn[:, tb, kc * P:(kc + 1) * P],
                                        ident[:, :])
                last.then_inc(transposed, 1)


def project(nc, sem, psum, tag, panels, n_panels, width, chunks, hT_hi, hT_lo, evacuate, transposed=False):
    with ExitStack() as ctx:
        raw = [ctx.enter_context(nc.sbuf_tensor(f"{tag}_raw{i}", [P, chunks, width], F32)) for i in range(2)]
        w_hi = [ctx.enter_context(nc.sbuf_tensor(f"{tag}_whi{i}", [P, chunks, width], F32R)) for i in range(2)]
        w_lo = [ctx.enter_context(nc.sbuf_tensor(f"{tag}_wlo{i}", [P, chunks, width], F32R)) for i in range(2)]
        loaded = [sem(f"{tag}_loaded{i}") for i in range(2)]
        hi_done, lo_done = sem(f"{tag}_hi_done"), sem(f"{tag}_lo_done")
        panel_used, bank_full, bank_free = sem(f"{tag}_panel_used"), sem(f"{tag}_bank_full"), sem(f"{tag}_bank_free")
        units = 4
        n_pairs = n_panels // 2
        block = ctx.enter_context(nc.Block())

        @block.sync
        def _(sp):
            sp.sem_inc(lo_done, 2)
            with sp.Fori(0, n_pairs) as pair:
                for i in range(2):
                    sp.wait_ge(lo_done, pair * 2 + i + 1)
                    sp.dma_start(raw[i][:, :, :], panels[bass.ds(pair * 2 + i, 1), :, :, :]
                                 .rearrange("o p c n -> (o p) c n")).then_inc(loaded[i], 16)

        @block.scalar
        def _(act):
            act.sem_inc(panel_used, 2)
            with act.Fori(0, n_pairs) as pair:
                for i in range(2):
                    act.wait_ge(loaded[i], pair * 16 + 16)
                    act.wait_ge(panel_used, pair * 2 + i + 1)
                    act.activation(w_hi[i][:, :, :], raw[i][:, :, :], ACT.Copy).then_inc(hi_done, 1)

        @block.vector
        def _(dve):
            def split(pair, i):
                dve.wait_ge(hi_done, pair * 2 + i + 1)
                dve.tensor_tensor(w_lo[i][:, :, :], raw[i][:, :, :], w_hi[i][:, :, :].bitcast(F32),
                                  ALU.subtract).then_inc(lo_done, 1)

            dve.sem_inc(bank_free, 2 * units)
            with dve.Fori(0, n_pairs) as pair:
                for i in range(2):
                    split(pair, i)
                for i in range(2):
                    for u in range(units):
                        dve.wait_ge(bank_full, pair * 2 * units + i * units + u + 1)
                        evacuate(dve, pair, i, u, psum[i * units + u][:, 0:SEQ if transposed else width])\
                            .then_inc(bank_free, 1)

        @block.tensor
        def _(pe):
            with pe.Fori(0, n_pairs) as pair:
                for i in range(2):
                    pe.wait_ge(lo_done, pair * 2 + i + 3)
                    for u in range(units):
                        pe.wait_ge(bank_free, pair * 2 * units + i * units + u + 1)
                        if transposed:
                            pairs = [((w_hi[i][:, c, u * P:(u + 1) * P], w_lo[i][:, c, u * P:(u + 1) * P]),
                                      (hT_hi[:, c, :], hT_lo[:, c, :])) for c in range(chunks)]
                            out = psum[i * units + u][:, :]
                        else:
                            pairs = [((hT_hi[:, c, u * P:(u + 1) * P], hT_lo[:, c, u * P:(u + 1) * P]),
                                      (w_hi[i][:, c, :], w_lo[i][:, c, :])) for c in range(chunks)]
                            out = psum[i * units + u][:, 0:width]
                        last = split_product(pe, out, pairs)
                        last.then_inc(bank_full, 1)
                    pe.wait_ge(bank_full, pair * 2 * units + i * units + units)
                    pe.sem_inc(panel_used, 1)


def load_all(nc, sem, tag, pairs):
    done = sem(f"{tag}_loaded")
    with nc.Block() as block:
        @block.sync
        def _(sp):
            for dst, src in pairs:
                sp.dma_start(dst, src).then_inc(done, 16)
            sp.wait_ge(done, 16 * len(pairs))


def hybrid_layer(nc, x, p_t, g_mix, w_in, q_norm, k_norm, sinks, w_out, g_ffn, w_query, keys_t, peer_u, peer_v,
                 g_ple, w_gate, w_ple, ident_c, cos_c, sin_c, decay_c, wq_c, wk_c, chunk_c, mask_c, out):
    gates_dram = nc.dram_tensor("gates", [TILES, P, SEQ], F32).ap()
    with ExitStack() as ctx:
        def sb(name, shape, dt=F32):
            return ctx.enter_context(nc.sbuf_tensor(name, shape, dt))

        def sem(name):
            return ctx.enter_context(nc.semaphore(name))

        psum = [ctx.enter_context(nc.psum_tensor(f"bank{i}", [P, BANK], F32)) for i in range(8)]
        res = sb("res", [P, TB, D])
        hT_hi = sb("hT_hi", [P, KC, SEQ], F32R)
        hT_lo = sb("hT_lo", [P, KC, SEQ], F32R)
        ident = sb("ident", [P, P])
        gains = sb("gains", [P, 3, KC])

        load_all(nc, sem, "start", [
            (res[:, :, :], x.rearrange("(t p) d -> p t d", p=P)),
            (ident[:, :], ident_c), (gains[:, 0, :], g_mix), (gains[:, 1, :], g_ffn), (gains[:, 2, :], g_ple)])

        to_transposed_parts(nc, sem, psum, "mix", res, gains[:, 0, :], hT_hi, hT_lo, ident, True)
        with ExitStack() as mixer:
            proj = mixer.enter_context(nc.sbuf_tensor("proj", [P, TB, IN_W], F32))

            def keep_proj(dve, pair, i, tb, bank):
                return dve.tensor_copy(proj[:, tb, bass.ds((pair * 2 + i) * IN_PW, IN_PW)], bank)

            project(nc, sem, psum, "win", w_in, IN_PANELS, IN_PW, KC, hT_hi, hT_lo, keep_proj)
            attention(nc, sem, psum, proj, ident, hT_hi, hT_lo, q_norm, k_norm, sinks,
                      cos_c, sin_c, decay_c, wq_c, wk_c, chunk_c, mask_c)

        def add_to_res(dve, pair, i, tb, bank):
            at = res[:, tb, i * BANK:(i + 1) * BANK]
            return dve.tensor_tensor(at, bank, at, ALU.add)

        project(nc, sem, psum, "wout", w_out, 2, BANK, KC, hT_hi, hT_lo, add_to_res)

        to_transposed_parts(nc, sem, psum, "ffn", res, gains[:, 1, :], hT_hi, hT_lo, ident, True)
        with ExitStack() as peer:
            picks = [peer.enter_context(nc.sbuf_tensor(n, [P, TB, PICKS], F32))
                     for n in ("pick_i1", "pick_i2", "pick_gate")]
            with ExitStack() as route:
                qT = route.enter_context(nc.sbuf_tensor("qT", [P, HALVES, SEQ], F32))

                def keep_q(dve, pair, i, u, bank):
                    return dve.tensor_copy(qT[:, bass.ds(pair * 8 + i * 4 + u, 1), :]
                                           .rearrange("p o t -> p (o t)"), bank)

                project(nc, sem, psum, "wqry", w_query, 4, BANK, KC, hT_hi, hT_lo, keep_q, transposed=True)
                choose_experts(nc, sem, psum, qT, keys_t, picks)
            spread_gates(nc, sem, psum, picks, ident, gates_dram)
        evaluate_experts(nc, sem, psum, res, hT_hi, hT_lo, peer_u, peer_v, gates_dram)

        to_transposed_parts(nc, sem, psum, "ple", res, gains[:, 2, :], hT_hi, hT_lo, ident, True)
        add_embedding(nc, sem, psum, res, hT_hi, hT_lo, p_t, w_gate, w_ple, out)


def attention(nc, sem, psum, proj, ident, hT_hi, hT_lo, q_norm, k_norm, sinks,
              cos_c, sin_c, decay_c, wq_c, wk_c, chunk_c, mask_c):
    PAIRS = RH // 2
    with ExitStack() as ctx:
        def sb(name, shape, dt=F32):
            return ctx.enter_context(nc.sbuf_tensor(name, shape, dt))

        mixed = sb("mixed", [P, TB, D])
        rqT, rkT, rqwT = (sb(n, [P, PAIRS, SEQ]) for n in ("rqT", "rkT", "rqwT"))
        sqT = sb("sqT", [P, PAIRS, SEQ])
        skT = sb("skT", [P, KVH, SEQ])
        kw = sb("kw", [P, TB, RW])
        mask = sb("mask", [P, 2 * P])
        decay = sb("decay", [P, RH, P])
        chunk = sb("chunk", [P, PAIRS])
        sink = sb("sink", [P, QH])
        small = sb("small", [P, 8, TB * (QH + KVH)])
        prepare(nc, sem, psum, proj, ident, q_norm, k_norm, cos_c, sin_c, wq_c, wk_c,
                rqT, rkT, rqwT, sqT, skT, kw, small,
                [(mask[:, :], mask_c), (decay[:, :, :], decay_c), (chunk[:, :], chunk_c), (sink[:, :], sinks)])
        retention(nc, sem, psum, proj, rqT, rkT, rqwT, kw, decay, chunk, mixed)
        sliding_window(nc, sem, psum, proj, sqT, skT, ident, mask, sink, mixed)
        to_transposed_parts(nc, sem, psum, "mixed", mixed, None, hT_hi, hT_lo, ident, False)


def prepare(nc, sem, psum, proj, ident, q_norm, k_norm, cos_c, sin_c, wq_c, wk_c,
            rqT, rkT, rqwT, sqT, skT, kw, small, loads):
    PAIRS = RH // 2
    NH = QH + KVH
    HALF = HD // 2
    with ExitStack() as ctx:
        def sb(name, shape, dt=F32):
            return ctx.enter_context(nc.sbuf_tensor(name, shape, dt))

        cos, sin = sb("cos", [P, TB, HALF]), sb("sin", [P, TB, HALF])
        wq = sb("wq", [P, PAIRS, P])
        wk = sb("wk", [P, RH])
        qn, kn = sb("qn", [P, 1]), sb("kn", [P, 1])
        rot = sb("rot", [P, TB, 2 * RH, HD])
        t1, t2 = sb("t1", [P, TB, 2 * RH, HALF]), sb("t2", [P, TB, 2 * RH, HALF])
        skn = sb("skn", [P, TB, KVH, 2, HD])
        loaded = sem("prep_loaded")
        steps, inv_ready, rstd_ready = sem("prep_steps"), sem("prep_inv"), sem("prep_rstd")
        rot_ready, norm_ready = sem("rot_ready"), sem("norm_ready")
        tr_full, tr_free, tr_evac = sem("tr_full"), sem("tr_free"), sem("tr_evac")
        all_loads = loads + [(cos[:, :, :], cos_c), (sin[:, :, :], sin_c), (wq[:, :, :], wq_c), (wk[:, :], wk_c),
                             (qn[:, :], q_norm), (kn[:, :], k_norm)]
        block = ctx.enter_context(nc.Block())

        @block.sync
        def _(sp):
            for dst, src in all_loads:
                sp.dma_start(dst, src).then_inc(loaded, 16)

        sqk = proj[:, :, SQ:SV].rearrange("p t (h d) -> p t h d", d=HD)
        ssq, mean, inv, rstd = (small[:, i, :].rearrange("p (t h) -> p t h", t=TB) for i in range(4))

        def wide(a, n):
            return a.unsqueeze(3).broadcast_to([P, a.shape[1], a.shape[2], n])

        @block.vector
        def _(dve):
            chain = Chain(dve, steps)
            sq = rot[:, :, 0:NH, :]
            chain.step(dve.tensor_tensor(sq, sqk, sqk, ALU.mult))
            chain.settle()
            chain.step(dve.tensor_reduce(ssq, sq, AX.X, ALU.add))
            chain.settle()
            chain.step(dve.tensor_scalar(mean, ssq, 1.0 / HD, EPS, ALU.mult, ALU.add))
            chain.settle()
            dve.reciprocal(inv, mean).then_inc(inv_ready, 1)
            dve.wait_ge(loaded, 16 * len(all_loads))
            qk = proj[:, :, RQ:RV].rearrange("p t (h d) -> p t h d", d=HD)
            x1, x2 = qk[:, :, :, 0:HALF], qk[:, :, :, HALF:HD]
            c = cos[:, :, :].unsqueeze(2).broadcast_to([P, TB, 2 * RH, HALF])
            s = sin[:, :, :].unsqueeze(2).broadcast_to([P, TB, 2 * RH, HALF])
            for part, (cx, sx, op) in enumerate(((x1, x2, ALU.subtract), (x2, x1, ALU.add))):
                chain.step(dve.tensor_tensor(t1[:, :, :, :], cx, c, ALU.mult))
                chain.step(dve.tensor_tensor(t2[:, :, :, :], sx, s, ALU.mult))
                chain.settle()
                chain.step(dve.tensor_tensor(rot[:, :, :, part * HALF:(part + 1) * HALF],
                                             t1[:, :, :, :], t2[:, :, :, :], op))
                chain.settle()
            dve.sem_inc(rot_ready, 1)
            chain.step(dve.tensor_tensor(kw[:, :, :].rearrange("p t (h d) -> p t h d", d=HD), rot[:, :, RH:2 * RH, :],
                                         wk[:, :].unsqueeze(1).unsqueeze(3).broadcast_to([P, TB, RH, HD]), ALU.mult))
            dve.wait_ge(rstd_ready, 1)
            for tb in range(TB):
                q_at = sqk[:, tb, 0:QH, :]
                chain.step(dve.tensor_tensor(q_at, q_at, rstd[:, tb, 0:QH].unsqueeze(2).broadcast_to([P, QH, HD]),
                                             ALU.mult))
            for twice in range(2):
                chain.step(dve.tensor_tensor(skn[:, :, :, twice, :], sqk[:, :, QH:NH, :], wide(rstd[:, :, QH:NH], HD),
                                             ALU.mult))
            chain.settle()
            dve.sem_inc(norm_ready, 1)
            for pair in range(PAIRS):
                dve.wait_ge(tr_evac, pair + 1)
                chain.step(dve.tensor_tensor(rqwT[:, pair, :].rearrange("p (t i) -> p t i", t=TB),
                                             rqT[:, pair, :].rearrange("p (t i) -> p t i", t=TB),
                                             wq[:, pair, :].unsqueeze(1).broadcast_to([P, TB, P]), ALU.mult))

        jobs = []
        for part, dst in ((0, rqT), (1, rkT)):
            for pair in range(PAIRS):
                jobs.append((lambda tb, h=part * RH + 2 * pair: rot[:, tb, h:h + 2, :].rearrange("p h d -> p (h d)"),
                             dst[:, pair, :], None))
        for pair in range(PAIRS):
            jobs.append((lambda tb, c=SQ + pair * P: proj[:, tb, c:c + P], sqT[:, pair, :], qn))
        for g in range(KVH):
            jobs.append((lambda tb, g=g: skn[:, tb, g, :, :].rearrange("p w d -> p (w d)"), skT[:, g, :], kn))

        @block.tensor
        def _(pe):
            for n, (source, _, gain) in enumerate(jobs):
                if n == 0:
                    pe.wait_ge(rot_ready, 1)
                if n == 2 * PAIRS:
                    pe.wait_ge(norm_ready, 1)
                if n >= 8:
                    pe.wait_ge(tr_evac, n - 7)
                for tb in range(TB):
                    last = pe.transpose(psum[n % 8][:, tb * P:(tb + 1) * P], source(tb), ident[:, :])
                last.then_inc(tr_full, 1)

        @block.scalar
        def _(act):
            act.wait_ge(inv_ready, 1)
            act.activation(rstd, inv, ACT.Sqrt).then_inc(rstd_ready, 1)
            for n, (_, dst, gain) in enumerate(jobs):
                act.wait_ge(tr_full, n + 1)
                if n == 0:
                    act.wait_ge(loaded, 16 * len(all_loads))
                act.activation(dst, psum[n % 8][:, :], ACT.Copy,
                               scale=gain[:, 0:1] if gain is not None else 1.0).then_inc(tr_evac, 1)


def retention(nc, sem, psum, proj, rqT, rkT, rqwT, kw, decay, chunk, mixed):
    PAIRS = RH // 2
    HH = RH // 2
    with ExitStack() as ctx:
        def sb(name, shape, dt=F32):
            return ctx.enter_context(nc.sbuf_tensor(name, shape, dt))

        attn = sb("attn", [P, RH, P])
        state = sb("state", [P, PAIRS, 2, HD])
        ret = sb("ret", [P, TB, RH, HD])
        sq = sb("ret_sq", [P, TB, RH, HD])
        gate = sb("ret_gate", [P, TB, RW])
        stats = sb("ret_stats", [P, 5, TB * RH])
        score_full, attn_done, out_full, kv_full = sem("score_full"), sem("attn_done"), sem("out_full"), sem("kv_full")
        state_done, out_copied, steps = sem("state_done"), sem("out_copied"), sem("ret_steps")
        silu_done, inv_done, root_done = sem("silu_done"), sem("ret_inv"), sem("ret_root")
        block = ctx.enter_context(nc.Block())

        def half(h):
            return slice((h % 2) * HD, (h % 2 + 1) * HD)

        @block.tensor
        def _(pe):
            for n in range(TB):
                t = slice(n * P, (n + 1) * P)
                for b in range(2):
                    if n:
                        pe.wait_ge(attn_done, 2 * (n - 1) + b + 1)
                    for pair in range(PAIRS):
                        last = pe.matmul(psum[b][:, pair * P:(pair + 1) * P], rkT[half(b), pair, t],
                                         rqT[half(b), pair, t], start=True, stop=True)
                    last.then_inc(score_full, 1)
                if n < TB - 1:
                    if n:
                        pe.wait_ge(state_done, n)
                    for pair in range(PAIRS):
                        last = pe.matmul(psum[2][:, pair * P:(pair + 1) * P], kw[:, n, pair * P:(pair + 1) * P],
                                         proj[:, n, RV + pair * P:RV + (pair + 1) * P], start=True, stop=True)
                    last.then_inc(kv_full, 1)
                if n >= 2:
                    pe.wait_ge(out_copied, n - 1)
                pe.wait_ge(attn_done, 2 * n + 2)
                if n:
                    pe.wait_ge(state_done, n)
                for h in range(RH):
                    o = psum[4 + n % 2][:, h * HD:(h + 1) * HD]
                    last = pe.matmul(o, attn[:, h % 2 * PAIRS + h // 2, :], proj[:, n, RV + h * HD:RV + (h + 1) * HD],
                                     start=True, stop=(n == 0))
                    if n:
                        last = pe.matmul(o, rqwT[:, h // 2, t], state[:, h // 2, h % 2, :],
                                         start=False, stop=True)
                last.then_inc(out_full, 1)

        @block.vector
        def _(dve):
            chain = Chain(dve, steps)
            chain.step(dve.memset(state[:, :, :, :], 0.0))
            chain.settle()
            for n in range(TB):
                for b in range(2):
                    dve.wait_ge(score_full, 2 * n + b + 1)
                    if n:
                        dve.wait_ge(out_full, n)
                    dve.tensor_tensor(attn[:, b * HH:(b + 1) * HH, :].rearrange("p h i -> p (h i)"), psum[b][:, :],
                                      decay[:, b * HH:(b + 1) * HH, :].rearrange("p h i -> p (h i)"),
                                      ALU.mult).then_inc(attn_done, 1)
                if n < TB - 1:
                    dve.wait_ge(kv_full, n + 1)
                    if n:
                        dve.wait_ge(out_full, n + 1)
                    for par in range(2):
                        rows = slice(par * HD, (par + 1) * HD)
                        kv = psum[2][rows, :].rearrange("p (a c) -> p a c", a=PAIRS)[:, :, par * HD:(par + 1) * HD]
                        if n:
                            for pair in range(PAIRS):
                                last = dve.scalar_tensor_tensor(
                                    out=state[rows, pair, par, :], in0=state[rows, pair, par, :], scalar=chunk[rows, pair:pair + 1],
                                    in1=kv[:, pair, :], op0=ALU.mult, op1=ALU.add)
                                chain.step(last)
                        else:
                            chain.step(dve.tensor_copy(state[rows, :, par, :], kv))
                    chain.settle()
                    dve.sem_inc(state_done, 1)
            total, mean, ssq, var, inv = (stats[:, i, :].rearrange("p (t h) -> p t h", t=TB) for i in range(5))
            dve.wait_ge(out_copied, TB)

            def flat(a):
                return a.rearrange("p t h -> p (t h)")

            r3 = ret[:, :, :, :].rearrange("p t h d -> p (t h) d")
            s3 = sq[:, :, :, :].rearrange("p t h d -> p (t h) d")
            chain.step(dve.tensor_reduce(flat(total), r3, AX.X, ALU.add))
            chain.settle()
            chain.step(dve.tensor_scalar(flat(mean), flat(total), 1.0 / HD, None, ALU.mult))
            chain.settle()
            chain.step(dve.tensor_tensor(r3, r3, flat(mean).unsqueeze(2).broadcast_to([P, TB * RH, HD]), ALU.subtract))
            chain.settle()
            chain.step(dve.tensor_tensor(s3, r3, r3, ALU.mult))
            chain.settle()
            chain.step(dve.tensor_reduce(flat(ssq), s3, AX.X, ALU.add))
            chain.settle()
            chain.step(dve.tensor_scalar(flat(var), flat(ssq), 1.0 / HD, EPS, ALU.mult, ALU.add))
            chain.settle()
            dve.reciprocal(flat(inv), flat(var)).then_inc(inv_done, 1)
            dve.wait_ge(root_done, 1)
            chain.step(dve.tensor_tensor(r3, r3, flat(total).unsqueeze(2).broadcast_to([P, TB * RH, HD]), ALU.mult))
            chain.settle()
            dve.wait_ge(silu_done, 1)
            chain.step(dve.tensor_tensor(mixed[:, :, 0:RW], ret[:, :, :, :].rearrange("p t h d -> p t (h d)"),
                                         gate[:, :, :], ALU.mult))

        @block.scalar
        def _(act):
            for n in range(TB):
                act.wait_ge(out_full, n + 1)
                act.activation(ret[:, n, :, :].rearrange("p h d -> p (h d)"), psum[4 + n % 2][:, :],
                               ACT.Copy).then_inc(out_copied, 1)
            act.activation(gate[:, :, :], proj[:, :, RG:SQ], ACT.Silu).then_inc(silu_done, 1)
            act.wait_ge(inv_done, 1)
            act.activation(stats[:, 0, :], stats[:, 4, :], ACT.Sqrt).then_inc(root_done, 1)


def sliding_window(nc, sem, psum, proj, sqT, skT, ident, mask, sink, mixed):
    SCALE = float(HD) ** -0.5
    with ExitStack() as ctx:
        def sb(name, shape, dt=F32):
            return ctx.enter_context(nc.sbuf_tensor(name, shape, dt))

        masked = sb("masked", [P, QH, 2 * P])
        prob = sb("prob", [P, QH, 2 * P])
        probT = sb("probT", [P, QH, 2, P])
        st = sb("swa_stats", [P, 8, QH])
        top, m, negm, sink_gap, sink_e, row_sum, den, rden = (st[:, i, :] for i in range(8))
        s_full, s_read, negm_ready, exp_done = sem("s_full"), sem("s_read"), sem("negm_ready"), sem("exp_done")
        pt_full, pt_copied, o_full, o_done, steps = (sem("pt_full"), sem("pt_copied"), sem("o_full"),
                                                     sem("o_done"), sem("swa_steps"))
        block = ctx.enter_context(nc.Block())
        blocks_of = [1] + [2] * (TB - 1)
        pt_banks = [0]
        for n in range(TB):
            pt_banks.append(pt_banks[-1] + 2 * blocks_of[n])

        @block.tensor
        def _(pe):
            for n in range(TB):
                nb = blocks_of[n]
                for b in range(4):
                    if n:
                        pe.wait_ge(s_read, 4 * (n - 1) + b + 1)
                    for i in range(2):
                        h = b // 2 * 4 + b % 2 + 2 * i
                        half = slice((h % 2) * HD, (h % 2 + 1) * HD)
                        last = pe.matmul(psum[b][:, i * 256:i * 256 + nb * P],
                                         sqT[half, h // 2, n * P:(n + 1) * P],
                                         skT[half, h // (QH // KVH), (n + 1 - nb) * P:(n + 1) * P],
                                         start=True, stop=True)
                    last.then_inc(s_full, 1)
                done = pt_banks[n]
                for q in range(2 * nb):
                    if done + q >= 2:
                        pe.wait_ge(pt_copied, done + q - 1)
                    for k in range(4):
                        h, kb = (4 * q + k) // nb, (4 * q + k) % nb
                        pe.wait_ge(exp_done, QH * n + h + 1)
                        last = pe.transpose(psum[4 + (done + q) % 2][:, k * P:(k + 1) * P],
                                            prob[:, h, kb * P:(kb + 1) * P], ident[:, :])
                    last.then_inc(pt_full, 1)
                pe.wait_ge(pt_copied, pt_banks[n + 1])
                if n >= 1:
                    pe.wait_ge(o_done, n)
                for h in range(QH):
                    for kb in range(nb):
                        vb = n + 1 - nb + kb
                        vc = SV + (h // (QH // KVH)) * HD
                        last = pe.matmul(psum[6][:, h * HD:(h + 1) * HD], probT[:, h, kb, :],
                                         proj[:, vb, vc:vc + HD], start=(kb == 0), stop=(kb == nb - 1))
                last.then_inc(o_full, 1)

        @block.vector
        def _(dve):
            chain = Chain(dve, steps)
            for n in range(TB):
                nb = blocks_of[n]
                if n:
                    dve.wait_ge(exp_done, QH * n)
                for b in range(4):
                    dve.wait_ge(s_full, 4 * n + b + 1)
                    h0 = b // 2 * 4 + b % 2
                    dve.tensor_tensor(masked[:, h0:h0 + 3:2, 0:nb * P],
                                      psum[b][:, :].rearrange("p (h k) -> p h k", h=2)[:, :, 0:nb * P],
                                      mask[:, 2 * P - nb * P:2 * P].unsqueeze(1).broadcast_to([P, 2, nb * P]),
                                      ALU.add).then_inc(s_read, 1)
                dve.wait_ge(s_read, 4 * n + 4)
                chain.step(dve.tensor_reduce(top, masked[:, :, 0:nb * P], AX.X, ALU.max))
                chain.settle()
                chain.step(dve.scalar_tensor_tensor(out=m, in0=top, scalar=SCALE, in1=sink[:, :],
                                                    op0=ALU.mult, op1=ALU.max))
                chain.settle()
                chain.step(dve.tensor_scalar(negm, m, -1.0, None, ALU.mult))
                chain.step(dve.tensor_tensor(sink_gap, sink[:, :], m, ALU.subtract))
                chain.settle()
                dve.sem_inc(negm_ready, 1)
                dve.wait_ge(exp_done, QH * (n + 1))
                chain.step(dve.tensor_tensor(den, row_sum, sink_e, ALU.add))
                chain.settle()
                chain.step(dve.reciprocal(rden, den))
                chain.settle()
                dve.wait_ge(o_full, n + 1)
                dve.tensor_tensor(mixed[:, n, RW:].rearrange("p (h d) -> p h d", d=HD),
                                  psum[6][:, :].rearrange("p (h d) -> p h d", d=HD),
                                  rden.unsqueeze(2).broadcast_to([P, QH, HD]), ALU.mult).then_inc(o_done, 1)

        @block.scalar
        def _(act):
            for n in range(TB):
                nb = blocks_of[n]
                act.wait_ge(negm_ready, n + 1)
                act.activation(sink_e, sink_gap, ACT.Exp)
                for h in range(QH):
                    act.activation(prob[:, h, 0:nb * P], masked[:, h, 0:nb * P], ACT.Exp, bias=negm[:, h:h + 1],
                                   scale=SCALE, accum_out=row_sum[:, h:h + 1]).then_inc(exp_done, 1)
                flat = probT[:, :, 0:nb, :]
                for q in range(2 * nb):
                    act.wait_ge(pt_full, pt_banks[n] + q + 1)
                    if n and q == 0:
                        act.wait_ge(o_full, n)
                    heads = 4 // nb
                    act.activation(flat[:, q * heads:(q + 1) * heads, :, :],
                                   psum[4 + (pt_banks[n] + q) % 2][:, :].rearrange("p (h k i) -> p h k i", h=heads, k=nb),
                                   ACT.Copy).then_inc(pt_copied, 1)


def choose_experts(nc, sem, psum, qT, keys_t, picks):
    pick_i1, pick_i2, pick_gate = picks
    with ExitStack() as ctx:
        def sb(name, shape, dt=F32):
            return ctx.enter_context(nc.sbuf_tensor(name, shape, dt))

        keys = sb("keys", [P, 2, KEYS])
        top_s = sb("top_s", [P, HALVES, TOPK])
        top_i = sb("top_i", [P, HALVES, TOPK], U32)
        top_f = sb("top_f", [P, HALVES, TOPK])
        rest = sb("rest", [P, HALVES, KEYS])
        cand = sb("cand", [P, PH, TOPK, TOPK])
        crest = sb("crest", [P, PH, TOPK * TOPK])
        best = sb("best", [P, PH, TOPK])
        pos = sb("pos", [P, PH, TOPK], U32)
        pos_ab = sb("pos_ab", [P, 2, PICKS], U32)
        pos_f = sb("pos_f", [P, 2, PICKS])
        iota_i = sb("iota16_i", [P, TOPK], I32)
        iota = sb("iota16", [P, TOPK])
        hit = [sb(f"hit{i}", [P, PICKS, TOPK]) for i in range(2)]
        gap, expd = sb("gap", [P, PH, TOPK]), sb("expd", [P, PH, TOPK])
        total, inv = sb("gate_total", [P, PH]), sb("gate_inv", [P, PH])
        loaded, iota_done, sc_full, sc_free = sem("keys_loaded"), sem("iota_done"), sem("sc_full"), sem("sc_free")
        gap_ready, exp_ready, steps = sem("gap_ready"), sem("exp_ready"), sem("topk_steps")
        block = ctx.enter_context(nc.Block())

        @block.sync
        def _(sp):
            sp.dma_start(keys[:, :, :], keys_t).then_inc(loaded, 16)

        @block.gpsimd
        def _(pool):
            pool.iota(iota_i[:, :], pattern=[[1, TOPK]], base=0, channel_multiplier=0).then_inc(iota_done, 1)

        @block.tensor
        def _(pe):
            pe.wait_ge(loaded, 16)
            for tb in range(TB):
                if tb:
                    pe.wait_ge(sc_free, tb)
                for hp in range(HALVES):
                    last = pe.matmul(psum[hp // 4][:, (hp % 4) * KEYS:(hp % 4 + 1) * KEYS],
                                     qT[:, hp, tb * P:(tb + 1) * P], keys[:, hp % 2, :], start=True, stop=True)
                last.then_inc(sc_full, 1)

        @block.scalar
        def _(act):
            act.preload_act_table(ACT.Exp)
            with act.Fori(0, TB) as tb:
                act.wait_ge(gap_ready, tb + 1)
                act.activation(expd[:, :, :], gap[:, :, :], ACT.Exp).then_inc(exp_ready, 1)

        @block.vector
        def _(dve):
            settled = sem("topk_settled")
            chain = Chain(dve, steps, settled)

            def score(hp):
                return psum[hp // 4][:, (hp % 4) * KEYS:(hp % 4 + 1) * KEYS]

            dve.wait_ge(iota_done, 1)
            chain.step(dve.tensor_copy(iota[:, :], iota_i[:, :]))
            chain.settle()
            PER_BLOCK = 5 * HALVES + 2 + 5 * PH + 2 * 5 + 3
            base = chain.n
            with dve.Fori(0, TB) as tb:
                chain.off = tb * PER_BLOCK
                dve.wait_ge(sc_full, tb + 1)
                dve.sem_inc(settled, 1)
                for hp in range(HALVES):
                    chain.step(dve.max(top_s[:, hp, 0:8], score(hp)))
                chain.settle()
                for hp in range(HALVES):
                    chain.step(dve.max_index(top_i[:, hp, 0:8], top_s[:, hp, 0:8], score(hp)))
                for hp in range(HALVES):
                    chain.step(dve.match_replace(rest[:, hp, :], top_s[:, hp, 0:8], score(hp), NEG))
                chain.settle()
                dve.sem_inc(sc_free, 1)
                for hp in range(HALVES):
                    chain.step(dve.max(top_s[:, hp, 8:16], rest[:, hp, :]))
                chain.settle()
                for hp in range(HALVES):
                    chain.step(dve.max_index(top_i[:, hp, 8:16], top_s[:, hp, 8:16], rest[:, hp, :]))
                s4 = top_s[:, :, :].rearrange("p (h two) k -> p h two k", two=2)
                chain.step(dve.tensor_tensor(cand[:, :, :, :],
                                             s4[:, :, 0, :].unsqueeze(3).broadcast_to([P, PH, TOPK, TOPK]),
                                             s4[:, :, 1, :].unsqueeze(2).broadcast_to([P, PH, TOPK, TOPK]), ALU.add))
                chain.settle()
                chain.step(dve.tensor_copy(top_f[:, :, :], top_i[:, :, :]))

                def sums(h):
                    return cand[:, h, :, :].rearrange("p a b -> p (a b)")

                for h in range(PH):
                    chain.step(dve.max(best[:, h, 0:8], sums(h)))
                chain.settle()
                for h in range(PH):
                    chain.step(dve.max_index(pos[:, h, 0:8], best[:, h, 0:8], sums(h)))
                for h in range(PH):
                    chain.step(dve.match_replace(crest[:, h, :], best[:, h, 0:8], sums(h), NEG))
                chain.settle()
                for h in range(PH):
                    chain.step(dve.max(best[:, h, 8:16], crest[:, h, :]))
                chain.settle()
                for h in range(PH):
                    chain.step(dve.max_index(pos[:, h, 8:16], best[:, h, 8:16], crest[:, h, :]))
                dve.tensor_tensor(gap[:, :, :], best[:, :, :], best[:, :, 0:1].broadcast_to([P, PH, TOPK]),
                                  ALU.subtract).then_inc(gap_ready, 1)
                chain.settle()
                p2 = pos[:, :, :].rearrange("p h k -> p (h k)")
                chain.step(dve.tensor_scalar(pos_ab[:, 0, :], p2, 4, None, ALU.logical_shift_right))
                chain.step(dve.tensor_scalar(pos_ab[:, 1, :], p2, TOPK - 1, None, ALU.bitwise_and))
                chain.settle()
                for half in range(2):
                    chain.step(dve.tensor_copy(pos_f[:, half, :], pos_ab[:, half, :]))
                chain.settle()
                f4 = top_f[:, :, :].rearrange("p (h two) k -> p h two k", two=2)
                for half in range(2):
                    chain.step(dve.tensor_tensor(hit[half][:, :, :],
                                                 pos_f[:, half, :].unsqueeze(2).broadcast_to([P, PICKS, TOPK]),
                                                 iota[:, :].unsqueeze(1).broadcast_to([P, PICKS, TOPK]), ALU.is_equal))
                chain.settle()
                for half in range(2):
                    at = hit[half][:, :, :].rearrange("p (h k) a -> p h k a", h=PH)
                    chain.step(dve.tensor_tensor(at, at, f4[:, :, half, :].unsqueeze(2)
                                                 .broadcast_to([P, PH, TOPK, TOPK]), ALU.mult))
                chain.settle()
                for half, dst in enumerate((pick_i1, pick_i2)):
                    chain.step(dve.tensor_reduce(dst[:, bass.ds(tb, 1), :].rearrange("p o k -> p (o k)"),
                                                 hit[half][:, :, :], AX.X, ALU.add))
                dve.wait_ge(exp_ready, tb + 1)
                chain.step(dve.tensor_reduce(total[:, :], expd[:, :, :], AX.X, ALU.add))
                chain.settle()
                chain.step(dve.reciprocal(inv[:, :], total[:, :]))
                chain.settle()
                chain.step(dve.tensor_tensor(pick_gate[:, bass.ds(tb, 1), :]
                                             .rearrange("p o (h k) -> p (o h) k", h=PH), expd[:, :, :],
                                             inv[:, :].unsqueeze(2).broadcast_to([P, PH, TOPK]), ALU.mult))
                chain.settle()
                assert chain.n - base == PER_BLOCK, chain.n - base


def spread_gates(nc, sem, psum, picks, ident, gates_dram):
    CH = SEQ // TCH
    QUADS = TCH // 4
    with ExitStack() as ctx:
        def sb(name, shape, dt=F32):
            return ctx.enter_context(nc.sbuf_tensor(name, shape, dt))

        i1T, i2T, gT_hi, gT_lo = (sb(n, [P, SEQ], F16) for n in ("i1T", "i2T", "gT_hi", "gT_lo"))
        iota_i = sb("iota128_i", [P, KEYS, 4], I32)
        iota = sb("iota128", [P, KEYS, 4], F16)
        hot1, hot2_hi, hot2_lo = ([sb(f"{n}{b}", [P, QUADS, KEYS, 4], F16) for b in range(2)]
                                  for n in ("hot1_", "hot2hi_", "hot2lo_"))
        hot2 = sb("hot2", [P, QUADS, KEYS, 4], F16)
        stage = [sb(f"stage{b}", [P, KEYS, GST], F32) for b in range(2)]
        turned, iota_done, cols_done, steps = sem("picks_turned"), sem("iota128_done"), sem("cols_done"), sem("hot_steps")
        hots_ready, hots_used, quad_full, quad_free = sem("hots_ready"), sem("hots_used"), sem("quad_full"), sem("quad_free")
        stage_full = sem("stage_full")
        stored = [sem(f"stored{b}") for b in range(2)]
        block = ctx.enter_context(nc.Block())

        @block.gpsimd
        def _(pool):
            pool.iota(iota_i[:, :, :], pattern=[[1, KEYS], [0, 4]], base=0, channel_multiplier=0)\
                .then_inc(iota_done, 1)

        @block.vector
        def _(dve):
            dve.wait_ge(iota_done, 1)
            dve.tensor_copy(iota[:, :, :], iota_i[:, :, :]).then_inc(cols_done, 1)
            for n, dst in enumerate((i1T, i2T, gT_hi)):
                dve.wait_ge(turned, n + 1)
                dve.tensor_scalar(dst[:, :], psum[n][:, :], GATE_SCALE if n == 2 else 1.0, None,
                                  ALU.mult).then_inc(cols_done, 1)
            dve.wait_ge(cols_done, 4)
            dve.scalar_tensor_tensor(out=gT_lo[:, :], in0=psum[2][:, :], scalar=GATE_SCALE, in1=gT_hi[:, :],
                                     op0=ALU.mult, op1=ALU.subtract).then_inc(cols_done, 1)
            dve.wait_ge(cols_done, 5)
            dve.sem_inc(hots_used, 2)

            def rows(t0, src):
                return src[:, bass.ds(t0, TCH)].rearrange("p (q f) -> p q f", f=4).unsqueeze(2)\
                    .broadcast_to([P, QUADS, KEYS, 4])

            keys_row = iota[:, :, :].unsqueeze(1).broadcast_to([P, QUADS, KEYS, 4])
            with dve.Fori(0, CH // 2) as pair:
                for b in range(2):
                    t0 = (pair * 2 + b) * TCH
                    done = (pair * 2 + b) * 4
                    dve.wait_ge(hots_used, pair * 2 + b + 1)
                    dve.tensor_tensor(hot1[b][:, :, :, :], rows(t0, i1T), keys_row, ALU.is_equal).then_inc(steps, 1)
                    dve.tensor_tensor(hot2[:, :, :, :], rows(t0, i2T), keys_row, ALU.is_equal).then_inc(steps, 1)
                    dve.wait_ge(steps, done + 2)
                    dve.tensor_tensor(hot2_hi[b][:, :, :, :], hot2[:, :, :, :], rows(t0, gT_hi),
                                      ALU.mult).then_inc(steps, 1)
                    dve.tensor_tensor(hot2_lo[b][:, :, :, :], hot2[:, :, :, :], rows(t0, gT_lo),
                                      ALU.mult).then_inc(steps, 1)
                    dve.wait_ge(steps, done + 4)
                    dve.sem_inc(hots_ready, 1)

        @block.tensor
        def _(pe):
            for n, src in enumerate(picks):
                for tb in range(TB):
                    last = pe.transpose(psum[n][:, tb * P:(tb + 1) * P], src[:, tb, :], ident[:, :])
                last.then_inc(turned, 1)
            pe.wait_ge(cols_done, 5)
            with pe.Fori(0, CH // 2) as pair:
                for b in range(2):
                    pe.wait_ge(hots_ready, pair * 2 + b + 1)
                    for q in range(QUADS):
                        bank = psum[q % 8]
                        pe.wait_ge(quad_free, (pair * 2 + b) * QUADS + q + 1)
                        for f in range(4):
                            out = bank[:, f * KEYS:(f + 1) * KEYS]
                            pe.matmul(out, hot1[b][:, q, :, f], hot2_hi[b][:, q, :, f], start=True, stop=False)
                            last = pe.matmul(out, hot1[b][:, q, :, f], hot2_lo[b][:, q, :, f], start=False, stop=True)
                        last.then_inc(quad_full, 1)
                    pe.wait_ge(quad_full, (pair * 2 + b) * QUADS + QUADS)
                    pe.sem_inc(hots_used, 1)

        per_stage = GST // 4

        @block.scalar
        def _(act):
            act.preload_act_table(ACT.Copy)
            act.sem_inc(quad_free, 8)
            act.sem_inc(stored[0], 16)
            act.sem_inc(stored[1], 16)
            with act.Fori(0, SEQ // GST // 2) as pair:
                for b in range(2):
                    act.wait_ge(stored[b], pair * 16 + 16)
                    for q in range(per_stage):
                        act.wait_ge(quad_full, (pair * 2 + b) * per_stage + q + 1)
                        act.activation(stage[b][:, :, 4 * q:4 * q + 4].rearrange("p k f -> p f k"),
                                       psum[q % 8][:, :].rearrange("p (f k) -> p f k", f=4), ACT.Copy,
                                       scale=1.0 / GATE_SCALE).then_inc(quad_free, 1)
                    act.wait_ge(quad_free, (pair * 2 + b) * per_stage + per_stage + 8)
                    act.sem_inc(stage_full, 1)

        @block.sync
        def _(sp):
            with sp.Fori(0, SEQ // GST // 2) as pair:
                for b in range(2):
                    sp.wait_ge(stage_full, pair * 2 + b + 1)
                    sp.dma_start(gates_dram[:, :, bass.ds((pair * 2 + b) * GST, GST)].rearrange("k p t -> p k t"),
                                 stage[b][:, :, :]).then_inc(stored[b], 16)
            for b in range(2):
                sp.wait_ge(stored[b], SEQ // GST // 2 * 16 + 16)


def evaluate_experts(nc, sem, psum, res, hT_hi, hT_lo, peer_u, peer_v, gates_dram):
    G = GROUP
    RING = 2 * G
    NG = TILES // G
    OUTS = TB * D // BANK
    A_BANKS, Y_BANKS = 2, 4
    with ExitStack() as ctx:
        def sb(name, shape, dt=F32):
            return ctx.enter_context(nc.sbuf_tensor(name, shape, dt))

        u_raw = [sb(f"u_raw{i}", [P, KC, P]) for i in range(2)]
        u_hi = [sb(f"u_hi{i}", [P, KC, P], F32R) for i in range(2)]
        u_lo = [sb(f"u_lo{i}", [P, KC, P], F32R) for i in range(2)]
        v_raw = [sb(f"v_raw{i}", [P, D]) for i in range(2)]
        v_hi = [sb(f"v_hi{i}", [P, D], F32R) for i in range(RING)]
        v_lo = [sb(f"v_lo{i}", [P, D], F32R) for i in range(RING)]
        gates = [sb(f"gates{i}", [P, SEQ]) for i in range(2)]
        act32 = [sb(f"act32_{i}", [P, SEQ]) for i in range(2)]
        a_hi = [sb(f"a_hi{i}", [P, SEQ], F32R) for i in range(RING)]
        a_lo = [sb(f"a_lo{i}", [P, SEQ], F32R) for i in range(RING)]
        u_in, v_in, g_in = ([sem(f"{n}_in{i}") for i in range(2)] for n in "uvg")
        u_hi_done, u_lo_done, v_hi_done, v_lo_done = sem("u_hi_done"), sem("u_lo_done"), sem("v_hi_done"), sem("v_lo_done")
        a_full, gelu_done, gated, a_hi_done, a_lo_done = (
            sem("a_full"), sem("gelu_done"), sem("gated"), sem("a_hi_done"), sem("a_lo_done"))
        y_full, y_added = sem("y_full"), sem("y_added")
        block = ctx.enter_context(nc.Block())

        def count(m, c, per=1):
            return m * (RING * per) + c * per if c or not isinstance(m, int) or m else 0

        def reached(eng, semaphore, value):
            if not isinstance(value, int) or value > 0:
                eng.wait_ge(semaphore, value)

        def landed(m, c):
            return m * (RING // 2 * 16) + (c // 2 + 1) * 16

        @block.sync
        def _(sp):
            def load(m, c):
                b = c % 2
                j = count(m, c)
                reached(sp, u_lo_done, j - 1)
                sp.dma_start(u_raw[b][:, :, :], peer_u[bass.ds(j, 1), :, :, :]
                             .rearrange("o p c e -> (o p) c e")).then_inc(u_in[b], 16)
                reached(sp, v_lo_done, j - 1)
                sp.dma_start(v_raw[b][:, :], peer_v[bass.ds(j, 1), :, :]
                             .rearrange("o p d -> (o p) d")).then_inc(v_in[b], 16)
                reached(sp, gated, j - 1)
                sp.dma_start(gates[b][:, :], gates_dram[bass.ds(j, 1), :, :]
                             .rearrange("o p t -> (o p) t")).then_inc(g_in[b], 16)

            for c in range(RING):
                load(0, c)
            with sp.Fori(0, TILES // RING - 1) as dg:
                for c in range(RING):
                    load(dg, RING + c)

        def slots(eng, front, back):
            front(0, 0)
            for c in range(1, RING):
                front(0, c)
                back(0, c - 1)
            with eng.Fori(0, TILES // RING - 1) as dg:
                for c in range(RING, 2 * RING):
                    front(dg, c)
                    back(dg, c - 1)
            back(0, TILES - 1)

        @block.scalar
        def _(act):
            def front(m, c):
                b = c % 2
                act.wait_ge(u_in[b], landed(m, c))
                reached(act, a_full, count(m, c - 1))
                act.activation(u_hi[b][:, :, :], u_raw[b][:, :, :], ACT.Copy).then_inc(u_hi_done, 1)

            def back(m, c):
                b, r = c % 2, c % RING
                if r % G == 0:
                    reached(act, y_full, count(m, c - RING + G, OUTS // G))
                act.wait_ge(v_in[b], landed(m, c))
                act.activation(v_hi[r][:, :], v_raw[b][:, :], ACT.Copy).then_inc(v_hi_done, 1)
                act.wait_ge(a_full, count(m, c + 1))
                reached(act, a_lo_done, count(m, c - 1))
                act.activation(act32[b][:, :], psum[b][:, :], ACT.Gelu).then_inc(gelu_done, 1)
                act.wait_ge(gated, count(m, c + 1))
                act.activation(a_hi[r][:, :], act32[b][:, :], ACT.Copy).then_inc(a_hi_done, 1)

            act.preload_act_table(ACT.Gelu)
            slots(act, front, back)

        @block.vector
        def _(dve):
            def add_output(m, c, n):
                dve.wait_ge(y_full, count(m, c // G * G - G, OUTS // G) + (n + 1))
                at = res[:, n // 2, n % 2 * BANK:(n % 2 + 1) * BANK]
                dve.tensor_tensor(at, psum[A_BANKS + n % Y_BANKS][:, :], at, ALU.add).then_inc(y_added, 1)

            def front(m, c):
                b = c % 2
                dve.wait_ge(u_hi_done, count(m, c + 1))
                dve.tensor_tensor(u_lo[b][:, :, :], u_raw[b][:, :, :], u_hi[b][:, :, :].bitcast(F32),
                                  ALU.subtract).then_inc(u_lo_done, 1)

            def back(m, c):
                b, r = c % 2, c % RING
                dve.wait_ge(v_hi_done, count(m, c + 1))
                dve.tensor_tensor(v_lo[r][:, :], v_raw[b][:, :], v_hi[r][:, :].bitcast(F32),
                                  ALU.subtract).then_inc(v_lo_done, 1)
                dve.wait_ge(gelu_done, count(m, c + 1))
                dve.wait_ge(g_in[b], landed(m, c))
                dve.tensor_tensor(act32[b][:, :], act32[b][:, :], gates[b][:, :], ALU.mult).then_inc(gated, 1)
                dve.wait_ge(a_hi_done, count(m, c + 1))
                dve.tensor_tensor(a_lo[r][:, :], act32[b][:, :], a_hi[r][:, :].bitcast(F32),
                                  ALU.subtract).then_inc(a_lo_done, 1)
                if c >= G:
                    for n in range(2 * (r % G), 2 * (r % G) + 2):
                        add_output(m, c, n)

            slots(dve, front, back)
            for n in range(OUTS):
                add_output(0, TILES, n)

        @block.tensor
        def _(pe):
            def first_product(m, c):
                b = c % 2
                pe.wait_ge(u_lo_done, count(m, c + 1))
                reached(pe, gelu_done, count(m, c - 1))
                split_product(pe, psum[b][:, :], [((u_hi[b][:, k, :], u_lo[b][:, k, :]),
                                                   (hT_hi[:, k, :], hT_lo[:, k, :])) for k in range(KC)])\
                    .then_inc(a_full, 1)

            def output(m, c, n):
                r = c % RING
                if n == 0:
                    pe.wait_ge(v_lo_done, count(m, c + G))
                    pe.wait_ge(a_lo_done, count(m, c + G))
                reached(pe, y_added, count(m, c, OUTS // G) + (n + 1 - Y_BANKS))
                t, d = slice(n // 2 * P, (n // 2 + 1) * P), slice(n % 2 * BANK, (n % 2 + 1) * BANK)
                split_product(pe, psum[A_BANKS + n % Y_BANKS][:, :],
                              [((a_hi[r + i][:, t], a_lo[r + i][:, t]), (v_hi[r + i][:, d], v_lo[r + i][:, d]))
                               for i in range(G)]).then_inc(y_full, 1)

            def slot(m, c):
                first_product(m, c)
                if c >= G:
                    for n in range(2 * (c % G), 2 * (c % G) + 2):
                        output(m, c // G * G - G, n)

            for c in range(RING):
                slot(0, c)
            with pe.Fori(0, TILES // RING - 1) as dg:
                for c in range(RING, 2 * RING):
                    slot(dg, c)
            for n in range(OUTS):
                output(0, TILES - G, n)


def add_embedding(nc, sem, psum, res, hT_hi, hT_lo, p_t, w_gate, w_ple, out):
    PC = PLE // P
    with ExitStack() as ctx:
        def sb(name, shape, dt=F32):
            return ctx.enter_context(nc.sbuf_tensor(name, shape, dt))

        p_raw, p_hi, p_lo = sb("p_raw", [P, PC, SEQ]), sb("p_hi", [P, PC, SEQ], F32R), sb("p_lo", [P, PC, SEQ], F32R)
        e_raw, e_hi, e_lo = sb("e_raw", [P, PC, D]), sb("e_hi", [P, PC, D], F32R), sb("e_lo", [P, PC, D], F32R)
        g_raw = [sb(f"g_raw{i}", [P, KC, BANK]) for i in range(2)]
        g_hi = [sb(f"g_hi{i}", [P, KC, BANK], F32R) for i in range(2)]
        g_lo = [sb(f"g_lo{i}", [P, KC, BANK], F32R) for i in range(2)]
        sig = [sb(f"sig{i}", [P, BANK]) for i in range(4)]
        loaded = [sem(f"ple_loaded{i}") for i in range(4)]
        hi_done, lo_done, bank_full, sig_done, mult_done, sum_done, stored = (
            sem("ple_hi"), sem("ple_lo"), sem("ple_full"), sem("sig_done"), sem("mult_done"), sem("sum_done"),
            sem("out_stored"))
        splits = [(p_raw, p_hi, p_lo), (e_raw, e_hi, e_lo), (g_raw[0], g_hi[0], g_lo[0]), (g_raw[1], g_hi[1], g_lo[1])]
        sources = [p_t, w_ple, w_gate[0], w_gate[1]]
        units = [(i, tb) for i in range(2) for tb in range(TB)]
        block = ctx.enter_context(nc.Block())

        @block.sync
        def _(sp):
            for n, (raw, _, _) in enumerate(splits):
                sp.dma_start(raw[:, :, :], sources[n]).then_inc(loaded[n], 16)
            for n, (i, tb) in enumerate(units):
                sp.wait_ge(sum_done, n + 1)
                sp.dma_start(out[tb * P:(tb + 1) * P, i * BANK:(i + 1) * BANK],
                             res[:, tb, i * BANK:(i + 1) * BANK]).then_inc(stored, 16)
            sp.wait_ge(stored, 16 * len(units))

        @block.scalar
        def _(act):
            for n, (raw, hi, _) in enumerate(splits):
                act.wait_ge(loaded[n], 16)
                act.activation(hi[:, :, :], raw[:, :, :], ACT.Copy).then_inc(hi_done, 1)
            for n in range(len(units)):
                act.wait_ge(bank_full, n + 1)
                if n >= 4:
                    act.wait_ge(sum_done, n - 3)
                act.activation(sig[n % 4][:, :], psum[n % 4][:, :], ACT.Sigmoid).then_inc(sig_done, 1)

        @block.vector
        def _(dve):
            for n, (raw, hi, lo) in enumerate(splits):
                dve.wait_ge(hi_done, n + 1)
                dve.tensor_tensor(lo[:, :, :], raw[:, :, :], hi[:, :, :].bitcast(F32), ALU.subtract)\
                   .then_inc(lo_done, 1)
            for n, (i, tb) in enumerate(units):
                dve.wait_ge(sig_done, n + 1)
                dve.tensor_tensor(sig[n % 4][:, :], psum[4 + n % 4][:, :], sig[n % 4][:, :], ALU.mult)\
                   .then_inc(mult_done, 1)
                dve.wait_ge(mult_done, n + 1)
                at = res[:, tb, i * BANK:(i + 1) * BANK]
                dve.tensor_tensor(at, at, sig[n % 4][:, :], ALU.add).then_inc(sum_done, 1)

        @block.tensor
        def _(pe):
            for n, (i, tb) in enumerate(units):
                t = slice(tb * P, (tb + 1) * P)
                if tb == 0:
                    pe.wait_ge(lo_done, 3 + i)
                if n >= 4:
                    pe.wait_ge(mult_done, n - 3)
                split_product(pe, psum[4 + n % 4][:, :],
                              [((p_hi[:, c, t], p_lo[:, c, t]),
                                (e_hi[:, c, i * BANK:(i + 1) * BANK], e_lo[:, c, i * BANK:(i + 1) * BANK]))
                               for c in range(PC)])
                split_product(pe, psum[n % 4][:, :],
                              [((hT_hi[:, c, t], hT_lo[:, c, t]), (g_hi[i][:, c, :], g_lo[i][:, c, :]))
                               for c in range(KC)]).then_inc(bank_full, 1)


def kernel(x, p, g_mix, w_in, q_norm, k_norm, sinks, w_out, g_ffn,
           peer_w_query, peer_sub_keys, peer_u, peer_v, g_ple, w_ple_gate, w_ple_proj):
    import numpy as np
    import concourse.bacc as bacc
    from concourse.bass_utils import run_bass_kernel_spmd

    def panels(w, chunks, n, width):
        return np.asarray(w).reshape(chunks, P, n, width).transpose(2, 1, 0, 3)

    def column(g):
        return np.asarray(g).reshape(KC, P).T

    heads = np.arange(RH)
    gamma = 1.0 - np.exp2(-5.0 - heads)
    idx = np.arange(P)
    rel = idx[None, :] - idx[:, None]
    decay = np.where(rel[:, None, :] >= 0, gamma[None, :, None] ** np.maximum(rel, 0)[:, None, :], 0.0) * HD ** -0.5
    wq = np.repeat(gamma[:, None] ** (idx + 1)[None, :], HD, axis=0).reshape(RH // 2, P, P).transpose(1, 0, 2)
    wk = gamma[None, :] ** (P - 1 - idx)[:, None] * HD ** -0.5
    chunk = np.repeat(gamma ** P, HD).reshape(RH // 2, P).T
    half = HD // 2
    freqs = (np.float32(10000.0) ** (-np.arange(half, dtype=np.float32) / np.float32(half))).astype(np.float32)
    ang = np.arange(SEQ, dtype=np.float32)[:, None] * freqs[None, :]
    cos, sin = (f(ang).reshape(TB, P, half).transpose(1, 0, 2) for f in (np.cos, np.sin))
    back = idx[:, None] + P - np.arange(2 * P)[None, :]
    mask = np.where((back >= 0) & (back < P), 0.0, -1.0e30)

    arrays = {
        "x": np.asarray(x)[0], "p_t": np.asarray(p)[0, 0].T.reshape(PLE // P, P, SEQ).transpose(1, 0, 2),
        "g_mix": column(g_mix), "w_in": panels(w_in, KC, IN_PANELS, IN_PW),
        "q_norm": np.tile(np.asarray(q_norm)[0], 2)[:, None], "k_norm": np.tile(np.asarray(k_norm)[0], 2)[:, None],
        "sinks": np.broadcast_to(np.asarray(sinks)[0], (P, QH)), "w_out": panels(w_out, KC, 2, BANK),
        "g_ffn": column(g_ffn), "w_query": panels(peer_w_query, KC, 4, BANK),
        "keys_t": np.asarray(peer_sub_keys)[0].transpose(2, 0, 1),
        "peer_u": np.asarray(peer_u)[0].reshape(KEYS, KEYS, KC, P).transpose(1, 3, 2, 0),
        "peer_v": np.asarray(peer_v)[0].reshape(KEYS, KEYS, D).transpose(1, 0, 2),
        "g_ple": column(g_ple), "w_gate": panels(w_ple_gate, KC, 2, BANK),
        "w_ple": np.asarray(w_ple_proj).reshape(PLE // P, P, D).transpose(1, 0, 2),
        "ident_c": np.eye(P, dtype=np.float32),
        "cos_c": cos, "sin_c": sin, "decay_c": decay[:, [0, 2, 4, 6, 1, 3, 5, 7]].astype(np.float32), "wq_c": wq.astype(np.float32),
        "wk_c": wk.astype(np.float32), "chunk_c": chunk.astype(np.float32), "mask_c": mask.astype(np.float32),
    }
    arrays = {n: np.ascontiguousarray(a) for n, a in arrays.items()}
    nc = bacc.Bacc("TRN2", target_bir_lowering=False, num_devices=1)
    args = {n: nc.dram_tensor(n, a.shape, mybir.dt.from_np(a.dtype), kind="ExternalInput").ap()
            for n, a in arrays.items()}
    out = nc.dram_tensor("out", (SEQ, D), F32, kind="ExternalOutput").ap()
    hybrid_layer(nc, out=out, **args)
    r = run_bass_kernel_spmd(nc, [arrays], core_ids=[0])
    return np.asarray(r.results[0]["out"]).reshape(1, SEQ, D)
```

```python
from contextlib import ExitStack

import concourse.bass as bass
from concourse import mybir

F32 = mybir.dt.float32
F32R = mybir.dt.float32r
F16 = mybir.dt.float16
U32 = mybir.dt.uint32
I32 = mybir.dt.int32
ALU = mybir.AluOpType
ACT = mybir.ActivationFunctionType
AX = mybir.AxisListType

P = 128
D = 1024
SEQ = 512
TB = SEQ // P
KC = D // P
HD = 64
RH = 8
QH = 8
KVH = 2
RW = RH * HD
IN_W = 4 * RW + QH * HD + 2 * KVH * HD
RQ, RK, RV, RG, SQ, SK, SV = 0, RW, 2 * RW, 3 * RW, 4 * RW, 4 * RW + QH * HD, 4 * RW + (QH + KVH) * HD
IN_PANELS = 8
IN_PW = IN_W // IN_PANELS
PANELS, PW = 4, D // 4
BANK = 512
PH = 8
KEYS = 128
TOPK = 16
HALVES = 2 * PH
PICKS = PH * TOPK
TILES = KEYS
GROUP = 4
PLE = 256
EPS = 1e-6
NEG = -3.0e38
FULL_A = 4
CANDS = FULL_A * TOPK + (TOPK - FULL_A) * FULL_A
GATE_SCALE = 4096.0
EARLY = TILES // 2
EARLY_PER_BLOCK = 12
EARLY_PER_CHUNK = 1
TCH = 32
GST = 64


class Chain:

    def __init__(self, eng, sem, settled=None):
        self.eng, self.sem, self.settled, self.n, self.off = eng, sem, settled, 0, 0

    def step(self, ins):
        ins.then_inc(self.sem, 1)
        self.n += 1

    def settle(self):
        self.eng.wait_ge(self.sem, self.off + self.n)
        if self.settled is not None:
            self.eng.sem_inc(self.settled, 1)


def split_product(pe, out, pairs):
    last = None
    for n, ((ah, al), (bh, bl)) in enumerate(pairs):
        pe.matmul(out, ah, bh, start=(n == 0), stop=False)
        pe.matmul(out, ah, bl, start=False, stop=False)
        last = pe.matmul(out, al, bh, start=False, stop=(n == len(pairs) - 1))
    return last


def to_transposed_parts(nc, sem, psum, tag, src, gain, hT_hi, hT_lo, ident, normalize):
    with ExitStack() as ctx:
        sumsq = ctx.enter_context(nc.sbuf_tensor(f"{tag}_sumsq", [P, TB], F32))
        mean = ctx.enter_context(nc.sbuf_tensor(f"{tag}_mean", [P, TB], F32))
        inv = ctx.enter_context(nc.sbuf_tensor(f"{tag}_inv", [P, TB], F32))
        rstd = ctx.enter_context(nc.sbuf_tensor(f"{tag}_rstd", [P, TB], F32))
        square = ctx.enter_context(nc.sbuf_tensor(f"{tag}_square", [P, D], F32))
        xn = ctx.enter_context(nc.sbuf_tensor(f"{tag}_xn", [P, TB, D], F32)) if normalize else src
        sq_done, inv_done, rstd_done = sem(f"{tag}_sq_done"), sem(f"{tag}_inv_done"), sem(f"{tag}_rstd_done")
        dve_steps, xn_done = sem(f"{tag}_dve_steps"), sem(f"{tag}_xn_done")
        transposed, hi_done = sem(f"{tag}_transposed"), sem(f"{tag}_hi_done")
        block = ctx.enter_context(nc.Block())

        @block.scalar
        def _(act):
            if normalize:
                for tb in range(TB):
                    if tb:
                        act.wait_ge(sq_done, tb)
                    act.activation(square[:, :], src[:, tb, :], ACT.Square,
                                   accum_out=sumsq[:, tb:tb + 1]).then_inc(sq_done, 1)
                act.wait_ge(inv_done, 1)
                act.activation(rstd[:, :], inv[:, :], ACT.Sqrt).then_inc(rstd_done, 1)
            for kc in range(KC):
                act.wait_ge(transposed, kc + 1)
                act.activation(hT_hi[:, kc, :], psum[kc][:, :], ACT.Copy,
                               scale=gain[:, kc:kc + 1] if normalize else 1.0).then_inc(hi_done, 1)

        @block.vector
        def _(dve):
            if normalize:
                chain = Chain(dve, dve_steps)
                dve.wait_ge(sq_done, TB)
                chain.step(dve.tensor_scalar(mean[:, :], sumsq[:, :], 1.0 / D, EPS, ALU.mult, ALU.add))
                chain.settle()
                dve.reciprocal(inv[:, :], mean[:, :]).then_inc(inv_done, 1)
                dve.wait_ge(rstd_done, 1)
                for tb in range(TB):
                    dve.tensor_scalar(xn[:, tb, :], src[:, tb, :], rstd[:, tb:tb + 1], None,
                                      ALU.mult).then_inc(xn_done, 1)
            for kc in range(KC):
                dve.wait_ge(hi_done, kc + 1)
                dve.scalar_tensor_tensor(out=hT_lo[:, kc, :], in0=psum[kc][:, :],
                                         scalar=gain[:, kc:kc + 1] if normalize else 1.0,
                                         in1=hT_hi[:, kc, :].bitcast(F32), op0=ALU.mult, op1=ALU.subtract)\
                   .then_inc(dve_steps, 1)

        @block.tensor
        def _(pe):
            if normalize:
                pe.wait_ge(xn_done, TB)
            for kc in range(KC):
                for tb in range(TB):
                    last = pe.transpose(psum[kc][:, tb * P:(tb + 1) * P], xn[:, tb, kc * P:(kc + 1) * P],
                                        ident[:, :])
                last.then_inc(transposed, 1)


def project(nc, sem, psum, tag, panels, n_panels, width, chunks, hT_hi, hT_lo, evacuate, transposed=False,
            then=None):
    with ExitStack() as ctx:
        raw = [ctx.enter_context(nc.sbuf_tensor(f"{tag}_raw{i}", [P, chunks, width], F32)) for i in range(2)]
        w_hi = [ctx.enter_context(nc.sbuf_tensor(f"{tag}_whi{i}", [P, chunks, width], F32R)) for i in range(2)]
        w_lo = [ctx.enter_context(nc.sbuf_tensor(f"{tag}_wlo{i}", [P, chunks, width], F32R)) for i in range(2)]
        loaded = [sem(f"{tag}_loaded{i}") for i in range(2)]
        hi_done, lo_done = sem(f"{tag}_hi_done"), sem(f"{tag}_lo_done")
        panel_used, bank_full, bank_free = sem(f"{tag}_panel_used"), sem(f"{tag}_bank_full"), sem(f"{tag}_bank_free")
        units = width // P if transposed else TB
        n_pairs = n_panels // 2
        block = ctx.enter_context(nc.Block())

        @block.sync
        def _(sp):
            sp.sem_inc(lo_done, 2)
            with sp.Fori(0, n_pairs) as pair:
                for i in range(2):
                    sp.wait_ge(lo_done, pair * 2 + i + 1)
                    sp.dma_start(raw[i][:, :, :], panels[bass.ds(pair * 2 + i, 1), :, :, :]
                                 .rearrange("o p c n -> (o p) c n")).then_inc(loaded[i], 16)
            if then:
                then(sp)

        @block.scalar
        def _(act):
            act.sem_inc(panel_used, 2)
            with act.Fori(0, n_pairs) as pair:
                for i in range(2):
                    act.wait_ge(loaded[i], pair * 16 + 16)
                    act.wait_ge(panel_used, pair * 2 + i + 1)
                    act.activation(w_hi[i][:, :, :], raw[i][:, :, :], ACT.Copy).then_inc(hi_done, 1)

        @block.vector
        def _(dve):
            def split(pair, i):
                dve.wait_ge(hi_done, pair * 2 + i + 1)
                dve.tensor_tensor(w_lo[i][:, :, :], raw[i][:, :, :], w_hi[i][:, :, :].bitcast(F32),
                                  ALU.subtract).then_inc(lo_done, 1)

            dve.sem_inc(bank_free, 2 * units)
            with dve.Fori(0, n_pairs) as pair:
                for i in range(2):
                    split(pair, i)
                for i in range(2):
                    for u in range(units):
                        dve.wait_ge(bank_full, pair * 2 * units + i * units + u + 1)
                        evacuate(dve, pair, i, u, psum[i * units + u][:, 0:SEQ if transposed else width])\
                            .then_inc(bank_free, 1)

        @block.tensor
        def _(pe):
            with pe.Fori(0, n_pairs) as pair:
                for i in range(2):
                    pe.wait_ge(lo_done, pair * 2 + i + 3)
                    for u in range(units):
                        pe.wait_ge(bank_free, pair * 2 * units + i * units + u + 1)
                        if transposed:
                            pairs = [((w_hi[i][:, c, u * P:(u + 1) * P], w_lo[i][:, c, u * P:(u + 1) * P]),
                                      (hT_hi[:, c, :], hT_lo[:, c, :])) for c in range(chunks)]
                            out = psum[i * units + u][:, :]
                        else:
                            pairs = [((hT_hi[:, c, u * P:(u + 1) * P], hT_lo[:, c, u * P:(u + 1) * P]),
                                      (w_hi[i][:, c, :], w_lo[i][:, c, :])) for c in range(chunks)]
                            out = psum[i * units + u][:, 0:width]
                        last = split_product(pe, out, pairs)
                        last.then_inc(bank_full, 1)
                    pe.wait_ge(bank_full, pair * 2 * units + i * units + units)
                    pe.sem_inc(panel_used, 1)


class FirstProducts:

    def __init__(self, nc, ctx, sem, psum, peer_u, hT_hi, hT_lo):
        def sb(name, dt):
            return [ctx.enter_context(nc.sbuf_tensor(f"{name}{i}", [P, KC, P], dt)) for i in range(2)]

        self.peer_u, self.hT_hi, self.hT_lo = peer_u, hT_hi, hT_lo
        self.raw, self.hi, self.lo = sb("u_raw", F32), sb("u_hi", F32R), sb("u_lo", F32R)
        self.out = [ctx.enter_context(nc.sbuf_tensor(f"gelu{i}", [P, SEQ], F32)) for i in range(2)]
        self.bank = psum[6:8]
        self.landed = [sem(f"u_in{i}") for i in range(2)]
        self.hi_done, self.lo_done, self.full, self.gelu_done = sem("u_hi_done"), sem("u_lo_done"), sem("a_full"), sem("gelu_done")

    @staticmethod
    def number(tile):
        m, K, c = tile
        return m * K + c if not isinstance(m, int) or m else c

    @staticmethod
    def of_buffer(tile):
        m, K, c = tile
        return m * (K // 2) + c // 2 if not isinstance(m, int) or m else c // 2

    def load(self, sp, tile, wait=True):
        b = tile[2] % 2
        if wait:
            sp.wait_ge(self.lo_done, self.number(tile) + 1)
        sp.dma_start(self.raw[b][:, :, :], self.peer_u[bass.ds(self.number(tile), 1), :, :, :]
                     .rearrange("o p c e -> (o p) c e")).then_inc(self.landed[b], 16)

    def split_hi(self, act, tile):
        b = tile[2] % 2
        act.wait_ge(self.landed[b], self.of_buffer(tile) * 16 + 16)
        act.wait_ge(self.full, self.number(tile) + 1)
        act.activation(self.hi[b][:, :, :], self.raw[b][:, :, :], ACT.Copy).then_inc(self.hi_done, 1)

    def split_lo(self, dve, tile):
        b = tile[2] % 2
        dve.wait_ge(self.hi_done, self.number(tile) + 1)
        dve.tensor_tensor(self.lo[b][:, :, :], self.raw[b][:, :, :], self.hi[b][:, :, :].bitcast(F32),
                          ALU.subtract).then_inc(self.lo_done, 1)

    def product(self, pe, tile):
        b = tile[2] % 2
        pe.wait_ge(self.lo_done, self.number(tile) + 3)
        pe.wait_ge(self.gelu_done, self.number(tile) + 1)
        split_product(pe, self.bank[b][:, :], [((self.hi[b][:, k, :], self.lo[b][:, k, :]),
                                                (self.hT_hi[:, k, :], self.hT_lo[:, k, :])) for k in range(KC)])\
            .then_inc(self.full, 1)

    def gelu(self, act, tile):
        act.wait_ge(self.full, self.number(tile) + 3)
        act.activation(self.out[tile[2] % 2][:, :], self.bank[tile[2] % 2][:, :], ACT.Gelu).then_inc(self.gelu_done, 1)


class EarlyTiles:

    def __init__(self, first, dram, spilled):
        self.first, self.dram, self.spilled = first, dram, spilled

    @staticmethod
    def later(tile, n):
        return tile[0], tile[1], tile[2] + n

    def sync(self, sp, tile):
        f, b = self.first, tile[2] % 2
        f.load(sp, self.later(tile, 3))
        sp.wait_ge(f.gelu_done, f.number(tile) + 3)
        sp.dma_start(self.dram[bass.ds(f.number(tile), 1), :, :].rearrange("o p t -> (o p) t"), f.out[b][:, :])\
            .then_inc(self.spilled[b], 16)

    def scalar(self, act, tile):
        f, b = self.first, tile[2] % 2
        f.split_hi(act, self.later(tile, 1))
        act.wait_ge(self.spilled[b], f.of_buffer(tile) * 16 + 16)
        f.gelu(act, tile)

    def vector(self, dve, tile):
        self.first.split_lo(dve, self.later(tile, 1))

    def tensor(self, pe, tile):
        self.first.product(pe, tile)

    def wait_stored(self, eng, b):
        eng.wait_ge(self.spilled[b], EARLY // 2 * 16 + 16)


def load_all(nc, sem, tag, pairs):
    done = sem(f"{tag}_loaded")
    with nc.Block() as block:
        @block.sync
        def _(sp):
            for dst, src in pairs:
                sp.dma_start(dst, src).then_inc(done, 16)
            sp.wait_ge(done, 16 * len(pairs))


def hybrid_layer(nc, x, p_t, g_mix, w_in, q_norm, k_norm, sinks, w_out, g_ffn, w_query, keys_t, peer_u, peer_v,
                 g_ple, w_gate, w_ple, ident_c, cos_c, sin_c, decay_c, wq_c, wk_c, chunk_c, mask_c, out):
    gates_dram = nc.dram_tensor("gates", [SEQ // GST, P, TILES, GST], F32).ap()
    gelu_dram = nc.dram_tensor("early_gelu", [EARLY, P, SEQ], F32).ap()
    with ExitStack() as ctx:
        def sb(name, shape, dt=F32):
            return ctx.enter_context(nc.sbuf_tensor(name, shape, dt))

        def sem(name):
            return ctx.enter_context(nc.semaphore(name))

        psum = [ctx.enter_context(nc.psum_tensor(f"bank{i}", [P, BANK], F32)) for i in range(8)]
        res = sb("res", [P, TB, D])
        hT_hi = sb("hT_hi", [P, KC, SEQ], F32R)
        hT_lo = sb("hT_lo", [P, KC, SEQ], F32R)
        ident = sb("ident", [P, P])
        gains = sb("gains", [P, 3, KC])

        load_all(nc, sem, "start", [
            (res[:, :, :], x.rearrange("(t p) d -> p t d", p=P)),
            (ident[:, :], ident_c), (gains[:, 0, :], g_mix), (gains[:, 1, :], g_ffn), (gains[:, 2, :], g_ple)])

        to_transposed_parts(nc, sem, psum, "mix", res, gains[:, 0, :], hT_hi, hT_lo, ident, True)
        with ExitStack() as mixer:
            proj = mixer.enter_context(nc.sbuf_tensor("proj", [P, TB, IN_W], F32))

            def keep_proj(dve, pair, i, tb, bank):
                return dve.tensor_copy(proj[:, tb, bass.ds((pair * 2 + i) * IN_PW, IN_PW)], bank)

            project(nc, sem, psum, "win", w_in, IN_PANELS, IN_PW, KC, hT_hi, hT_lo, keep_proj)
            attention(nc, sem, psum, proj, ident, hT_hi, hT_lo, q_norm, k_norm, sinks,
                      cos_c, sin_c, decay_c, wq_c, wk_c, chunk_c, mask_c)

        def add_to_res(dve, pair, i, tb, bank):
            at = res[:, tb, bass.ds((pair * 2 + i) * PW, PW)]
            return dve.tensor_tensor(at, bank, at, ALU.add)

        project(nc, sem, psum, "wout", w_out, PANELS, PW, KC, hT_hi, hT_lo, add_to_res)

        to_transposed_parts(nc, sem, psum, "ffn", res, gains[:, 1, :], hT_hi, hT_lo, ident, True)
        with ExitStack() as peer:
            first = FirstProducts(nc, peer, sem, psum, peer_u, hT_hi, hT_lo)
            spilled, stored = ([sem(f"{n}{i}") for i in range(2)] for n in ("spilled", "stored"))
            early = EarlyTiles(first, gelu_dram, spilled)
            with ExitStack() as routing:
                picks = [routing.enter_context(nc.sbuf_tensor(n, [P, TB, PICKS], F32))
                         for n in ("pick_i1", "pick_i2", "pick_gate")]
                with ExitStack() as route:
                    qT = route.enter_context(nc.sbuf_tensor("qT", [P, HALVES, SEQ], F32))

                    def keep_q(dve, pair, i, u, bank):
                        return dve.tensor_copy(qT[:, bass.ds((pair * 2 + i) * (PW // P) + u, 1), :]
                                               .rearrange("p o t -> p (o t)"), bank)

                    def load_first_tiles(sp):
                        for tile in range(2):
                            first.load(sp, (0, 2, tile), wait=False)

                    project(nc, sem, psum, "wqry", w_query, 2 * PANELS, PW, KC, hT_hi, hT_lo, keep_q, transposed=True,
                            then=load_first_tiles)
                    choose_experts(nc, sem, psum, qT, keys_t, picks, early)
                spread_gates(nc, sem, psum, picks, ident, gates_dram, stored, early)
            evaluate_experts(nc, sem, psum, res, first, early, stored, peer_v, gates_dram)

        to_transposed_parts(nc, sem, psum, "ple", res, gains[:, 2, :], hT_hi, hT_lo, ident, True)
        add_embedding(nc, sem, psum, res, hT_hi, hT_lo, p_t, w_gate, w_ple, out)


def attention(nc, sem, psum, proj, ident, hT_hi, hT_lo, q_norm, k_norm, sinks,
              cos_c, sin_c, decay_c, wq_c, wk_c, chunk_c, mask_c):
    PAIRS = RH // 2
    with ExitStack() as ctx:
        def sb(name, shape, dt=F32):
            return ctx.enter_context(nc.sbuf_tensor(name, shape, dt))

        mixed = sb("mixed", [P, TB, D])
        rqT, rkT, rqwT = (sb(n, [P, PAIRS, SEQ]) for n in ("rqT", "rkT", "rqwT"))
        sqT = sb("sqT", [P, PAIRS, SEQ])
        skT = sb("skT", [P, KVH, SEQ])
        kw = sb("kw", [P, TB, RW])
        mask = sb("mask", [P, 2 * P])
        decay = sb("decay", [P, RH, P])
        chunk = sb("chunk", [P, PAIRS])
        sink = sb("sink", [P, QH])
        small = sb("small", [P, 8, TB * (QH + KVH)])
        prepare(nc, sem, psum, proj, ident, q_norm, k_norm, cos_c, sin_c, wq_c, wk_c,
                rqT, rkT, rqwT, sqT, skT, kw, small,
                [(mask[:, :], mask_c), (decay[:, :, :], decay_c), (chunk[:, :], chunk_c), (sink[:, :], sinks)])
        retention(nc, sem, psum, proj, rqT, rkT, rqwT, kw, decay, chunk, mixed)
        sliding_window(nc, sem, psum, proj, sqT, skT, ident, mask, sink, mixed)
        to_transposed_parts(nc, sem, psum, "mixed", mixed, None, hT_hi, hT_lo, ident, False)


def prepare(nc, sem, psum, proj, ident, q_norm, k_norm, cos_c, sin_c, wq_c, wk_c,
            rqT, rkT, rqwT, sqT, skT, kw, small, loads):
    PAIRS = RH // 2
    NH = QH + KVH
    HALF = HD // 2
    with ExitStack() as ctx:
        def sb(name, shape, dt=F32):
            return ctx.enter_context(nc.sbuf_tensor(name, shape, dt))

        cos, sin = sb("cos", [P, TB, HALF]), sb("sin", [P, TB, HALF])
        wq = sb("wq", [P, PAIRS, P])
        wk = sb("wk", [P, RH])
        qn, kn = sb("qn", [P, 1]), sb("kn", [P, 1])
        rot = sb("rot", [P, TB, 2 * RH, HD])
        t1, t2 = sb("t1", [P, TB, 2 * RH, HALF]), sb("t2", [P, TB, 2 * RH, HALF])
        skn = sb("skn", [P, TB, KVH, 2, HD])
        loaded = sem("prep_loaded")
        steps, inv_ready, rstd_ready = sem("prep_steps"), sem("prep_inv"), sem("prep_rstd")
        rot_ready, norm_ready = sem("rot_ready"), sem("norm_ready")
        tr_full, tr_free, tr_evac = sem("tr_full"), sem("tr_free"), sem("tr_evac")
        all_loads = loads + [(cos[:, :, :], cos_c), (sin[:, :, :], sin_c), (wq[:, :, :], wq_c), (wk[:, :], wk_c),
                             (qn[:, :], q_norm), (kn[:, :], k_norm)]
        block = ctx.enter_context(nc.Block())

        @block.sync
        def _(sp):
            for dst, src in all_loads:
                sp.dma_start(dst, src).then_inc(loaded, 16)

        sqk = proj[:, :, SQ:SV].rearrange("p t (h d) -> p t h d", d=HD)
        ssq, mean, inv, rstd = (small[:, i, :].rearrange("p (t h) -> p t h", t=TB) for i in range(4))

        def wide(a, n):
            return a.unsqueeze(3).broadcast_to([P, a.shape[1], a.shape[2], n])

        @block.vector
        def _(dve):
            chain = Chain(dve, steps)
            sq = rot[:, :, 0:NH, :]
            chain.step(dve.tensor_tensor(sq, sqk, sqk, ALU.mult))
            chain.settle()
            chain.step(dve.tensor_reduce(ssq, sq, AX.X, ALU.add))
            chain.settle()
            chain.step(dve.tensor_scalar(mean, ssq, 1.0 / HD, EPS, ALU.mult, ALU.add))
            chain.settle()
            dve.reciprocal(inv, mean).then_inc(inv_ready, 1)
            dve.wait_ge(loaded, 16 * len(all_loads))
            qk = proj[:, :, RQ:RV].rearrange("p t (h d) -> p t h d", d=HD)
            x1, x2 = qk[:, :, :, 0:HALF], qk[:, :, :, HALF:HD]
            c = cos[:, :, :].unsqueeze(2).broadcast_to([P, TB, 2 * RH, HALF])
            s = sin[:, :, :].unsqueeze(2).broadcast_to([P, TB, 2 * RH, HALF])
            for part, (cx, sx, op) in enumerate(((x1, x2, ALU.subtract), (x2, x1, ALU.add))):
                chain.step(dve.tensor_tensor(t1[:, :, :, :], cx, c, ALU.mult))
                chain.step(dve.tensor_tensor(t2[:, :, :, :], sx, s, ALU.mult))
                chain.settle()
                chain.step(dve.tensor_tensor(rot[:, :, :, part * HALF:(part + 1) * HALF],
                                             t1[:, :, :, :], t2[:, :, :, :], op))
                chain.settle()
            dve.sem_inc(rot_ready, 1)
            chain.step(dve.tensor_tensor(kw[:, :, :].rearrange("p t (h d) -> p t h d", d=HD), rot[:, :, RH:2 * RH, :],
                                         wk[:, :].unsqueeze(1).unsqueeze(3).broadcast_to([P, TB, RH, HD]), ALU.mult))
            dve.wait_ge(rstd_ready, 1)
            for tb in range(TB):
                q_at = sqk[:, tb, 0:QH, :]
                chain.step(dve.tensor_tensor(q_at, q_at, rstd[:, tb, 0:QH].unsqueeze(2).broadcast_to([P, QH, HD]),
                                             ALU.mult))
            for twice in range(2):
                chain.step(dve.tensor_tensor(skn[:, :, :, twice, :], sqk[:, :, QH:NH, :], wide(rstd[:, :, QH:NH], HD),
                                             ALU.mult))
            chain.settle()
            dve.sem_inc(norm_ready, 1)
            for pair in range(PAIRS):
                dve.wait_ge(tr_evac, pair + 1)
                chain.step(dve.tensor_tensor(rqwT[:, pair, :].rearrange("p (t i) -> p t i", t=TB),
                                             rqT[:, pair, :].rearrange("p (t i) -> p t i", t=TB),
                                             wq[:, pair, :].unsqueeze(1).broadcast_to([P, TB, P]), ALU.mult))

        jobs = []
        for part, dst in ((0, rqT), (1, rkT)):
            for pair in range(PAIRS):
                jobs.append((lambda tb, h=part * RH + 2 * pair: rot[:, tb, h:h + 2, :].rearrange("p h d -> p (h d)"),
                             dst[:, pair, :], None))
        for pair in range(PAIRS):
            jobs.append((lambda tb, c=SQ + pair * P: proj[:, tb, c:c + P], sqT[:, pair, :], qn))
        for g in range(KVH):
            jobs.append((lambda tb, g=g: skn[:, tb, g, :, :].rearrange("p w d -> p (w d)"), skT[:, g, :], kn))

        @block.tensor
        def _(pe):
            for n, (source, _, gain) in enumerate(jobs):
                if n == 0:
                    pe.wait_ge(rot_ready, 1)
                if n == 2 * PAIRS:
                    pe.wait_ge(norm_ready, 1)
                if n >= 8:
                    pe.wait_ge(tr_evac, n - 7)
                for tb in range(TB):
                    last = pe.transpose(psum[n % 8][:, tb * P:(tb + 1) * P], source(tb), ident[:, :])
                last.then_inc(tr_full, 1)

        @block.scalar
        def _(act):
            act.wait_ge(inv_ready, 1)
            act.activation(rstd, inv, ACT.Sqrt).then_inc(rstd_ready, 1)
            for n, (_, dst, gain) in enumerate(jobs):
                act.wait_ge(tr_full, n + 1)
                if n == 0:
                    act.wait_ge(loaded, 16 * len(all_loads))
                act.activation(dst, psum[n % 8][:, :], ACT.Copy,
                               scale=gain[:, 0:1] if gain is not None else 1.0).then_inc(tr_evac, 1)


def retention(nc, sem, psum, proj, rqT, rkT, rqwT, kw, decay, chunk, mixed):
    PAIRS = RH // 2
    HH = RH // 2
    with ExitStack() as ctx:
        def sb(name, shape, dt=F32):
            return ctx.enter_context(nc.sbuf_tensor(name, shape, dt))

        attn = sb("attn", [P, RH, P])
        state = sb("state", [P, PAIRS, 2, HD])
        ret = sb("ret", [P, TB, RH, HD])
        sq = sb("ret_sq", [P, TB, RH, HD])
        gate = sb("ret_gate", [P, TB, RW])
        stats = sb("ret_stats", [P, 5, TB * RH])
        score_full, attn_done, out_full, kv_full = sem("score_full"), sem("attn_done"), sem("out_full"), sem("kv_full")
        state_done, out_copied, steps = sem("state_done"), sem("out_copied"), sem("ret_steps")
        silu_done, inv_done, root_done = sem("silu_done"), sem("ret_inv"), sem("ret_root")
        block = ctx.enter_context(nc.Block())

        def half(h):
            return slice((h % 2) * HD, (h % 2 + 1) * HD)

        @block.tensor
        def _(pe):
            for n in range(TB):
                t = slice(n * P, (n + 1) * P)
                for b in range(2):
                    if n:
                        pe.wait_ge(attn_done, 2 * (n - 1) + b + 1)
                    for pair in range(PAIRS):
                        last = pe.matmul(psum[b][:, pair * P:(pair + 1) * P], rkT[half(b), pair, t],
                                         rqT[half(b), pair, t], start=True, stop=True)
                    last.then_inc(score_full, 1)
                if n < TB - 1:
                    if n:
                        pe.wait_ge(state_done, n)
                    for pair in range(PAIRS):
                        last = pe.matmul(psum[2][:, pair * P:(pair + 1) * P], kw[:, n, pair * P:(pair + 1) * P],
                                         proj[:, n, RV + pair * P:RV + (pair + 1) * P], start=True, stop=True)
                    last.then_inc(kv_full, 1)
                if n >= 2:
                    pe.wait_ge(out_copied, n - 1)
                pe.wait_ge(attn_done, 2 * n + 2)
                if n:
                    pe.wait_ge(state_done, n)
                for h in range(RH):
                    o = psum[4 + n % 2][:, h * HD:(h + 1) * HD]
                    last = pe.matmul(o, attn[:, h % 2 * PAIRS + h // 2, :], proj[:, n, RV + h * HD:RV + (h + 1) * HD],
                                     start=True, stop=(n == 0))
                    if n:
                        last = pe.matmul(o, rqwT[:, h // 2, t], state[:, h // 2, h % 2, :],
                                         start=False, stop=True)
                last.then_inc(out_full, 1)

        @block.vector
        def _(dve):
            chain = Chain(dve, steps)
            chain.step(dve.memset(state[:, :, :, :], 0.0))
            chain.settle()
            for n in range(TB):
                for b in range(2):
                    dve.wait_ge(score_full, 2 * n + b + 1)
                    if n:
                        dve.wait_ge(out_full, n)
                    dve.tensor_tensor(attn[:, b * HH:(b + 1) * HH, :].rearrange("p h i -> p (h i)"), psum[b][:, :],
                                      decay[:, b * HH:(b + 1) * HH, :].rearrange("p h i -> p (h i)"),
                                      ALU.mult).then_inc(attn_done, 1)
                if n < TB - 1:
                    dve.wait_ge(kv_full, n + 1)
                    if n:
                        dve.wait_ge(out_full, n + 1)
                    for par in range(2):
                        rows = slice(par * HD, (par + 1) * HD)
                        kv = psum[2][rows, :].rearrange("p (a c) -> p a c", a=PAIRS)[:, :, par * HD:(par + 1) * HD]
                        if n:
                            for pair in range(PAIRS):
                                last = dve.scalar_tensor_tensor(
                                    out=state[rows, pair, par, :], in0=state[rows, pair, par, :], scalar=chunk[rows, pair:pair + 1],
                                    in1=kv[:, pair, :], op0=ALU.mult, op1=ALU.add)
                                chain.step(last)
                        else:
                            chain.step(dve.tensor_copy(state[rows, :, par, :], kv))
                    chain.settle()
                    dve.sem_inc(state_done, 1)
            total, mean, ssq, var, inv = (stats[:, i, :].rearrange("p (t h) -> p t h", t=TB) for i in range(5))
            dve.wait_ge(out_copied, TB)

            def flat(a):
                return a.rearrange("p t h -> p (t h)")

            r3 = ret[:, :, :, :].rearrange("p t h d -> p (t h) d")
            s3 = sq[:, :, :, :].rearrange("p t h d -> p (t h) d")
            chain.step(dve.tensor_reduce(flat(total), r3, AX.X, ALU.add))
            chain.settle()
            chain.step(dve.tensor_scalar(flat(mean), flat(total), 1.0 / HD, None, ALU.mult))
            chain.settle()
            chain.step(dve.tensor_tensor(r3, r3, flat(mean).unsqueeze(2).broadcast_to([P, TB * RH, HD]), ALU.subtract))
            chain.settle()
            chain.step(dve.tensor_tensor(s3, r3, r3, ALU.mult))
            chain.settle()
            chain.step(dve.tensor_reduce(flat(ssq), s3, AX.X, ALU.add))
            chain.settle()
            chain.step(dve.tensor_scalar(flat(var), flat(ssq), 1.0 / HD, EPS, ALU.mult, ALU.add))
            chain.settle()
            dve.reciprocal(flat(inv), flat(var)).then_inc(inv_done, 1)
            dve.wait_ge(root_done, 1)
            chain.step(dve.tensor_tensor(r3, r3, flat(total).unsqueeze(2).broadcast_to([P, TB * RH, HD]), ALU.mult))
            chain.settle()
            dve.wait_ge(silu_done, 1)
            chain.step(dve.tensor_tensor(mixed[:, :, 0:RW], ret[:, :, :, :].rearrange("p t h d -> p t (h d)"),
                                         gate[:, :, :], ALU.mult))

        @block.scalar
        def _(act):
            for n in range(TB):
                act.wait_ge(out_full, n + 1)
                act.activation(ret[:, n, :, :].rearrange("p h d -> p (h d)"), psum[4 + n % 2][:, :],
                               ACT.Copy).then_inc(out_copied, 1)
            act.activation(gate[:, :, :], proj[:, :, RG:SQ], ACT.Silu).then_inc(silu_done, 1)
            act.wait_ge(inv_done, 1)
            act.activation(stats[:, 0, :], stats[:, 4, :], ACT.Sqrt).then_inc(root_done, 1)


def sliding_window(nc, sem, psum, proj, sqT, skT, ident, mask, sink, mixed):
    SCALE = float(HD) ** -0.5
    with ExitStack() as ctx:
        def sb(name, shape, dt=F32):
            return ctx.enter_context(nc.sbuf_tensor(name, shape, dt))

        masked = sb("masked", [P, QH, 2 * P])
        prob = sb("prob", [P, QH, 2 * P])
        probT = sb("probT", [P, QH, 2, P])
        st = sb("swa_stats", [P, 8, QH])
        top, m, negm, sink_gap, sink_e, row_sum, den, rden = (st[:, i, :] for i in range(8))
        s_full, s_read, negm_ready, exp_done = sem("s_full"), sem("s_read"), sem("negm_ready"), sem("exp_done")
        pt_full, pt_copied, o_full, o_done, steps = (sem("pt_full"), sem("pt_copied"), sem("o_full"),
                                                     sem("o_done"), sem("swa_steps"))
        block = ctx.enter_context(nc.Block())
        blocks_of = [1] + [2] * (TB - 1)
        pt_banks = [0]
        for n in range(TB):
            pt_banks.append(pt_banks[-1] + 2 * blocks_of[n])

        @block.tensor
        def _(pe):
            for n in range(TB):
                nb = blocks_of[n]
                for b in range(4):
                    if n:
                        pe.wait_ge(s_read, 4 * (n - 1) + b + 1)
                    for i in range(2):
                        h = b // 2 * 4 + b % 2 + 2 * i
                        half = slice((h % 2) * HD, (h % 2 + 1) * HD)
                        last = pe.matmul(psum[b][:, i * 256:i * 256 + nb * P],
                                         sqT[half, h // 2, n * P:(n + 1) * P],
                                         skT[half, h // (QH // KVH), (n + 1 - nb) * P:(n + 1) * P],
                                         start=True, stop=True)
                    last.then_inc(s_full, 1)
                done = pt_banks[n]
                for q in range(2 * nb):
                    if done + q >= 2:
                        pe.wait_ge(pt_copied, done + q - 1)
                    for k in range(4):
                        h, kb = (4 * q + k) // nb, (4 * q + k) % nb
                        pe.wait_ge(exp_done, QH * n + h + 1)
                        last = pe.transpose(psum[4 + (done + q) % 2][:, k * P:(k + 1) * P],
                                            prob[:, h, kb * P:(kb + 1) * P], ident[:, :])
                    last.then_inc(pt_full, 1)
                pe.wait_ge(pt_copied, pt_banks[n + 1])
                if n >= 1:
                    pe.wait_ge(o_done, n)
                for h in range(QH):
                    for kb in range(nb):
                        vb = n + 1 - nb + kb
                        vc = SV + (h // (QH // KVH)) * HD
                        last = pe.matmul(psum[6][:, h * HD:(h + 1) * HD], probT[:, h, kb, :],
                                         proj[:, vb, vc:vc + HD], start=(kb == 0), stop=(kb == nb - 1))
                last.then_inc(o_full, 1)

        @block.vector
        def _(dve):
            chain = Chain(dve, steps)
            for n in range(TB):
                nb = blocks_of[n]
                if n:
                    dve.wait_ge(exp_done, QH * n)
                for b in range(4):
                    dve.wait_ge(s_full, 4 * n + b + 1)
                    h0 = b // 2 * 4 + b % 2
                    dve.tensor_tensor(masked[:, h0:h0 + 3:2, 0:nb * P],
                                      psum[b][:, :].rearrange("p (h k) -> p h k", h=2)[:, :, 0:nb * P],
                                      mask[:, 2 * P - nb * P:2 * P].unsqueeze(1).broadcast_to([P, 2, nb * P]),
                                      ALU.add).then_inc(s_read, 1)
                dve.wait_ge(s_read, 4 * n + 4)
                chain.step(dve.tensor_reduce(top, masked[:, :, 0:nb * P], AX.X, ALU.max))
                chain.settle()
                chain.step(dve.scalar_tensor_tensor(out=m, in0=top, scalar=SCALE, in1=sink[:, :],
                                                    op0=ALU.mult, op1=ALU.max))
                chain.settle()
                chain.step(dve.tensor_scalar(negm, m, -1.0, None, ALU.mult))
                chain.step(dve.tensor_tensor(sink_gap, sink[:, :], m, ALU.subtract))
                chain.settle()
                dve.sem_inc(negm_ready, 1)
                dve.wait_ge(exp_done, QH * (n + 1))
                chain.step(dve.tensor_tensor(den, row_sum, sink_e, ALU.add))
                chain.settle()
                chain.step(dve.reciprocal(rden, den))
                chain.settle()
                dve.wait_ge(o_full, n + 1)
                dve.tensor_tensor(mixed[:, n, RW:].rearrange("p (h d) -> p h d", d=HD),
                                  psum[6][:, :].rearrange("p (h d) -> p h d", d=HD),
                                  rden.unsqueeze(2).broadcast_to([P, QH, HD]), ALU.mult).then_inc(o_done, 1)

        @block.scalar
        def _(act):
            for n in range(TB):
                nb = blocks_of[n]
                act.wait_ge(negm_ready, n + 1)
                act.activation(sink_e, sink_gap, ACT.Exp)
                for h in range(QH):
                    act.activation(prob[:, h, 0:nb * P], masked[:, h, 0:nb * P], ACT.Exp, bias=negm[:, h:h + 1],
                                   scale=SCALE, accum_out=row_sum[:, h:h + 1]).then_inc(exp_done, 1)
                flat = probT[:, :, 0:nb, :]
                for q in range(2 * nb):
                    act.wait_ge(pt_full, pt_banks[n] + q + 1)
                    if n and q == 0:
                        act.wait_ge(o_full, n)
                    heads = 4 // nb
                    act.activation(flat[:, q * heads:(q + 1) * heads, :, :],
                                   psum[4 + (pt_banks[n] + q) % 2][:, :].rearrange("p (h k i) -> p h k i", h=heads, k=nb),
                                   ACT.Copy).then_inc(pt_copied, 1)


def choose_experts(nc, sem, psum, qT, keys_t, picks, early):
    K = EARLY_PER_BLOCK
    SCORES_AT = K - 3
    EXP_AT = K - 2
    first = early.first
    pick_i1, pick_i2, pick_gate = picks
    with ExitStack() as ctx:
        def sb(name, shape, dt=F32):
            return ctx.enter_context(nc.sbuf_tensor(name, shape, dt))

        keys = sb("keys", [P, 2, KEYS])
        q_next = sb("q_next", [P, HALVES, P])
        top_s = sb("top_s", [P, HALVES, TOPK])
        top_i = sb("top_i", [P, HALVES, TOPK], U32)
        top_f = sb("top_f", [P, HALVES, TOPK])
        rest = sb("rest", [P, HALVES, KEYS])
        cand = sb("cand", [P, PH, CANDS])
        crest = sb("crest", [P, PH, CANDS])
        best = sb("best", [P, PH, TOPK])
        pos = sb("pos", [P, PH, TOPK], U32)
        pos_ab = sb("pos_ab", [P, 4, PICKS], U32)
        pos_f = sb("pos_f", [P, 4, PICKS])
        pos_all = sb("pos_all", [P, PICKS])
        iota_i = sb("iota16_i", [P, TOPK], I32)
        iota = sb("iota16", [P, TOPK])
        hit = [sb(f"hit{i}", [P, PICKS, TOPK]) for i in range(2)]
        gap, expd = sb("gap", [P, PH, TOPK]), sb("expd", [P, PH, TOPK])
        total, inv = sb("gate_total", [P, PH]), sb("gate_inv", [P, PH])
        loaded, iota_done, sc_full, sc_free = sem("keys_loaded"), sem("iota_done"), sem("sc_full"), sem("sc_free")
        q_copied = sem("q_copied")
        gap_ready, exp_ready, steps = sem("gap_ready"), sem("exp_ready"), sem("topk_steps")
        block = ctx.enter_context(nc.Block())

        @block.sync
        def _(sp):
            sp.dma_start(keys[:, :, :], keys_t).then_inc(loaded, 16)
            sp.sem_inc(early.spilled[0], 16)
            sp.sem_inc(early.spilled[1], 16)
            first.load(sp, (0, K, 2))
            with sp.Fori(0, TB) as tb:
                for c in range(K):
                    early.sync(sp, (tb, K, c))

        @block.gpsimd
        def _(pool):
            pool.iota(iota_i[:, :], pattern=[[1, TOPK]], base=0, channel_multiplier=0).then_inc(iota_done, 1)
            with pool.Fori(0, TB - 1) as tb:
                pool.wait_ge(sc_full, tb + 1)
                pool.dma_start(q_next[:, :, :], qT[:, :, bass.ds(tb * P + P, P)]).then_inc(q_copied, 16)

        @block.tensor
        def _(pe):
            def scores(q):
                for hp in range(HALVES):
                    last = pe.matmul(psum[hp // 4][:, (hp % 4) * KEYS:(hp % 4 + 1) * KEYS],
                                     q[:, hp, :],
                                     keys[:, hp % 2, :], start=True, stop=True)
                last.then_inc(sc_full, 1)

            pe.sem_inc(first.full, 2)
            pe.wait_ge(loaded, 16)
            scores(qT[:, :, 0:P])
            with pe.Fori(0, TB - 1) as tb:
                for c in range(K):
                    early.tensor(pe, (tb, K, c))
                    if c == SCORES_AT:
                        pe.wait_ge(sc_free, tb + 1)
                        pe.wait_ge(q_copied, tb * 16 + 16)
                        scores(q_next)
            for c in range(K):
                early.tensor(pe, (0, K, (TB - 1) * K + c))

        @block.scalar
        def _(act):
            act.sem_inc(first.gelu_done, 2)
            first.split_hi(act, (0, K, 0))
            with act.Fori(0, TB) as tb:
                for c in range(K):
                    if c == EXP_AT:
                        act.wait_ge(gap_ready, tb + 1)
                        act.activation(expd[:, :, :], gap[:, :, :], ACT.Exp).then_inc(exp_ready, 1)
                    early.scalar(act, (tb, K, c))

        @block.vector
        def _(dve):
            settled = sem("topk_settled")
            chain = Chain(dve, steps, settled)

            def score(hp):
                return psum[hp // 4][:, (hp % 4) * KEYS:(hp % 4 + 1) * KEYS]

            dve.wait_ge(iota_done, 1)
            chain.step(dve.tensor_copy(iota[:, :], iota_i[:, :]))
            chain.settle()
            dve.sem_inc(first.lo_done, 2)
            first.split_lo(dve, (0, K, 0))
            PER_BLOCK = 5 * HALVES + 3 + 5 * PH + 20
            base = chain.n
            with dve.Fori(0, TB) as tb:
                chain.off = tb * PER_BLOCK
                beside = iter(range(K))

                def early_step():
                    early.vector(dve, (tb, K, next(beside)))

                early_step()
                dve.wait_ge(sc_full, tb + 1)
                dve.sem_inc(settled, 1)
                for hp in range(HALVES):
                    chain.step(dve.max(top_s[:, hp, 0:8], score(hp)))
                early_step()
                chain.settle()
                for hp in range(HALVES):
                    chain.step(dve.max_index(top_i[:, hp, 0:8], top_s[:, hp, 0:8], score(hp)))
                early_step()
                dve.sem_inc(settled, 1)
                for hp in range(HALVES):
                    chain.step(dve.match_replace(rest[:, hp, :], top_s[:, hp, 0:8], score(hp), NEG))
                early_step()
                chain.settle()
                dve.sem_inc(sc_free, 1)
                for hp in range(HALVES):
                    chain.step(dve.max(top_s[:, hp, 8:16], rest[:, hp, :]))
                early_step()
                chain.settle()
                for hp in range(HALVES):
                    chain.step(dve.max_index(top_i[:, hp, 8:16], top_s[:, hp, 8:16], rest[:, hp, :]))
                early_step()
                s4 = top_s[:, :, :].rearrange("p (h two) k -> p h two k", two=2)
                whole = FULL_A * TOPK
                for at, n_a, n_b, a0 in ((cand[:, :, 0:whole], FULL_A, TOPK, 0),
                                         (cand[:, :, whole:], TOPK - FULL_A, FULL_A, FULL_A)):
                    chain.step(dve.tensor_tensor(at.rearrange("p h (a b) -> p h a b", a=n_a),
                                                 s4[:, :, 0, a0:a0 + n_a].unsqueeze(3).broadcast_to([P, PH, n_a, n_b]),
                                                 s4[:, :, 1, 0:n_b].unsqueeze(2).broadcast_to([P, PH, n_a, n_b]), ALU.add))
                chain.settle()
                chain.step(dve.tensor_copy(top_f[:, :, :], top_i[:, :, :]))
                for h in range(PH):
                    chain.step(dve.max(best[:, h, 0:8], cand[:, h, :]))
                chain.settle()
                for h in range(PH):
                    chain.step(dve.max_index(pos[:, h, 0:8], best[:, h, 0:8], cand[:, h, :]))
                early_step()
                dve.sem_inc(settled, 1)
                for h in range(PH):
                    chain.step(dve.match_replace(crest[:, h, :], best[:, h, 0:8], cand[:, h, :], NEG))
                chain.settle()
                for h in range(PH):
                    chain.step(dve.max(best[:, h, 8:16], crest[:, h, :]))
                chain.settle()
                for h in range(PH):
                    chain.step(dve.max_index(pos[:, h, 8:16], best[:, h, 8:16], crest[:, h, :]))
                dve.tensor_tensor(gap[:, :, :], best[:, :, :], best[:, :, 0:1].broadcast_to([P, PH, TOPK]),
                                  ALU.subtract).then_inc(gap_ready, 1)
                early_step()
                chain.settle()
                p2 = pos[:, :, :].rearrange("p h k -> p (h k)")
                for i, (amount, op) in enumerate(((4, ALU.logical_shift_right), (TOPK - 1, ALU.bitwise_and),
                                                  (2, ALU.logical_shift_right), (FULL_A - 1, ALU.bitwise_and))):
                    chain.step(dve.tensor_scalar(pos_ab[:, i, :], p2, amount, None, op))
                chain.settle()
                chain.step(dve.tensor_copy(pos_f[:, :, :], pos_ab[:, :, :]))
                chain.step(dve.tensor_copy(pos_all[:, :], p2))
                chain.settle()
                chain.step(dve.tensor_scalar(pos_all[:, :], pos_all[:, :], float(whole), None, ALU.is_ge))
                chain.step(dve.tensor_scalar(pos_f[:, 2, :], pos_f[:, 2, :], float(whole // FULL_A - FULL_A), None,
                                             ALU.subtract))
                chain.settle()
                chain.step(dve.tensor_tensor(pos_f[:, 2:4, :], pos_f[:, 2:4, :], pos_f[:, 0:2, :], ALU.subtract))
                chain.settle()
                chain.step(dve.tensor_tensor(pos_f[:, 2:4, :], pos_f[:, 2:4, :],
                                             pos_all[:, :].unsqueeze(1).broadcast_to([P, 2, PICKS]), ALU.mult))
                chain.settle()
                chain.step(dve.tensor_tensor(pos_f[:, 0:2, :], pos_f[:, 0:2, :], pos_f[:, 2:4, :], ALU.add))
                early_step()
                chain.settle()
                f4 = top_f[:, :, :].rearrange("p (h two) k -> p h two k", two=2)
                for half in range(2):
                    chain.step(dve.tensor_tensor(hit[half][:, :, :],
                                                 pos_f[:, half, :].unsqueeze(2).broadcast_to([P, PICKS, TOPK]),
                                                 iota[:, :].unsqueeze(1).broadcast_to([P, PICKS, TOPK]), ALU.is_equal))
                early_step()
                chain.settle()
                for half in range(2):
                    at = hit[half][:, :, :].rearrange("p (h k) a -> p h k a", h=PH)
                    chain.step(dve.tensor_tensor(at, at, f4[:, :, half, :].unsqueeze(2)
                                                 .broadcast_to([P, PH, TOPK, TOPK]), ALU.mult))
                early_step()
                chain.settle()
                for half, dst in enumerate((pick_i1, pick_i2)):
                    chain.step(dve.tensor_reduce(dst[:, bass.ds(tb, 1), :].rearrange("p o k -> p (o k)"),
                                                 hit[half][:, :, :], AX.X, ALU.add))
                early_step()
                dve.wait_ge(exp_ready, tb + 1)
                chain.step(dve.tensor_reduce(total[:, :], expd[:, :, :], AX.X, ALU.add))
                chain.settle()
                chain.step(dve.reciprocal(inv[:, :], total[:, :]))
                chain.settle()
                chain.step(dve.tensor_tensor(pick_gate[:, bass.ds(tb, 1), :]
                                             .rearrange("p o (h k) -> p (o h) k", h=PH), expd[:, :, :],
                                             inv[:, :].unsqueeze(2).broadcast_to([P, PH, TOPK]), ALU.mult))
                chain.settle()
                assert chain.n - base == PER_BLOCK and next(beside, None) is None, chain.n - base


def spread_gates(nc, sem, psum, picks, ident, gates_dram, stored, early):
    CH = SEQ // TCH
    QUADS = TCH // 4
    K = EARLY_PER_CHUNK
    START = EARLY_PER_BLOCK * TB
    BANKS = 4
    assert START + K * CH == EARLY
    with ExitStack() as ctx:
        def sb(name, shape, dt=F32):
            return ctx.enter_context(nc.sbuf_tensor(name, shape, dt))

        i1T, i2T, gT_hi, gT_lo = (sb(n, [P, SEQ], F16) for n in ("i1T", "i2T", "gT_hi", "gT_lo"))
        iota = sb("iota128", [P, KEYS, 4], F16)
        hot1, hot2_hi, hot2_lo = ([sb(f"{n}{b}", [P, QUADS, KEYS, 4], F16) for b in range(2)]
                                  for n in ("hot1_", "hot2hi_", "hot2lo_"))
        hot2 = sb("hot2", [P, QUADS, KEYS, 4], F16)
        iota_i = hot2[:, 0:2, :, :].rearrange("p q k w -> p (q k w)").bitcast(I32)
        stage = [sb(f"stage{b}", [P, KEYS, GST], F32) for b in range(2)]
        turned, iota_done, cols_done, steps = sem("picks_turned"), sem("iota128_done"), sem("cols_done"), sem("hot_steps")
        hots_ready, hots_used, quad_full, quad_free = sem("hots_ready"), sem("hots_used"), sem("quad_full"), sem("quad_free")
        stage_full = sem("stage_full")
        block = ctx.enter_context(nc.Block())

        @block.gpsimd
        def _(pool):
            pool.iota(iota_i, pattern=[[1, KEYS], [0, 4]], base=0, channel_multiplier=0)\
                .then_inc(iota_done, 1)

        @block.vector
        def _(dve):
            dve.wait_ge(iota_done, 1)
            dve.tensor_copy(iota[:, :, :].rearrange("p k f -> p (k f)"), iota_i).then_inc(cols_done, 1)
            for n, dst in enumerate((i1T, i2T, gT_hi)):
                dve.wait_ge(turned, n + 1)
                dve.tensor_scalar(dst[:, :], psum[n][:, :], GATE_SCALE if n == 2 else 1.0, None,
                                  ALU.mult).then_inc(cols_done, 1)
            dve.wait_ge(cols_done, 4)
            dve.scalar_tensor_tensor(out=gT_lo[:, :], in0=psum[2][:, :], scalar=GATE_SCALE, in1=gT_hi[:, :],
                                     op0=ALU.mult, op1=ALU.subtract).then_inc(cols_done, 1)
            dve.wait_ge(cols_done, 5)
            dve.sem_inc(hots_used, 2)

            def rows(t0, src):
                return src[:, bass.ds(t0, TCH)].rearrange("p (q f) -> p q f", f=4).unsqueeze(2)\
                    .broadcast_to([P, QUADS, KEYS, 4])

            keys_row = iota[:, :, :].unsqueeze(1).broadcast_to([P, QUADS, KEYS, 4])
            with dve.Fori(0, CH // 2) as pair:
                for b in range(2):
                    t0 = (pair * 2 + b) * TCH
                    done = (pair * 2 + b) * 4
                    dve.wait_ge(hots_used, pair * 2 + b + 1)
                    dve.tensor_tensor(hot1[b][:, :, :, :], rows(t0, i1T), keys_row, ALU.is_equal).then_inc(steps, 1)
                    dve.tensor_tensor(hot2[:, :, :, :], rows(t0, i2T), keys_row, ALU.is_equal).then_inc(steps, 1)
                    early.vector(dve, (pair, 2 * K, START + b * K))
                    dve.wait_ge(steps, done + 2)
                    dve.tensor_tensor(hot2_hi[b][:, :, :, :], hot2[:, :, :, :], rows(t0, gT_hi),
                                      ALU.mult).then_inc(steps, 1)
                    dve.tensor_tensor(hot2_lo[b][:, :, :, :], hot2[:, :, :, :], rows(t0, gT_lo),
                                      ALU.mult).then_inc(steps, 1)
                    dve.wait_ge(steps, done + 4)
                    dve.sem_inc(hots_ready, 1)

        @block.tensor
        def _(pe):
            for n, src in enumerate(picks):
                for tb in range(TB):
                    last = pe.transpose(psum[n][:, tb * P:(tb + 1) * P], src[:, tb, :], ident[:, :])
                last.then_inc(turned, 1)
            pe.wait_ge(cols_done, 5)
            with pe.Fori(0, CH // 2) as pair:
                for b in range(2):
                    early.tensor(pe, (pair, 2 * K, START + b * K))
                    pe.wait_ge(hots_ready, pair * 2 + b + 1)
                    for q in range(QUADS):
                        bank = psum[q % BANKS]
                        pe.wait_ge(quad_free, (pair * 2 + b) * QUADS + q + 1)
                        for f in range(4):
                            out = bank[:, f * KEYS:(f + 1) * KEYS]
                            pe.matmul(out, hot1[b][:, q, :, f], hot2_hi[b][:, q, :, f], start=True, stop=False)
                            last = pe.matmul(out, hot1[b][:, q, :, f], hot2_lo[b][:, q, :, f], start=False, stop=True)
                        last.then_inc(quad_full, 1)
                    pe.wait_ge(quad_full, (pair * 2 + b) * QUADS + QUADS)
                    pe.sem_inc(hots_used, 1)

        per_stage = GST // 4

        @block.scalar
        def _(act):
            act.preload_act_table(ACT.Gelu)
            act.sem_inc(quad_free, BANKS)
            act.sem_inc(stored[0], 16)
            act.sem_inc(stored[1], 16)
            with act.Fori(0, SEQ // GST // 2) as pair:
                for b in range(2):
                    act.wait_ge(stored[b], pair * 16 + 16)
                    for q in range(per_stage):
                        if q % QUADS == 0:
                            early.scalar(act, (pair, 4 * K, START + (2 * b + q // QUADS) * K))
                        act.wait_ge(quad_full, (pair * 2 + b) * per_stage + q + 1)
                        act.activation(stage[b][:, :, 4 * q:4 * q + 4].rearrange("p k f -> p f k"),
                                       psum[q % BANKS][:, :].rearrange("p (f k) -> p f k", f=4), ACT.Copy,
                                       scale=1.0 / GATE_SCALE).then_inc(quad_free, 1)
                    act.wait_ge(quad_free, (pair * 2 + b) * per_stage + per_stage + BANKS)
                    act.sem_inc(stage_full, 1)

        @block.sync
        def _(sp):
            with sp.Fori(0, SEQ // GST // 2) as pair:
                for b in range(2):
                    for chunk in range(2):
                        early.sync(sp, (pair, 4 * K, START + (2 * b + chunk) * K))
                    sp.wait_ge(stage_full, pair * 2 + b + 1)
                    sp.dma_start(gates_dram[bass.ds(pair * 2 + b, 1), :, :, :].rearrange("o p k t -> (o p) k t"),
                                 stage[b][:, :, :]).then_inc(stored[b], 16)


def evaluate_experts(nc, sem, psum, res, first, early, stored, peer_v, gates_dram):
    G = GROUP
    RING = 2 * G
    OUTS = TB * D // BANK
    Y_BANKS = 4
    TBL = SEQ // GST
    PRELOADED, PRESPLIT = 3, 1
    with ExitStack() as ctx:
        def sb(name, shape, dt=F32):
            return ctx.enter_context(nc.sbuf_tensor(name, shape, dt))

        v_raw = [sb(f"v_raw{i}", [P, D]) for i in range(2)]
        v_hi = [sb(f"v_hi{i}", [P, D], F32R) for i in range(RING)]
        v_lo = [sb(f"v_lo{i}", [P, D], F32R) for i in range(RING)]
        gates = [sb(f"gates{i}", [P, TBL, G, GST]) for i in range(2)]
        gelu_early = [sb(f"gelu_early{i}", [P, SEQ]) for i in range(G)]
        a_hi = [sb(f"a_hi{i}", [P, SEQ], F32R) for i in range(RING)]
        a_lo = [sb(f"a_lo{i}", [P, SEQ], F32R) for i in range(RING)]
        v_in, g_in, early_in = ([sem(f"{n}_in{i}") for i in range(many)]
                                for n, many in (("v", 2), ("gate", 2), ("early", G)))
        v_hi_done, v_lo_done = sem("v_hi_done"), sem("v_lo_done")
        gated, a_hi_done, a_lo_done = sem("gated"), sem("a_hi_done"), sem("a_lo_done")
        y_full, y_added = sem("y_full"), sem("y_added")
        block = ctx.enter_context(nc.Block())

        def count(m, c, per=1):
            return m * (RING * per) + c * per if c or not isinstance(m, int) or m else 0

        def reached(eng, semaphore, value):
            if not isinstance(value, int) or value > 0:
                eng.wait_ge(semaphore, value)

        def late(c):
            return c % RING < G

        def tile_of(m, c):
            return m, G, c // RING * G + (EARLY + c % RING if late(c) else c % RING - G)

        def v_landed(m, c):
            return m * (RING // 2 * 16) + (c // 2 + 1) * 16

        def once_landed(m, c):
            return m * 16 + (c // RING + 1) * 16

        def activations(c):
            return first.out[c % 2] if late(c) else gelu_early[c % G]

        @block.sync
        def _(sp):
            def load(m, c):
                tile = first.number(tile_of(m, c))
                if late(c) and c > PRELOADED:
                    first.load(sp, tile_of(m, c))
                if c % G == 0:
                    reached(sp, gated, count(m, c - G))
                    sp.dma_start(gates[c // G % 2][:, :, :, :], gates_dram[:, :, bass.ds(tile, G), :]
                                 .rearrange("b p k t -> p b k t")).then_inc(g_in[c // G % 2], 16)
                reached(sp, v_lo_done, count(m, c - 1))
                sp.dma_start(v_raw[c % 2][:, :], peer_v[bass.ds(tile, 1), :, :].rearrange("o p d -> (o p) d"))\
                    .then_inc(v_in[c % 2], 16)
                if not late(c):
                    reached(sp, a_lo_done, count(m, c - RING + 1))
                    sp.dma_start(gelu_early[c % G][:, :], early.dram[bass.ds(tile, 1), :, :]
                                 .rearrange("o p t -> (o p) t")).then_inc(early_in[c % G], 16)

            first.load(sp, tile_of(0, PRELOADED))
            for b in range(2):
                early.wait_stored(sp, b)
                sp.wait_ge(stored[b], SEQ // GST // 2 * 16 + 16)
            for c in range(RING):
                load(0, c)
            with sp.Fori(0, TILES // RING - 1) as ring:
                for c in range(RING):
                    load(ring, RING + c)

        def slots(eng, front, back):
            with eng.Fori(0, TILES // RING - 1) as ring:
                for c in range(RING, 2 * RING):
                    if late(c):
                        front(ring, c)
                    back(ring, c - 1)
            back(0, TILES - 1)

        @block.scalar
        def _(act):
            def front(m, c):
                first.split_hi(act, tile_of(m, c))

            def back(m, c, gelu=True):
                r = c % RING
                if r % G == 0:
                    reached(act, y_full, count(m, c - RING + G, OUTS // G))
                act.wait_ge(v_in[c % 2], v_landed(m, c))
                act.activation(v_hi[r][:, :], v_raw[c % 2][:, :], ACT.Copy).then_inc(v_hi_done, 1)
                if late(c) and gelu:
                    reached(act, a_lo_done, count(m, c - 1 if r >= 2 else c - 1 - G))
                    first.gelu(act, tile_of(m, c))
                act.wait_ge(gated, count(m, c + 1))
                act.activation(a_hi[r][:, :], activations(c)[:, :], ACT.Copy).then_inc(a_hi_done, 1)

            act.preload_act_table(ACT.Gelu)
            for c in range(PRESPLIT, G):
                front(0, c)
                if c <= 2:
                    early.wait_stored(act, c - 1)
                    first.gelu(act, tile_of(0, c - 1))
            for c in range(RING - 1):
                back(0, c, gelu=c >= 2)
            slots(act, front, back)

        @block.vector
        def _(dve):
            def add_output(m, c, n):
                dve.wait_ge(y_full, count(m, c // G * G - G, OUTS // G) + (n + 1))
                at = res[:, n // 2, n % 2 * BANK:(n % 2 + 1) * BANK]
                dve.tensor_tensor(at, psum[n % Y_BANKS][:, :], at, ALU.add).then_inc(y_added, 1)

            def front(m, c):
                first.split_lo(dve, tile_of(m, c))

            def back(m, c):
                r = c % RING
                dve.wait_ge(v_hi_done, count(m, c + 1))
                dve.tensor_tensor(v_lo[r][:, :], v_raw[c % 2][:, :], v_hi[r][:, :].bitcast(F32),
                                  ALU.subtract).then_inc(v_lo_done, 1)
                if late(c):
                    dve.wait_ge(first.gelu_done, first.number(tile_of(m, c)) + 3)
                else:
                    dve.wait_ge(early_in[c % G], once_landed(m, c))
                if c % G == 0:
                    dve.wait_ge(g_in[c // G % 2], once_landed(m, c))
                a = activations(c)
                by_block = a[:, :].rearrange("p (b t) -> p b t", b=TBL)
                dve.tensor_tensor(by_block, by_block, gates[c // G % 2][:, :, c % G, :], ALU.mult).then_inc(gated, 1)
                dve.wait_ge(a_hi_done, count(m, c + 1))
                dve.tensor_tensor(a_lo[r][:, :], a[:, :], a_hi[r][:, :].bitcast(F32),
                                  ALU.subtract).then_inc(a_lo_done, 1)
                if c >= G:
                    for n in range(2 * (r % G), 2 * (r % G) + 2):
                        add_output(m, c, n)

            for c in range(PRESPLIT, G):
                front(0, c)
            for c in range(RING - 1):
                back(0, c)
            slots(dve, front, back)
            for n in range(OUTS):
                add_output(0, TILES, n)

        @block.tensor
        def _(pe):
            def output(m, c, n):
                r = c % RING
                if n == 0:
                    pe.wait_ge(v_lo_done, count(m, c + G))
                    pe.wait_ge(a_lo_done, count(m, c + G))
                reached(pe, y_added, count(m, c, OUTS // G) + (n + 1 - Y_BANKS))
                t, d = slice(n // 2 * P, (n // 2 + 1) * P), slice(n % 2 * BANK, (n % 2 + 1) * BANK)
                split_product(pe, psum[n % Y_BANKS][:, :],
                              [((a_hi[r + i][:, t], a_lo[r + i][:, t]), (v_hi[r + i][:, d], v_lo[r + i][:, d]))
                               for i in range(G)]).then_inc(y_full, 1)

            def slot(m, c):
                if late(c):
                    first.product(pe, tile_of(m, c))
                if c >= G:
                    for n in range(2 * (c % G), 2 * (c % G) + 2):
                        output(m, c // G * G - G, n)

            for c in range(RING):
                slot(0, c)
            with pe.Fori(0, TILES // RING - 1) as ring:
                for c in range(RING, 2 * RING):
                    slot(ring, c)
            for n in range(OUTS):
                output(0, TILES - G, n)


def add_embedding(nc, sem, psum, res, hT_hi, hT_lo, p_t, w_gate, w_ple, out):
    PC = PLE // P
    with ExitStack() as ctx:
        def sb(name, shape, dt=F32):
            return ctx.enter_context(nc.sbuf_tensor(name, shape, dt))

        p_raw, p_hi, p_lo = sb("p_raw", [P, PC, SEQ]), sb("p_hi", [P, PC, SEQ], F32R), sb("p_lo", [P, PC, SEQ], F32R)
        e_raw, e_hi, e_lo = sb("e_raw", [P, PC, D]), sb("e_hi", [P, PC, D], F32R), sb("e_lo", [P, PC, D], F32R)
        g_raw = [sb(f"g_raw{i}", [P, KC, BANK]) for i in range(2)]
        g_hi = [sb(f"g_hi{i}", [P, KC, BANK], F32R) for i in range(2)]
        g_lo = [sb(f"g_lo{i}", [P, KC, BANK], F32R) for i in range(2)]
        sig = [sb(f"sig{i}", [P, BANK]) for i in range(4)]
        loaded = [sem(f"ple_loaded{i}") for i in range(4)]
        hi_done, lo_done, bank_full, sig_done, mult_done, sum_done, stored = (
            sem("ple_hi"), sem("ple_lo"), sem("ple_full"), sem("sig_done"), sem("mult_done"), sem("sum_done"),
            sem("out_stored"))
        splits = [(p_raw, p_hi, p_lo), (e_raw, e_hi, e_lo), (g_raw[0], g_hi[0], g_lo[0]), (g_raw[1], g_hi[1], g_lo[1])]
        sources = [p_t, w_ple, w_gate[0], w_gate[1]]
        units = [(i, tb) for i in range(2) for tb in range(TB)]
        block = ctx.enter_context(nc.Block())

        @block.sync
        def _(sp):
            for n, (raw, _, _) in enumerate(splits):
                sp.dma_start(raw[:, :, :], sources[n]).then_inc(loaded[n], 16)
            for n, (i, tb) in enumerate(units):
                sp.wait_ge(sum_done, n + 1)
                sp.dma_start(out[tb * P:(tb + 1) * P, i * BANK:(i + 1) * BANK],
                             res[:, tb, i * BANK:(i + 1) * BANK]).then_inc(stored, 16)
            sp.wait_ge(stored, 16 * len(units))

        @block.scalar
        def _(act):
            for n, (raw, hi, _) in enumerate(splits):
                act.wait_ge(loaded[n], 16)
                act.activation(hi[:, :, :], raw[:, :, :], ACT.Copy).then_inc(hi_done, 1)
            for n in range(len(units)):
                act.wait_ge(bank_full, n + 1)
                if n >= 4:
                    act.wait_ge(sum_done, n - 3)
                act.activation(sig[n % 4][:, :], psum[n % 4][:, :], ACT.Sigmoid).then_inc(sig_done, 1)

        @block.vector
        def _(dve):
            for n, (raw, hi, lo) in enumerate(splits):
                dve.wait_ge(hi_done, n + 1)
                dve.tensor_tensor(lo[:, :, :], raw[:, :, :], hi[:, :, :].bitcast(F32), ALU.subtract)\
                   .then_inc(lo_done, 1)
            for n, (i, tb) in enumerate(units):
                dve.wait_ge(sig_done, n + 1)
                dve.tensor_tensor(sig[n % 4][:, :], psum[4 + n % 4][:, :], sig[n % 4][:, :], ALU.mult)\
                   .then_inc(mult_done, 1)
                dve.wait_ge(mult_done, n + 1)
                at = res[:, tb, i * BANK:(i + 1) * BANK]
                dve.tensor_tensor(at, at, sig[n % 4][:, :], ALU.add).then_inc(sum_done, 1)

        @block.tensor
        def _(pe):
            for n, (i, tb) in enumerate(units):
                t = slice(tb * P, (tb + 1) * P)
                if tb == 0:
                    pe.wait_ge(lo_done, 3 + i)
                if n >= 4:
                    pe.wait_ge(mult_done, n - 3)
                split_product(pe, psum[4 + n % 4][:, :],
                              [((p_hi[:, c, t], p_lo[:, c, t]),
                                (e_hi[:, c, i * BANK:(i + 1) * BANK], e_lo[:, c, i * BANK:(i + 1) * BANK]))
                               for c in range(PC)])
                split_product(pe, psum[n % 4][:, :],
                              [((hT_hi[:, c, t], hT_lo[:, c, t]), (g_hi[i][:, c, :], g_lo[i][:, c, :]))
                               for c in range(KC)]).then_inc(bank_full, 1)


def kernel(x, p, g_mix, w_in, q_norm, k_norm, sinks, w_out, g_ffn,
           peer_w_query, peer_sub_keys, peer_u, peer_v, g_ple, w_ple_gate, w_ple_proj):
    import numpy as np
    import concourse.bacc as bacc
    from concourse.bass_utils import run_bass_kernel_spmd

    def panels(w, chunks, n, width):
        return np.asarray(w).reshape(chunks, P, n, width).transpose(2, 1, 0, 3)

    def column(g):
        return np.asarray(g).reshape(KC, P).T

    heads = np.arange(RH)
    gamma = 1.0 - np.exp2(-5.0 - heads)
    idx = np.arange(P)
    rel = idx[None, :] - idx[:, None]
    decay = np.where(rel[:, None, :] >= 0, gamma[None, :, None] ** np.maximum(rel, 0)[:, None, :], 0.0) * HD ** -0.5
    wq = np.repeat(gamma[:, None] ** (idx + 1)[None, :], HD, axis=0).reshape(RH // 2, P, P).transpose(1, 0, 2)
    wk = gamma[None, :] ** (P - 1 - idx)[:, None] * HD ** -0.5
    chunk = np.repeat(gamma ** P, HD).reshape(RH // 2, P).T
    half = HD // 2
    freqs = (np.float32(10000.0) ** (-np.arange(half, dtype=np.float32) / np.float32(half))).astype(np.float32)
    ang = np.arange(SEQ, dtype=np.float32)[:, None] * freqs[None, :]
    cos, sin = (f(ang).reshape(TB, P, half).transpose(1, 0, 2) for f in (np.cos, np.sin))
    back = idx[:, None] + P - np.arange(2 * P)[None, :]
    mask = np.where((back >= 0) & (back < P), 0.0, -1.0e30)

    arrays = {
        "x": np.asarray(x)[0], "p_t": np.asarray(p)[0, 0].T.reshape(PLE // P, P, SEQ).transpose(1, 0, 2),
        "g_mix": column(g_mix), "w_in": panels(w_in, KC, IN_PANELS, IN_PW),
        "q_norm": np.tile(np.asarray(q_norm)[0], 2)[:, None], "k_norm": np.tile(np.asarray(k_norm)[0], 2)[:, None],
        "sinks": np.broadcast_to(np.asarray(sinks)[0], (P, QH)), "w_out": panels(w_out, KC, PANELS, PW),
        "g_ffn": column(g_ffn), "w_query": panels(peer_w_query, KC, 2 * PANELS, PW),
        "keys_t": np.asarray(peer_sub_keys)[0].transpose(2, 0, 1),
        "peer_u": np.asarray(peer_u)[0].reshape(KEYS, KEYS, KC, P).transpose(1, 3, 2, 0),
        "peer_v": np.asarray(peer_v)[0].reshape(KEYS, KEYS, D).transpose(1, 0, 2),
        "g_ple": column(g_ple), "w_gate": panels(w_ple_gate, KC, 2, BANK),
        "w_ple": np.asarray(w_ple_proj).reshape(PLE // P, P, D).transpose(1, 0, 2),
        "ident_c": np.eye(P, dtype=np.float32),
        "cos_c": cos, "sin_c": sin, "decay_c": decay[:, [0, 2, 4, 6, 1, 3, 5, 7]].astype(np.float32), "wq_c": wq.astype(np.float32),
        "wk_c": wk.astype(np.float32), "chunk_c": chunk.astype(np.float32), "mask_c": mask.astype(np.float32),
    }
    arrays = {n: np.ascontiguousarray(a) for n, a in arrays.items()}
    nc = bacc.Bacc("TRN2", target_bir_lowering=False, num_devices=1)
    args = {n: nc.dram_tensor(n, a.shape, mybir.dt.from_np(a.dtype), kind="ExternalInput").ap()
            for n, a in arrays.items()}
    out = nc.dram_tensor("out", (SEQ, D), F32, kind="ExternalOutput").ap()
    hybrid_layer(nc, out=out, **args)
    r = run_bass_kernel_spmd(nc, [arrays], core_ids=[0])
    return np.asarray(r.results[0]["out"]).reshape(1, SEQ, D)
```

```python
from contextlib import ExitStack

import concourse.bass as bass
from concourse import mybir

F32 = mybir.dt.float32
F32R = mybir.dt.float32r
F16 = mybir.dt.float16
U32 = mybir.dt.uint32
I32 = mybir.dt.int32
ALU = mybir.AluOpType
ACT = mybir.ActivationFunctionType
AX = mybir.AxisListType

P = 128
D = 1024
SEQ = 512
TB = SEQ // P
KC = D // P
HD = 64
RH = 8
QH = 8
KVH = 2
RW = RH * HD
IN_W = 4 * RW + QH * HD + 2 * KVH * HD
RQ, RK, RV, RG, SQ, SK, SV = 0, RW, 2 * RW, 3 * RW, 4 * RW, 4 * RW + QH * HD, 4 * RW + (QH + KVH) * HD
MIXED = RG
PANELS, PW = 4, D // 4
WIN_PANELS = (QH + 2 * KVH) * HD // PW
RET_PANELS = 4 * RW // PW
BANK = 512
PH = 8
KEYS = 128
TOPK = 16
HALVES = 2 * PH
PICKS = PH * TOPK
TILES = KEYS
GROUP = 4
PLE = 256
EPS = 1e-6
NEG = -3.0e38
FULL_A = 4
CANDS = FULL_A * TOPK + (TOPK - FULL_A) * FULL_A
GATE_SCALE = 4096.0
EARLY = TILES // 2
EARLY_PER_BLOCK = 10
EARLY_OF_CHUNK = (2, 1, 2, 1)
TCH = 32


class Chain:

    def __init__(self, eng, sem, settled=None):
        self.eng, self.sem, self.settled, self.n, self.off = eng, sem, settled, 0, 0

    def step(self, ins):
        ins.then_inc(self.sem, 1)
        self.n += 1

    def settle(self):
        self.eng.wait_ge(self.sem, self.off + self.n)
        if self.settled is not None:
            self.eng.sem_inc(self.settled, 1)


def split_product(pe, out, pairs, made=None):
    last = None
    for n, ((ah, al), (bh, bl)) in enumerate(pairs):
        if made is not None:
            pe.wait_ge(made[0], made[1] + n + 1)
        pe.matmul(out, ah, bh, start=(n == 0), stop=False)
        pe.matmul(out, ah, bl, start=False, stop=False)
        last = pe.matmul(out, al, bh, start=False, stop=(n == len(pairs) - 1))
    return last


class Transposed:
    HB = TB // 2

    def __init__(self, nc, ctx, sem, psum, tag, src, xn, gain, hT_hi, hT_lo, ident):
        self.psum, self.src, self.xn, self.gain = psum, src, xn, gain
        self.hT_hi, self.hT_lo, self.ident = hT_hi, hT_lo, ident
        self.sumsq, self.mean, self.inv, self.rstd = (
            ctx.enter_context(nc.sbuf_tensor(f"{tag}_{n}", [P, TB], F32)) for n in ("sumsq", "mean", "inv", "rstd"))
        self.sq_done, self.mean_done, self.inv_done, self.rstd_done, self.xn_done = (
            sem(f"{tag}_{n}") for n in ("sq_done", "mean_done", "inv_done", "rstd_done", "xn_done"))
        self.turned, self.hi_done, self.lo_done = (sem(f"{tag}_{n}") for n in ("turned", "hT_hi_done", "hT_lo_done"))

    def blocks(self, half):
        return range(half * self.HB, (half + 1) * self.HB)

    def columns(self, half):
        return slice(half * self.HB, (half + 1) * self.HB)

    def roots(self, act, half, landed=None):
        for tb in self.blocks(half):
            if landed:
                act.wait_ge(landed[tb], 16)
            act.activation(self.xn[:, tb, :], self.src[:, tb, :], ACT.Square,
                           accum_out=self.sumsq[:, tb:tb + 1]).then_inc(self.sq_done, 1)
        act.wait_ge(self.inv_done, half + 1)
        act.activation(self.rstd[:, self.columns(half)], self.inv[:, self.columns(half)], ACT.Sqrt)\
           .then_inc(self.rstd_done, 1)

    def means(self, dve, half):
        at = self.columns(half)
        dve.wait_ge(self.sq_done, (half + 1) * self.HB)
        dve.tensor_scalar(self.mean[:, at], self.sumsq[:, at], 1.0 / D, EPS, ALU.mult, ALU.add)\
           .then_inc(self.mean_done, 1)
        dve.wait_ge(self.mean_done, half + 1)
        dve.reciprocal(self.inv[:, at], self.mean[:, at]).then_inc(self.inv_done, 1)

    def scale(self, dve, half):
        dve.wait_ge(self.rstd_done, half + 1)
        for tb in self.blocks(half):
            dve.tensor_scalar(self.xn[:, tb, :], self.src[:, tb, :], self.rstd[:, tb:tb + 1], None,
                              ALU.mult).then_inc(self.xn_done, 1)

    def scalar(self, act):
        for kc in range(KC):
            act.wait_ge(self.turned, kc + 1)
            act.activation(self.hT_hi[:, kc, :], self.psum[kc][:, :], ACT.Copy,
                           scale=self.gain[:, kc:kc + 1]).then_inc(self.hi_done, 1)

    def vector(self, dve):
        for kc in range(KC):
            dve.wait_ge(self.hi_done, kc + 1)
            dve.scalar_tensor_tensor(out=self.hT_lo[:, kc, :], in0=self.psum[kc][:, :], scalar=self.gain[:, kc:kc + 1],
                                     in1=self.hT_hi[:, kc, :].bitcast(F32), op0=ALU.mult, op1=ALU.subtract)\
               .then_inc(self.lo_done, 1)

    def tensor(self, pe):
        for half in range(2):
            pe.wait_ge(self.xn_done, (half + 1) * self.HB)
            for kc in range(KC):
                for tb in self.blocks(half):
                    last = pe.transpose(self.psum[kc][:, tb * P:(tb + 1) * P], self.xn[:, tb, kc * P:(kc + 1) * P],
                                        self.ident[:, :])
                if half:
                    last.then_inc(self.turned, 1)


def project(nc, sem, psum, tag, panels, n_panels, width, chunks, evacuate, hT,
            transposed=False, then=None):
    with ExitStack() as ctx:
        hT_hi, hT_lo = hT.hT_hi, hT.hT_lo
        raw = [ctx.enter_context(nc.sbuf_tensor(f"{tag}_raw{i}", [P, chunks, width], F32)) for i in range(2)]
        w_hi = [ctx.enter_context(nc.sbuf_tensor(f"{tag}_whi{i}", [P, chunks, width], F32R)) for i in range(2)]
        w_lo = [ctx.enter_context(nc.sbuf_tensor(f"{tag}_wlo{i}", [P, chunks, width], F32R)) for i in range(2)]
        loaded = [sem(f"{tag}_loaded{i}") for i in range(2)]
        hi_done, lo_done = sem(f"{tag}_hi_done"), sem(f"{tag}_lo_done")
        bank_full, bank_free = sem(f"{tag}_bank_full"), sem(f"{tag}_bank_free")
        units = width // P if transposed else TB
        n_pairs = n_panels // 2
        block = ctx.enter_context(nc.Block())

        @block.sync
        def _(sp):
            sp.sem_inc(lo_done, 2)
            with sp.Fori(0, n_pairs) as pair:
                for i in range(2):
                    sp.wait_ge(lo_done, pair * 2 + i + 1)
                    sp.dma_start(raw[i][:, :, :], panels[bass.ds(pair * 2 + i, 1), :, :, :]
                                 .rearrange("o p c n -> (o p) c n")).then_inc(loaded[i], 16)
            if then:
                then(sp)

        @block.scalar
        def _(act):
            def split(pair, i):
                act.wait_ge(loaded[i], pair * 16 + 16)
                act.activation(w_hi[i][:, :, :], raw[i][:, :, :], ACT.Copy).then_inc(hi_done, 1)

            hT.roots(act, 1)
            split(0, 0)
            hT.scalar(act)
            split(0, 1)
            with act.Fori(0, n_pairs - 1) as pair:
                for i in range(2):
                    act.wait_ge(bank_full, pair * 2 * units + i * units + units)
                    split(pair + 1, i)

        @block.vector
        def _(dve):
            def split(pair, i):
                dve.wait_ge(hi_done, pair * 2 + i + 1)
                dve.tensor_tensor(w_lo[i][:, :, :], raw[i][:, :, :], w_hi[i][:, :, :].bitcast(F32),
                                  ALU.subtract).then_inc(lo_done, 1)

            dve.sem_inc(bank_free, 2 * units)
            def evacuate_panel(pair, i):
                for u in range(units):
                    dve.wait_ge(bank_full, pair * 2 * units + i * units + u + 1)
                    evacuate(dve, pair, i, u, psum[i * units + u][:, 0:SEQ if transposed else width])\
                        .then_inc(bank_free, 1)

            hT.means(dve, 1)
            hT.scale(dve, 1)
            split(0, 0)
            hT.vector(dve)
            split(0, 1)
            with dve.Fori(0, n_pairs - 1) as pair:
                for i in range(2):
                    evacuate_panel(pair, i)
                    split(pair + 1, i)
            for i in range(2):
                evacuate_panel(n_pairs - 1, i)

        @block.tensor
        def _(pe):
            hT.tensor(pe)
            with pe.Fori(0, n_pairs) as pair:
                for i in range(2):
                    pe.wait_ge(lo_done, pair * 2 + i + 3)
                    for u in range(units):
                        pe.wait_ge(bank_free, pair * 2 * units + i * units + u + 1)
                        if transposed:
                            pairs = [((w_hi[i][:, c, u * P:(u + 1) * P], w_lo[i][:, c, u * P:(u + 1) * P]),
                                      (hT_hi[:, c, :], hT_lo[:, c, :])) for c in range(chunks)]
                            out = psum[i * units + u][:, :]
                        else:
                            pairs = [((hT_hi[:, c, u * P:(u + 1) * P], hT_lo[:, c, u * P:(u + 1) * P]),
                                      (w_hi[i][:, c, :], w_lo[i][:, c, :])) for c in range(chunks)]
                            out = psum[i * units + u][:, 0:width]
                        last = split_product(pe, out, pairs, made=(hT.lo_done, 0) if (i, u) == (0, 0) else None)
                        last.then_inc(bank_full, 1)


class FirstProducts:

    def __init__(self, nc, ctx, sem, psum, peer_u, hT_hi, hT_lo):
        def sb(name, dt):
            return [ctx.enter_context(nc.sbuf_tensor(f"{name}{i}", [P, KC, P], dt)) for i in range(2)]

        self.peer_u, self.hT_hi, self.hT_lo = peer_u, hT_hi, hT_lo
        self.raw, self.hi, self.lo = sb("u_raw", F32), sb("u_hi", F32R), sb("u_lo", F32R)
        self.out = [ctx.enter_context(nc.sbuf_tensor(f"gelu{i}", [P, SEQ], F32)) for i in range(2)]
        self.bank = psum[6:8]
        self.landed = [sem(f"u_in{i}") for i in range(2)]
        self.hi_done, self.lo_done, self.full, self.gelu_done = sem("u_hi_done"), sem("u_lo_done"), sem("a_full"), sem("gelu_done")

    @staticmethod
    def number(tile):
        m, K, c = tile
        return m * K + c if not isinstance(m, int) or m else c

    @staticmethod
    def of_buffer(tile):
        m, K, c = tile
        return m * (K // 2) + c // 2 if not isinstance(m, int) or m else c // 2

    def load(self, sp, tile, wait=True):
        b = tile[2] % 2
        if wait:
            sp.wait_ge(self.lo_done, self.number(tile) + 1)
        sp.dma_start(self.raw[b][:, :, :], self.peer_u[bass.ds(self.number(tile), 1), :, :, :]
                     .rearrange("o p c e -> (o p) c e")).then_inc(self.landed[b], 16)

    def split_hi(self, act, tile):
        b = tile[2] % 2
        act.wait_ge(self.landed[b], self.of_buffer(tile) * 16 + 16)
        act.wait_ge(self.full, self.number(tile) + 1)
        act.activation(self.hi[b][:, :, :], self.raw[b][:, :, :], ACT.Copy).then_inc(self.hi_done, 1)

    def split_lo(self, dve, tile):
        b = tile[2] % 2
        dve.wait_ge(self.hi_done, self.number(tile) + 1)
        dve.tensor_tensor(self.lo[b][:, :, :], self.raw[b][:, :, :], self.hi[b][:, :, :].bitcast(F32),
                          ALU.subtract).then_inc(self.lo_done, 1)

    def product(self, pe, tile):
        b = tile[2] % 2
        pe.wait_ge(self.lo_done, self.number(tile) + 3)
        pe.wait_ge(self.gelu_done, self.number(tile) + 1)
        split_product(pe, self.bank[b][:, :], [((self.hi[b][:, k, :], self.lo[b][:, k, :]),
                                                (self.hT_hi[:, k, :], self.hT_lo[:, k, :])) for k in range(KC)])\
            .then_inc(self.full, 1)

    def gelu(self, act, tile):
        act.wait_ge(self.full, self.number(tile) + 3)
        act.activation(self.out[tile[2] % 2][:, :], self.bank[tile[2] % 2][:, :], ACT.Gelu).then_inc(self.gelu_done, 1)


class EarlyTiles:

    def __init__(self, first, dram, spilled):
        self.first, self.dram, self.spilled = first, dram, spilled

    @staticmethod
    def later(tile, n):
        return tile[0], tile[1], tile[2] + n

    def sync(self, sp, tile):
        f, b = self.first, tile[2] % 2
        f.load(sp, self.later(tile, 3))
        sp.wait_ge(f.gelu_done, f.number(tile) + 3)
        sp.dma_start(self.dram[bass.ds(f.number(tile), 1), :, :].rearrange("o p t -> (o p) t"), f.out[b][:, :])\
            .then_inc(self.spilled[b], 16)

    def scalar(self, act, tile):
        f, b = self.first, tile[2] % 2
        f.split_hi(act, self.later(tile, 1))
        act.wait_ge(self.spilled[b], f.of_buffer(tile) * 16 + 16)
        f.gelu(act, tile)

    def vector(self, dve, tile):
        self.first.split_lo(dve, self.later(tile, 1))

    def tensor(self, pe, tile):
        self.first.product(pe, tile)

    def wait_stored(self, eng, b):
        eng.wait_ge(self.spilled[b], EARLY // 2 * 16 + 16)


def hybrid_layer(nc, x, p_t, g_mix, w_in, q_norm, k_norm, sinks, w_out, g_ffn, w_query, keys_t, peer_u, peer_v,
                 g_ple, w_gate, w_ple, ident_c, cos_c, sin_c, decay_c, wq_c, wk_c, chunk_c, mask_c, out):
    gates_dram = nc.dram_tensor("gates", [SEQ // TCH, P, TILES, TCH], F32).ap()
    gelu_dram = nc.dram_tensor("early_gelu", [EARLY, P, SEQ], F32).ap()
    with ExitStack() as ctx:
        def sb(name, shape, dt=F32):
            return ctx.enter_context(nc.sbuf_tensor(name, shape, dt))

        def sem(name):
            return ctx.enter_context(nc.semaphore(name))

        psum = [ctx.enter_context(nc.psum_tensor(f"bank{i}", [P, BANK], F32)) for i in range(8)]
        res = sb("res", [P, TB, D])
        hT_hi = sb("hT_hi", [P, KC, SEQ], F32R)
        hT_lo = sb("hT_lo", [P, KC, SEQ], F32R)
        ident = sb("ident", [P, P])
        gains = sb("gains", [P, 3, KC])
        xn = sb("xn", [P, TB, D])
        mix_hT, ffn_hT, ple_hT = (Transposed(nc, ctx, sem, psum, tag, res, xn, gains[:, i, :], hT_hi, hT_lo, ident)
                                  for i, tag in enumerate(("mix", "ffn", "ple")))

        x_landed, const_landed = [sem(f"x_landed{tb}") for tb in range(TB)], sem("const_landed")
        x_blocks = x.rearrange("(t p) d -> p t d", p=P)
        first_loads = [(res[:, tb, :], x_blocks[:, tb, :], x_landed[tb]) for tb in range(TB)]
        first_loads += [(dst, src, const_landed) for dst, src in (
            (ident[:, :], ident_c), (gains[:, 0, :], g_mix), (gains[:, 1, :], g_ffn), (gains[:, 2, :], g_ple))]

        with ExitStack() as mixer:
            proj = mixer.enter_context(nc.sbuf_tensor("proj", [P, TB, IN_W], F32))
            with ExitStack() as heads:
                decay, wq, wk, chunk = (heads.enter_context(nc.sbuf_tensor(n, shape, F32)) for n, shape in (
                    ("decay", [P, RH, P]), ("wq", [P, RH // 2, P]), ("wk", [P, RH]), ("chunk", [P, RH // 2])))
                window_beside_projection(nc, sem, psum, proj, mix_hT, x_landed, first_loads,
                                         (const_landed, 4 * 16), w_in, q_norm, k_norm, sinks, cos_c, sin_c, mask_c,
                                         [(decay[:, :, :], decay_c), (wq[:, :, :], wq_c), (wk[:, :], wk_c),
                                          (chunk[:, :], chunk_c)])
                retention_and_output(nc, sem, psum, res, proj, ffn_hT, w_out, decay, wq, wk, chunk)

        with ExitStack() as peer:
            first = FirstProducts(nc, peer, sem, psum, peer_u, hT_hi, hT_lo)
            spilled, stored = ([sem(f"{n}{i}") for i in range(2)] for n in ("spilled", "stored"))
            early = EarlyTiles(first, gelu_dram, spilled)
            with ExitStack() as routing:
                picks = [routing.enter_context(nc.sbuf_tensor(n, [P, TB, PICKS], F32))
                         for n in ("pick_i1", "pick_i2", "pick_gate")]
                with ExitStack() as route:
                    qT = route.enter_context(nc.sbuf_tensor("qT", [P, HALVES, SEQ], F32))

                    def keep_q(dve, pair, i, u, bank):
                        return dve.tensor_copy(qT[:, bass.ds((pair * 2 + i) * (PW // P) + u, 1), :]
                                               .rearrange("p o t -> p (o t)"), bank)

                    def load_first_tiles(sp):
                        for tile in range(2):
                            first.load(sp, (0, 2, tile), wait=False)

                    project(nc, sem, psum, "wqry", w_query, 2 * PANELS, PW, KC, keep_q,
                            ffn_hT, transposed=True, then=load_first_tiles)
                    choose_experts(nc, sem, psum, qT, keys_t, picks, early)
                spread_gates(nc, sem, psum, picks, ident, gates_dram, stored, early)
            evaluate_experts(nc, sem, psum, res, xn, first, early, stored, peer_v, gates_dram, ple_hT)

        add_embedding(nc, sem, psum, res, ple_hT, p_t, w_gate, w_ple, out)


def window_beside_projection(nc, sem, psum, proj, hT, x_landed, first_loads, first_landed, w_in,
                             q_norm, k_norm, sinks, cos_c, sin_c, mask_c, loads):
    SCALE = float(HD) ** -0.5
    NH = QH + KVH
    HALF = HD // 2
    PAIRS = QH // 2
    N_PANELS = WIN_PANELS + RET_PANELS
    SLOTS = N_PANELS * TB
    NORM_AT = WIN_PANELS * TB
    JOBS = PAIRS + KVH
    TURN_AT, WINDOW_AT, STEP = NORM_AT + 4, NORM_AT + 7, 5
    ROTATE_AT = SLOTS - TB * TB
    assert ROTATE_AT >= (WIN_PANELS + 2 * RW // PW) * TB
    ALL_SLOTS = WINDOW_AT + STEP * (TB + 1)
    blocks_of = [1] + [2] * (TB - 1)
    turns_before = [2 * sum(blocks_of[:n]) for n in range(TB + 1)]
    with ExitStack() as ctx:
        def sb(name, shape, dt=F32):
            return ctx.enter_context(nc.sbuf_tensor(name, shape, dt))

        hT_hi, hT_lo, ident = hT.hT_hi, hT.hT_lo, hT.ident
        raw = [sb(f"in_raw{i}", [P, KC, PW]) for i in range(2)]
        w_hi = [sb(f"in_whi{i}", [P, KC, PW], F32R) for i in range(2)]
        w_lo = [sb(f"in_wlo{i}", [P, KC, PW], F32R) for i in range(2)]
        sqT = sb("sqT", [P, PAIRS, SEQ])
        skT = sb("skT", [P, KVH, SEQ])
        skn = sb("skn", [P, TB, KVH, 2, HD])
        scratch = sb("scratch", [P, TB * NH * HD])
        masked, prob = (hT.xn[:, 2 * i:2 * i + 2, :].rearrange("p t (h k) -> p (t h) k", k=2 * P) for i in range(2))
        probT = sb("probT", [P, QH, 2, P])
        cos, sin, mask, sink = sb("cos", [P, TB, HALF]), sb("sin", [P, TB, HALF]), sb("mask", [P, 2 * P]), sb("sink", [P, QH])
        qn, kn = sb("qn", [P, 1]), sb("kn", [P, 1])
        norm_stats = sb("norm_stats", [P, 4, TB * NH])
        st = sb("window_stats", [P, 8, QH])
        top, m, negm, sink_gap, sink_e, row_sum, den, rden = (st[:, i, :] for i in range(8))
        landed = [sem(f"in_landed{i}") for i in range(2)]
        hi_done, lo_done, bank_full, bank_free = sem("in_hi"), sem("in_lo"), sem("in_full"), sem("in_free")
        consts_landed, steps, inv_ready, rstd_ready = (sem(n) for n in ("win_consts", "win_steps", "qk_inv", "qk_rstd"))
        norm_ready, job_full, job_copied = sem("norm_ready"), sem("job_full"), sem("job_copied")
        s_full, s_read, negm_ready, exp_done = sem("s_full"), sem("s_read"), sem("negm_ready"), sem("exp_done")
        pt_full, pt_copied, o_full, o_done = sem("pt_full"), sem("pt_copied"), sem("o_full"), sem("o_done")
        all_loads = [(qn[:, :], q_norm), (kn[:, :], k_norm), (mask[:, :], mask_c), (sink[:, :], sinks),
                     (cos[:, :, :], cos_c), (sin[:, :, :], sin_c)] + loads
        block = ctx.enter_context(nc.Block())

        def step_of(slot):
            return divmod(slot - WINDOW_AT, STEP) if slot >= WINDOW_AT else (-1, 0)

        def panel_bank(panel, tb):
            return psum[panel % 2 * 2 + tb // 2]

        def column(panel):
            return SQ + panel * PW if panel < WIN_PANELS else (panel - WIN_PANELS) * PW

        def jobs_of(slot):
            return [j for j in (2 * (slot - TURN_AT), 2 * (slot - TURN_AT) + 1) if 0 <= j < JOBS]

        @block.sync
        def _(sp):
            for dst, src, landing in first_loads:
                sp.dma_start(dst, src).then_inc(landing, 16)
            for panel in range(N_PANELS):
                if panel >= 2:
                    sp.wait_ge(lo_done, panel - 1)
                sp.dma_start(raw[panel % 2][:, :, :], w_in[panel]).then_inc(landed[panel % 2], 16)
                if panel == 1:
                    for dst, src in all_loads:
                        sp.dma_start(dst, src).then_inc(consts_landed, 16)

        @block.tensor
        def _(pe):
            def project_unit(panel, tb):
                if tb == 0:
                    pe.wait_ge(lo_done, panel + 1)
                if panel >= 2 and tb % 2 == 0:
                    pe.wait_ge(bank_free, 2 * (panel - 2) + tb // 2 + 1)
                t, i = slice(tb * P, (tb + 1) * P), panel % 2
                last = split_product(pe, panel_bank(panel, tb)[:, tb % 2 * PW:(tb % 2 + 1) * PW],
                                     [((hT_hi[:, c, t], hT_lo[:, c, t]), (w_hi[i][:, c, :], w_lo[i][:, c, :]))
                                      for c in range(KC)], made=(hT.lo_done, 0) if (panel, tb) == (0, 0) else None)
                if tb % 2:
                    last.then_inc(bank_full, 1)

            def transpose_heads(j):
                if j == 0:
                    pe.wait_ge(norm_ready, 1)
                if j >= 2:
                    pe.wait_ge(job_copied, j - 1)
                for tb in range(TB):
                    source = (skn[:, tb, j, :, :].rearrange("p w d -> p (w d)") if j < KVH
                              else proj[:, tb, SQ + (j - KVH) * P:SQ + (j - KVH + 1) * P])
                    last = pe.transpose(psum[6 + j % 2][:, tb * P:(tb + 1) * P], source, ident[:, :])
                last.then_inc(job_full, 1)

            def scores(n, b):
                nb = blocks_of[n]
                if n == 0 and b == 0:
                    pe.wait_ge(job_copied, JOBS)
                if 4 * n + b >= 2:
                    pe.wait_ge(s_read, 4 * n + b - 1)
                for i in range(2):
                    h = b // 2 * 4 + b % 2 + 2 * i
                    half = slice((h % 2) * HD, (h % 2 + 1) * HD)
                    last = pe.matmul(psum[4 + b % 2][:, i * 256:i * 256 + nb * P], sqT[half, h // 2, n * P:(n + 1) * P],
                                     skT[half, h // (QH // KVH), (n + 1 - nb) * P:(n + 1) * P], start=True, stop=True)
                last.then_inc(s_full, 1)

            def transpose_weights(n, q):
                nb, before = blocks_of[n], turns_before[n] + q
                if before:
                    pe.wait_ge(pt_copied, before)
                for k in range(4):
                    h, kb = (4 * q + k) // nb, (4 * q + k) % nb
                    pe.wait_ge(exp_done, QH * n + h + 1)
                    last = pe.transpose(psum[6][:, k * P:(k + 1) * P], prob[:, h, kb * P:(kb + 1) * P], ident[:, :])
                last.then_inc(pt_full, 1)

            def outputs(n):
                nb = blocks_of[n]
                pe.wait_ge(pt_copied, turns_before[n + 1])
                if n:
                    pe.wait_ge(o_done, n)
                for h in range(QH):
                    for kb in range(nb):
                        v = SV + (h // (QH // KVH)) * HD
                        last = pe.matmul(psum[7][:, h * HD:(h + 1) * HD], probT[:, h, kb, :],
                                         proj[:, n + 1 - nb + kb, v:v + HD], start=(kb == 0), stop=(kb == nb - 1))
                last.then_inc(o_full, 1)

            pe.wait_ge(*first_landed)
            hT.tensor(pe)
            for slot in range(ALL_SLOTS):
                if slot < SLOTS:
                    project_unit(slot // TB, slot % TB)
                for j in jobs_of(slot):
                    transpose_heads(j)
                g, k = step_of(slot)
                if 0 <= g < TB and k < 4:
                    scores(g, k)
                if g >= 1 and k < 2 * blocks_of[g - 1]:
                    transpose_weights(g - 1, k)
                if g >= 1 and k == 4:
                    outputs(g - 1)

        @block.scalar
        def _(act):
            def split_hi(panel):
                i = panel % 2
                act.wait_ge(landed[i], panel // 2 * 16 + 16)
                if panel >= 2:
                    act.wait_ge(bank_full, 2 * (panel - 2) + 2)
                act.activation(w_hi[i][:, :, :], raw[i][:, :, :], ACT.Copy).then_inc(hi_done, 1)

            def copy_heads(j):
                act.wait_ge(job_full, j + 1)
                dst, gain = (skT[:, j, :], kn) if j < KVH else (sqT[:, j - KVH, :], qn)
                act.activation(dst, psum[6 + j % 2][:, :], ACT.Copy, scale=gain[:, 0:1]).then_inc(job_copied, 1)

            def exponentials(n):
                nb = blocks_of[n]
                act.wait_ge(negm_ready, n + 1)
                act.activation(sink_e, sink_gap, ACT.Exp)
                for h in range(QH):
                    act.activation(prob[:, h, 0:nb * P], masked[:, h, 0:nb * P], ACT.Exp, bias=negm[:, h:h + 1],
                                   scale=SCALE, accum_out=row_sum[:, h:h + 1]).then_inc(exp_done, 1)

            def copy_weights(n, q):
                nb = blocks_of[n]
                act.wait_ge(pt_full, turns_before[n] + q + 1)
                if n and q == 0:
                    act.wait_ge(o_full, n)
                heads = 4 // nb
                act.activation(probT[:, q * heads:(q + 1) * heads, 0:nb, :],
                               psum[6][:, :].rearrange("p (h k i) -> p h k i", h=heads, k=nb),
                               ACT.Copy).then_inc(pt_copied, 1)

            act.preload_act_table(ACT.Sqrt)
            for half in range(2):
                hT.roots(act, half, x_landed)
            split_hi(0)
            hT.scalar(act)
            split_hi(1)
            act.wait_ge(consts_landed, 16 * len(all_loads))
            for slot in range(ALL_SLOTS):
                if slot == NORM_AT:
                    act.wait_ge(inv_ready, 1)
                    act.activation(norm_stats[:, 3, :], norm_stats[:, 2, :], ACT.Sqrt).then_inc(rstd_ready, 1)
                for j in jobs_of(slot):
                    copy_heads(j)
                g, k = step_of(slot)
                if g >= 1 and k < 2 * blocks_of[g - 1]:
                    copy_weights(g - 1, k)
                if 0 <= g < TB and k == 4:
                    exponentials(g)
                if slot % TB == TB - 1 and slot // TB + 2 < N_PANELS:
                    split_hi(slot // TB + 2)

        @block.vector
        def _(dve):
            chain = Chain(dve, steps)
            sqk = proj[:, :, SQ:SV].rearrange("p t (h d) -> p t h d", d=HD)
            ssq, mean, inv, rstd = (norm_stats[:, i, :].rearrange("p (t h) -> p t h", t=TB) for i in range(4))

            def split_lo(panel):
                i = panel % 2
                dve.wait_ge(hi_done, panel + 1)
                dve.tensor_tensor(w_lo[i][:, :, :], raw[i][:, :, :], w_hi[i][:, :, :].bitcast(F32),
                                  ALU.subtract).then_inc(lo_done, 1)

            def keep(panel, half):
                dve.wait_ge(bank_full, 2 * panel + half + 1)
                dve.tensor_copy(proj[:, 2 * half:2 * half + 2, column(panel):column(panel) + PW],
                                panel_bank(panel, 2 * half)[:, :].rearrange("p (t c) -> p t c", t=2))\
                   .then_inc(bank_free, 1)

            def norm_statistics():
                sq = scratch[:, :].rearrange("p (t h d) -> p t h d", t=TB, h=NH)
                dve.wait_ge(bank_free, 2 * WIN_PANELS)
                chain.step(dve.tensor_tensor(sq, sqk, sqk, ALU.mult))
                chain.settle()
                chain.step(dve.tensor_reduce(ssq, sq, AX.X, ALU.add))
                chain.settle()
                chain.step(dve.tensor_scalar(mean, ssq, 1.0 / HD, EPS, ALU.mult, ALU.add))
                chain.settle()
                dve.reciprocal(inv, mean).then_inc(inv_ready, 1)

            def normalise():
                dve.wait_ge(rstd_ready, 1)
                for twice in range(2):
                    chain.step(dve.tensor_tensor(skn[:, :, :, twice, :], sqk[:, :, QH:NH, :],
                                                 rstd[:, :, QH:NH].unsqueeze(3).broadcast_to([P, TB, KVH, HD]), ALU.mult))
                for tb in range(TB):
                    q_at = sqk[:, tb, 0:QH, :]
                    chain.step(dve.tensor_tensor(q_at, q_at, rstd[:, tb, 0:QH].unsqueeze(2).broadcast_to([P, QH, HD]),
                                                 ALU.mult))
                chain.settle()
                dve.sem_inc(norm_ready, 1)

            def mask_scores(n, b):
                nb, h0 = blocks_of[n], b // 2 * 4 + b % 2
                dve.wait_ge(s_full, 4 * n + b + 1)
                if n and b == 0:
                    dve.wait_ge(exp_done, QH * n)
                dve.tensor_tensor(masked[:, h0:h0 + 3:2, 0:nb * P],
                                  psum[4 + b % 2][:, :].rearrange("p (h k) -> p h k", h=2)[:, :, 0:nb * P],
                                  mask[:, 2 * P - nb * P:2 * P].unsqueeze(1).broadcast_to([P, 2, nb * P]),
                                  ALU.add).then_inc(s_read, 1)

            def maxima(n):
                dve.wait_ge(s_read, 4 * n + 4)
                chain.step(dve.tensor_reduce(top, masked[:, :, 0:blocks_of[n] * P], AX.X, ALU.max))
                chain.settle()
                chain.step(dve.scalar_tensor_tensor(out=m, in0=top, scalar=SCALE, in1=sink[:, :],
                                                    op0=ALU.mult, op1=ALU.max))
                chain.settle()
                chain.step(dve.tensor_scalar(negm, m, -1.0, None, ALU.mult))
                chain.step(dve.tensor_tensor(sink_gap, sink[:, :], m, ALU.subtract))
                chain.settle()
                dve.sem_inc(negm_ready, 1)

            def denominators(n):
                dve.wait_ge(exp_done, QH * (n + 1))
                chain.step(dve.tensor_tensor(den, row_sum, sink_e, ALU.add))
                chain.settle()
                chain.step(dve.reciprocal(rden, den))
                chain.settle()

            def normalise_outputs(n):
                dve.wait_ge(o_full, n + 1)
                dve.tensor_tensor(proj[:, n, SQ:SQ + QH * HD].rearrange("p (h d) -> p h d", d=HD),
                                  psum[7][:, :].rearrange("p (h d) -> p h d", d=HD),
                                  rden.unsqueeze(2).broadcast_to([P, QH, HD]), ALU.mult).then_inc(o_done, 1)

            def rotate(tb):
                qk = proj[:, tb, RQ:RV].rearrange("p (h d) -> p h d", d=HD)
                x1, x2 = qk[:, :, 0:HALF], qk[:, :, HALF:HD]
                c = cos[:, tb, :].unsqueeze(1).broadcast_to([P, 2 * RH, HALF])
                s = sin[:, tb, :].unsqueeze(1).broadcast_to([P, 2 * RH, HALF])
                size = 2 * RH * HALF
                products = [scratch[:, i * size:(i + 1) * size].rearrange("p (h d) -> p h d", d=HALF) for i in range(4)]
                chain.settle()
                dve.wait_ge(bank_free, 2 * (WIN_PANELS + 2 * RW // PW))
                for dst, x, w in zip(products, (x1, x2, x1, x2), (c, s, s, c)):
                    chain.step(dve.tensor_tensor(dst, x, w, ALU.mult))
                chain.settle()
                chain.step(dve.tensor_tensor(x1, products[0], products[1], ALU.subtract))
                chain.step(dve.tensor_tensor(x2, products[2], products[3], ALU.add))

            for half in range(2):
                hT.means(dve, half)
                hT.scale(dve, half)
            split_lo(0)
            hT.vector(dve)
            split_lo(1)
            dve.wait_ge(consts_landed, 16 * len(all_loads))
            for slot in range(ALL_SLOTS):
                if slot == NORM_AT:
                    norm_statistics()
                    normalise()
                if slot < SLOTS and slot % 2:
                    keep(slot // TB, slot % TB // 2)
                if slot % TB == TB - 1 and slot // TB + 2 < N_PANELS:
                    split_lo(slot // TB + 2)
                g, k = step_of(slot)
                if 0 <= g < TB and k < 4:
                    mask_scores(g, k)
                if 0 <= g < TB and k == 3:
                    maxima(g)
                if g >= 1 and k == 1:
                    denominators(g - 1)
                if g >= 1 and k == 4:
                    normalise_outputs(g - 1)
                if slot >= ROTATE_AT and slot % TB == 0:
                    rotate((slot - ROTATE_AT) // TB)


def retention_and_output(nc, sem, psum, res, proj, next_hT, w_out, decay, wq, wk, chunk):
    hT_hi, hT_lo, ident = next_hT.hT_hi, next_hT.hT_lo, next_hT.ident
    HC = KC // 2
    HPANELS = 2 * PANELS
    RING = 4
    UNITS = 2 * HPANELS
    PAIRS = RH // 2
    HH = RH // 2
    with ExitStack() as ctx:
        def sb(name, shape, dt=F32):
            return ctx.enter_context(nc.sbuf_tensor(name, shape, dt))

        rqT, rkT, rqwT = (sb(n, [P, PAIRS, SEQ]) for n in ("rqT", "rkT", "rqwT"))
        kw = sb("kw", [P, TB, RW])
        attn = sb("attn", [P, RH, P])
        state = sb("state", [P, PAIRS, 2, HD])
        ret = sb("ret", [P, TB, RH, HD])
        sq = sb("ret_sq", [P, RH, HD])
        stats = sb("ret_stats", [P, TB, 6, RH])
        raw = [sb(f"out_raw{i}", [P, HC, PW]) for i in range(2)]
        w_hi = [sb(f"out_whi{i}", [P, HC, PW], F32R) for i in range(RING)]
        w_lo = [sb(f"out_wlo{i}", [P, HC, PW], F32R) for i in range(RING)]
        landed = [sem(f"out_landed{i}") for i in range(2)]
        hi_done, lo_done, unit_full, unit_added = sem("out_hi"), sem("out_lo"), sem("unit_full"), sem("unit_added")
        finished = sem("ret_finished")
        mixed_turned, mixed_hi, mixed_lo = sem("mixed_turned"), sem("mixed_hi"), sem("mixed_lo")
        turn_full, turn_copied, weighted = sem("turn_full"), sem("turn_copied"), sem("q_weighted")
        score_full, attn_done, out_full, kv_full = sem("score_full"), sem("attn_done"), sem("out_full"), sem("kv_full")
        state_done, out_copied, steps, kw_done = sem("state_done"), sem("out_copied"), sem("ret_steps"), sem("kw_done")
        silu_done, inv_done, root_done = sem("silu_done"), sem("ret_inv"), sem("ret_root")
        block = ctx.enter_context(nc.Block())

        def half(h):
            return slice((h % 2) * HD, (h % 2 + 1) * HD)

        def tokens(n):
            return slice(n * P, (n + 1) * P)

        mixed_chunks = list(range(HC, KC)) + list(range(HC))
        mixed_banks = [3, 5, 2, 4, 0, 1, 2, 6]

        def unit_bank(u):
            return psum[3 + 2 * (u % 2)]

        def parts_of(u):
            if u < 2 * PANELS:
                return u // 2, u % 2
            return PANELS + (u - 2 * PANELS) % PANELS, (u - 2 * PANELS) // PANELS

        @block.sync
        def _(sp):
            for q in range(HPANELS):
                if q >= 2:
                    sp.wait_ge(lo_done, q - 1)
                sp.dma_start(raw[q % 2][:, :, :], w_out[q]).then_inc(landed[q % 2], 16)

        @block.tensor
        def _(pe):
            def turn_mixed(j, blocks):
                for tb in blocks:
                    at = MIXED + mixed_chunks[j] * P
                    last = pe.transpose(psum[mixed_banks[j]][:, tb * P:(tb + 1) * P], proj[:, tb, at:at + P],
                                        ident[:, :])
                if TB - 1 in blocks:
                    last.then_inc(mixed_turned, 1)

            def output_unit(u):
                q, pair = parts_of(u)
                pe.wait_ge(lo_done, q + 1)
                if u >= 2:
                    pe.wait_ge(unit_added, u - 1)
                c0 = mixed_chunks[q // PANELS * HC]
                for t in range(2):
                    rows = tokens(2 * pair + t)
                    last = split_product(pe, unit_bank(u)[:, t * PW:(t + 1) * PW],
                                         [((hT_hi[:, c0 + c, rows], hT_lo[:, c0 + c, rows]),
                                           (w_hi[q % RING][:, c, :], w_lo[q % RING][:, c, :])) for c in range(HC)],
                                         made=(mixed_lo, HC) if (u, t) == (2 * PANELS, 0) else None)
                last.then_inc(unit_full, 1)

            def turn(n):
                for part, at in enumerate((RQ, RK)):
                    if n:
                        pe.wait_ge(turn_copied, 2 * (n - 1) + part + 1)
                    for pair in range(PAIRS):
                        last = pe.transpose(psum[6 + part][:, pair * P:(pair + 1) * P],
                                            proj[:, n, at + pair * P:at + (pair + 1) * P], ident[:, :])
                    last.then_inc(turn_full, 1)

            turn(0)
            for j in range(HC):
                turn_mixed(j, range(TB))
            for n in range(TB):
                t = tokens(n)
                if n + 1 < TB:
                    turn(n + 1)
                pe.wait_ge(turn_copied, 2 * n + 2)
                for b in range(2):
                    if n:
                        pe.wait_ge(attn_done, 2 * (n - 1) + b + 1)
                    for pair in range(PAIRS):
                        last = pe.matmul(psum[b][:, pair * P:(pair + 1) * P], rkT[half(b), pair, t],
                                         rqT[half(b), pair, t], start=True, stop=True)
                    last.then_inc(score_full, 1)
                if n == 0:
                    pe.wait_ge(mixed_lo, HC)
                output_unit(2 * n)
                if n < TB - 1:
                    pe.wait_ge(kw_done, n + 1)
                    if n:
                        pe.wait_ge(state_done, n)
                    for pair in range(PAIRS):
                        last = pe.matmul(psum[2][:, pair * P:(pair + 1) * P], kw[:, n, pair * P:(pair + 1) * P],
                                         proj[:, n, RV + pair * P:RV + (pair + 1) * P], start=True, stop=True)
                    last.then_inc(kv_full, 1)
                    output_unit(2 * n + 1)
                if n:
                    pe.wait_ge(out_copied, n)
                pe.wait_ge(attn_done, 2 * n + 2)
                if n:
                    pe.wait_ge(state_done, n)
                    pe.wait_ge(weighted, n)
                for h in range(RH):
                    o = psum[4][:, h * HD:(h + 1) * HD]
                    last = pe.matmul(o, attn[:, h % 2 * PAIRS + h // 2, :], proj[:, n, RV + h * HD:RV + (h + 1) * HD],
                                     start=True, stop=(n == 0))
                    if n:
                        last = pe.matmul(o, rqwT[:, h // 2, t], state[:, h // 2, h % 2, :],
                                         start=False, stop=True)
                last.then_inc(out_full, 1)
            output_unit(2 * TB - 1)
            pe.wait_ge(finished, TB - 1)
            for j in range(HC, KC):
                turn_mixed(j, range(TB - 1))
            pe.wait_ge(finished, TB)
            for j in range(HC, KC):
                turn_mixed(j, (TB - 1,))
            for u in range(2 * PANELS, UNITS):
                output_unit(u)

        @block.vector
        def _(dve):
            chain = Chain(dve, steps)

            def weigh_keys(n):
                dve.tensor_tensor(kw[:, n, :].rearrange("p (h d) -> p h d", d=HD),
                                  proj[:, n, RK:RV].rearrange("p (h d) -> p h d", d=HD),
                                  wk[:, :].unsqueeze(2).broadcast_to([P, RH, HD]), ALU.mult).then_inc(kw_done, 1)

            def weigh_queries(n):
                dve.wait_ge(turn_copied, 2 * n + 1)
                dve.tensor_tensor(rqwT[:, :, tokens(n)], rqT[:, :, tokens(n)], wq[:, :, :], ALU.mult)\
                   .then_inc(weighted, 1)

            def decay_scores(n, b):
                dve.wait_ge(score_full, 2 * n + b + 1)
                if n:
                    dve.wait_ge(out_full, n)
                dve.tensor_tensor(attn[:, b * HH:(b + 1) * HH, :].rearrange("p h i -> p (h i)"), psum[b][:, :],
                                  decay[:, b * HH:(b + 1) * HH, :].rearrange("p h i -> p (h i)"),
                                  ALU.mult).then_inc(attn_done, 1)

            def update_state(n):
                dve.wait_ge(kv_full, n + 1)
                if n:
                    dve.wait_ge(out_full, n + 1)
                for par in range(2):
                    rows = slice(par * HD, (par + 1) * HD)
                    kv = psum[2][rows, :].rearrange("p (a c) -> p a c", a=PAIRS)[:, :, par * HD:(par + 1) * HD]
                    if n:
                        for pair in range(PAIRS):
                            chain.step(dve.scalar_tensor_tensor(
                                out=state[rows, pair, par, :], in0=state[rows, pair, par, :],
                                scalar=chunk[rows, pair:pair + 1], in1=kv[:, pair, :], op0=ALU.mult, op1=ALU.add))
                    else:
                        chain.step(dve.tensor_copy(state[rows, :, par, :], kv))
                chain.settle()
                dve.sem_inc(state_done, 1)

            def statistics(n):
                total, mean, ssq, var, inv, _ = (stats[:, n, i, :] for i in range(6))
                r = ret[:, n, :, :]
                dve.wait_ge(out_copied, n + 1)
                chain.step(dve.tensor_reduce(total, r, AX.X, ALU.add))
                chain.settle()
                chain.step(dve.tensor_scalar(mean, total, 1.0 / HD, None, ALU.mult))
                chain.settle()
                chain.step(dve.tensor_tensor(r, r, mean.unsqueeze(2).broadcast_to([P, RH, HD]), ALU.subtract))
                chain.settle()
                chain.step(dve.tensor_tensor(sq[:, :, :], r, r, ALU.mult))
                chain.settle()
                chain.step(dve.tensor_reduce(ssq, sq[:, :, :], AX.X, ALU.add))
                chain.settle()
                chain.step(dve.tensor_scalar(var, ssq, 1.0 / HD, EPS, ALU.mult, ALU.add))
                chain.settle()
                dve.reciprocal(inv, var).then_inc(inv_done, 1)

            def finish(n):
                r, root = ret[:, n, :, :], stats[:, n, 5, :]
                dve.wait_ge(root_done, n + 1)
                dve.wait_ge(silu_done, 1)
                chain.step(dve.tensor_tensor(r, r, root.unsqueeze(2).broadcast_to([P, RH, HD]), ALU.mult))
                chain.settle()
                dve.tensor_tensor(proj[:, n, MIXED:MIXED + RW], r.rearrange("p h d -> p (h d)"),
                                  proj[:, n, RG:SQ], ALU.mult).then_inc(finished, 1)

            def split_lo(q):
                dve.wait_ge(hi_done, q + 1)
                dve.tensor_tensor(w_lo[q % RING][:, :, :], raw[q % 2][:, :, :], w_hi[q % RING][:, :, :].bitcast(F32),
                                  ALU.subtract).then_inc(lo_done, 1)

            def mixed_part(j):
                kc = mixed_chunks[j]
                dve.wait_ge(mixed_hi, j + 1)
                dve.tensor_tensor(hT_lo[:, kc, :], psum[mixed_banks[j]][:, :], hT_hi[:, kc, :].bitcast(F32),
                                  ALU.subtract).then_inc(mixed_lo, 1)

            def add_unit(u):
                q, pair = parts_of(u)
                at = res[:, 2 * pair:2 * pair + 2, q % PANELS * PW:(q % PANELS + 1) * PW]
                dve.wait_ge(unit_full, u + 1)
                if u >= 2 * PANELS:
                    dve.wait_ge(unit_added, 2 * PANELS)
                dve.tensor_tensor(at, unit_bank(u)[:, :].rearrange("p (t d) -> p t d", t=2), at, ALU.add)\
                   .then_inc(unit_added, 1)

            weigh_keys(0)
            chain.step(dve.memset(state[:, :, :, :], 0.0))
            chain.settle()
            for j in range(HC):
                mixed_part(j)
            split_lo(0)
            for n in range(TB):
                decay_scores(n, 0)
                decay_scores(n, 1)
                add_unit(2 * n)
                if n + 1 < TB:
                    weigh_queries(n + 1)
                    if n + 1 < TB - 1:
                        weigh_keys(n + 1)
                if n:
                    statistics(n - 1)
                if n == 0:
                    split_lo(1)
                if n + 1 < TB:
                    add_unit(2 * n + 1)
                    update_state(n)
                    split_lo(n + 2)
                if n >= 2:
                    finish(n - 2)
            finish(TB - 2)
            statistics(TB - 1)
            finish(TB - 1)
            split_lo(TB + 1)
            add_unit(2 * TB - 1)
            for j in range(HC, KC):
                mixed_part(j)
            for q in range(TB + 2, HPANELS):
                split_lo(q)
            last = 2 * PANELS + PANELS
            for u in range(2 * PANELS, last + 1):
                add_unit(u)
            next_hT.means(dve, 0)
            add_unit(last + 1)
            next_hT.scale(dve, 0)
            for u in range(last + 2, UNITS):
                add_unit(u)

        @block.scalar
        def _(act):
            def copy_turned(n):
                for part, dst in enumerate((rqT, rkT)):
                    act.wait_ge(turn_full, 2 * n + part + 1)
                    act.activation(dst[:, :, tokens(n)], psum[6 + part][:, :].rearrange("p (a i) -> p a i", a=PAIRS),
                                   ACT.Copy).then_inc(turn_copied, 1)

            def root(n):
                act.wait_ge(inv_done, n + 1)
                act.activation(stats[:, n, 5, :], stats[:, n, 4, :], ACT.Sqrt).then_inc(root_done, 1)

            def split_hi(q):
                act.wait_ge(landed[q % 2], q // 2 * 16 + 16)
                if q >= RING:
                    act.wait_ge(unit_full, 2 * (q - RING) + 2)
                act.activation(w_hi[q % RING][:, :, :], raw[q % 2][:, :, :], ACT.Copy).then_inc(hi_done, 1)

            def mixed_part(j):
                act.wait_ge(mixed_turned, j + 1)
                act.activation(hT_hi[:, mixed_chunks[j], :], psum[mixed_banks[j]][:, :], ACT.Copy)\
                   .then_inc(mixed_hi, 1)

            copy_turned(0)
            for j in range(HC):
                mixed_part(j)
            split_hi(0)
            split_hi(1)
            act.activation(proj[:, :, RG:SQ], proj[:, :, RG:SQ], ACT.Silu).then_inc(silu_done, 1)
            for n in range(TB):
                if n + 1 < TB:
                    copy_turned(n + 1)
                    split_hi(n + 2)
                if n:
                    root(n - 1)
                act.wait_ge(out_full, n + 1)
                act.activation(ret[:, n, :, :].rearrange("p h d -> p (h d)"), psum[4][:, :],
                               ACT.Copy).then_inc(out_copied, 1)
            split_hi(TB + 1)
            root(TB - 1)
            for j in range(HC, KC):
                mixed_part(j)
            for q in range(TB + 2, HPANELS):
                split_hi(q)
            act.wait_ge(unit_added, 2 * PANELS + PANELS)
            next_hT.roots(act, 0)


def choose_experts(nc, sem, psum, qT, keys_t, picks, early):
    K = EARLY_PER_BLOCK
    SCORES_AT = K - 3
    EXP_AT = K - 2
    first = early.first
    pick_i1, pick_i2, pick_gate = picks
    with ExitStack() as ctx:
        def sb(name, shape, dt=F32):
            return ctx.enter_context(nc.sbuf_tensor(name, shape, dt))

        keys = sb("keys", [P, 2, KEYS])
        q_next = sb("q_next", [P, HALVES, P])
        top_s = sb("top_s", [P, HALVES, TOPK])
        top_i = sb("top_i", [P, HALVES, TOPK], U32)
        QUAD = 4
        top_f = sb("top_f", [P, 2, TOPK, PH, QUAD], F16)
        rest = sb("rest", [P, HALVES, KEYS])
        cand = sb("cand", [P, PH, CANDS])
        crest = sb("crest", [P, PH, CANDS])
        best = sb("best", [P, PH, TOPK])
        pos = sb("pos", [P, PH, TOPK], U32)
        pos_ab = sb("pos_ab", [P, 4, PICKS], U32)
        pos_f = sb("pos_f", [P, 4, PICKS], F16)
        pos_all = sb("pos_all", [P, PICKS], F16)
        iota_i = sb("iota16_i", [P, TOPK], I32)
        iota = sb("iota16", [P, TOPK, PICKS], F16)
        hit = [sb(f"hit{i}", [P, TOPK, PICKS], F16) for i in range(2)]
        gap, expd = sb("gap", [P, PH, TOPK]), sb("expd", [P, PH, TOPK])
        total, inv = sb("gate_total", [P, PH]), sb("gate_inv", [P, PH])
        loaded, iota_done, sc_full, sc_free = sem("keys_loaded"), sem("iota_done"), sem("sc_full"), sem("sc_free")
        q_copied = sem("q_copied")
        gap_ready, exp_ready, steps = sem("gap_ready"), sem("exp_ready"), sem("topk_steps")
        block = ctx.enter_context(nc.Block())

        @block.sync
        def _(sp):
            sp.dma_start(keys[:, :, :], keys_t).then_inc(loaded, 16)
            sp.sem_inc(early.spilled[0], 16)
            sp.sem_inc(early.spilled[1], 16)
            first.load(sp, (0, K, 2))
            with sp.Fori(0, TB) as tb:
                for c in range(K):
                    early.sync(sp, (tb, K, c))

        @block.gpsimd
        def _(pool):
            pool.iota(iota_i[:, :], pattern=[[1, TOPK]], base=0, channel_multiplier=0).then_inc(iota_done, 1)
            with pool.Fori(0, TB - 1) as tb:
                pool.wait_ge(sc_full, tb + 1)
                pool.dma_start(q_next[:, :, :], qT[:, :, bass.ds(tb * P + P, P)]).then_inc(q_copied, 16)

        @block.tensor
        def _(pe):
            def scores(q):
                for hp in range(HALVES):
                    last = pe.matmul(psum[hp // 4][:, (hp % 4) * KEYS:(hp % 4 + 1) * KEYS],
                                     q[:, hp, :],
                                     keys[:, hp % 2, :], start=True, stop=True)
                last.then_inc(sc_full, 1)

            pe.sem_inc(first.full, 2)
            pe.wait_ge(loaded, 16)
            scores(qT[:, :, 0:P])
            with pe.Fori(0, TB - 1) as tb:
                for c in range(K):
                    early.tensor(pe, (tb, K, c))
                    if c == SCORES_AT:
                        pe.wait_ge(sc_free, tb + 1)
                        pe.wait_ge(q_copied, tb * 16 + 16)
                        scores(q_next)
            for c in range(K):
                early.tensor(pe, (0, K, (TB - 1) * K + c))

        @block.scalar
        def _(act):
            act.sem_inc(first.gelu_done, 2)
            first.split_hi(act, (0, K, 0))
            with act.Fori(0, TB) as tb:
                for c in range(K):
                    if c == EXP_AT:
                        act.wait_ge(gap_ready, tb + 1)
                        act.activation(expd[:, :, :], gap[:, :, :], ACT.Exp).then_inc(exp_ready, 1)
                    early.scalar(act, (tb, K, c))

        @block.vector
        def _(dve):
            settled = sem("topk_settled")
            chain = Chain(dve, steps, settled)

            def score(hp):
                return psum[hp // 4][:, (hp % 4) * KEYS:(hp % 4 + 1) * KEYS]

            dve.wait_ge(iota_done, 1)
            chain.step(dve.tensor_copy(iota[:, :, :], iota_i[:, :].unsqueeze(2).broadcast_to([P, TOPK, PICKS])))
            chain.settle()
            dve.sem_inc(first.lo_done, 2)
            first.split_lo(dve, (0, K, 0))
            PER_BLOCK = 5 * HALVES + 4 + 5 * PH + 20
            base = chain.n
            with dve.Fori(0, TB) as tb:
                chain.off = tb * PER_BLOCK
                beside = iter(range(K))

                def early_step():
                    early.vector(dve, (tb, K, next(beside)))

                early_step()
                dve.wait_ge(sc_full, tb + 1)
                dve.sem_inc(settled, 1)
                for hp in range(HALVES):
                    chain.step(dve.max(top_s[:, hp, 0:8], score(hp)))
                early_step()
                chain.settle()
                for hp in range(HALVES):
                    chain.step(dve.max_index(top_i[:, hp, 0:8], top_s[:, hp, 0:8], score(hp)))
                for hp in range(HALVES):
                    if hp == HALVES // 2:
                        early_step()
                        dve.sem_inc(settled, 1)
                    chain.step(dve.match_replace(rest[:, hp, :], top_s[:, hp, 0:8], score(hp), NEG))
                chain.settle()
                dve.sem_inc(sc_free, 1)
                for hp in range(HALVES):
                    chain.step(dve.max(top_s[:, hp, 8:16], rest[:, hp, :]))
                early_step()
                chain.settle()
                for hp in range(HALVES):
                    chain.step(dve.max_index(top_i[:, hp, 8:16], top_s[:, hp, 8:16], rest[:, hp, :]))
                early_step()
                s4 = top_s[:, :, :].rearrange("p (h two) k -> p h two k", two=2)
                whole = FULL_A * TOPK
                for at, n_a, n_b, a0 in ((cand[:, :, 0:whole], FULL_A, TOPK, 0),
                                         (cand[:, :, whole:], TOPK - FULL_A, FULL_A, FULL_A)):
                    chain.step(dve.tensor_tensor(at.rearrange("p h (a b) -> p h a b", a=n_a),
                                                 s4[:, :, 0, a0:a0 + n_a].unsqueeze(3).broadcast_to([P, PH, n_a, n_b]),
                                                 s4[:, :, 1, 0:n_b].unsqueeze(2).broadcast_to([P, PH, n_a, n_b]), ALU.add))
                chain.settle()
                for half in range(2):
                    chain.step(dve.tensor_copy(top_f[:, half, :, :, :],
                                               top_i[:, :, :].rearrange("p (h two) a -> p two a h", two=2)[:, half, :, :]
                                               .unsqueeze(3).broadcast_to([P, TOPK, PH, QUAD])))
                for h in range(PH):
                    chain.step(dve.max(best[:, h, 0:8], cand[:, h, :]))
                chain.settle()
                for h in range(PH):
                    chain.step(dve.max_index(pos[:, h, 0:8], best[:, h, 0:8], cand[:, h, :]))
                early_step()
                dve.sem_inc(settled, 1)
                for h in range(PH):
                    chain.step(dve.match_replace(crest[:, h, :], best[:, h, 0:8], cand[:, h, :], NEG))
                chain.settle()
                for h in range(PH):
                    chain.step(dve.max(best[:, h, 8:16], crest[:, h, :]))
                chain.settle()
                for h in range(PH):
                    chain.step(dve.max_index(pos[:, h, 8:16], best[:, h, 8:16], crest[:, h, :]))
                dve.tensor_tensor(gap[:, :, :], best[:, :, :], best[:, :, 0:1].broadcast_to([P, PH, TOPK]),
                                  ALU.subtract).then_inc(gap_ready, 1)
                early_step()
                chain.settle()
                p2 = pos[:, :, :].rearrange("p h k -> p (h k)")
                for i, (amount, op) in enumerate(((4, ALU.logical_shift_right), (TOPK - 1, ALU.bitwise_and),
                                                  (2, ALU.logical_shift_right), (FULL_A - 1, ALU.bitwise_and))):
                    chain.step(dve.tensor_scalar(pos_ab[:, i, :], p2, amount, None, op))
                chain.settle()
                chain.step(dve.tensor_copy(pos_f[:, :, :], pos_ab[:, :, :]))
                chain.step(dve.tensor_copy(pos_all[:, :], p2))
                chain.settle()
                chain.step(dve.tensor_scalar(pos_all[:, :], pos_all[:, :], float(whole), None, ALU.is_ge))
                chain.step(dve.tensor_scalar(pos_f[:, 2, :], pos_f[:, 2, :], float(whole // FULL_A - FULL_A), None,
                                             ALU.subtract))
                chain.settle()
                chain.step(dve.tensor_tensor(pos_f[:, 2:4, :], pos_f[:, 2:4, :], pos_f[:, 0:2, :], ALU.subtract))
                chain.settle()
                chain.step(dve.tensor_tensor(pos_f[:, 2:4, :], pos_f[:, 2:4, :],
                                             pos_all[:, :].unsqueeze(1).broadcast_to([P, 2, PICKS]), ALU.mult))
                chain.settle()
                chain.step(dve.tensor_tensor(pos_f[:, 0:2, :], pos_f[:, 0:2, :], pos_f[:, 2:4, :], ALU.add))
                chain.settle()
                for half in range(2):
                    chain.step(dve.tensor_tensor(hit[half][:, :, :],
                                                 pos_f[:, half, :].unsqueeze(1).broadcast_to([P, TOPK, PICKS]),
                                                 iota[:, :, :], ALU.is_equal))
                chain.settle()
                early_step()
                for half in range(2):
                    at = hit[half][:, :, :].rearrange("p a (h o i) -> p (a h) o i", h=PH, i=QUAD)
                    chain.step(dve.tensor_tensor(at, at, top_f[:, half, :, :, :].rearrange("p a h i -> p (a h) i")
                                                 .unsqueeze(2).broadcast_to([P, TOPK * PH, TOPK // QUAD, QUAD]),
                                                 ALU.mult))
                chain.settle()
                for half, dst in enumerate((pick_i1, pick_i2)):
                    chain.step(dve.tensor_reduce(dst[:, bass.ds(tb, 1), :].rearrange("p o k -> p (o k)"),
                                                 hit[half][:, :, :].rearrange("p a k -> p k a"), AX.X, ALU.add))
                    early_step()
                dve.wait_ge(exp_ready, tb + 1)
                chain.step(dve.tensor_reduce(total[:, :], expd[:, :, :], AX.X, ALU.add))
                chain.settle()
                chain.step(dve.reciprocal(inv[:, :], total[:, :]))
                chain.settle()
                chain.step(dve.tensor_tensor(pick_gate[:, bass.ds(tb, 1), :]
                                             .rearrange("p o (h k) -> p (o h) k", h=PH), expd[:, :, :],
                                             inv[:, :].unsqueeze(2).broadcast_to([P, PH, TOPK]), ALU.mult))
                chain.settle()
                assert chain.n - base == PER_BLOCK and next(beside, None) is None, chain.n - base


def spread_gates(nc, sem, psum, picks, ident, gates_dram, stored, early):
    CH = SEQ // TCH
    QUADS = TCH // 4
    FOUR = len(EARLY_OF_CHUNK)
    START = EARLY_PER_BLOCK * TB
    BANKS = 4
    K = sum(EARLY_OF_CHUNK)
    assert START + K * CH // FOUR == EARLY
    with ExitStack() as ctx:
        def sb(name, shape, dt=F32):
            return ctx.enter_context(nc.sbuf_tensor(name, shape, dt))

        i1T, i2T, gT_hi, gT_lo = (sb(n, [P, SEQ], F16) for n in ("i1T", "i2T", "gT_hi", "gT_lo"))
        iota = sb("iota128", [P, KEYS, 4], F16)
        hot1, hot2_hi, hot2_lo = ([sb(f"{n}{b}", [P, QUADS, KEYS, 4], F16) for b in range(2)]
                                  for n in ("hot1_", "hot2hi_", "hot2lo_"))
        hot2 = sb("hot2", [P, QUADS, KEYS, 4], F16)
        iota_i = hot2[:, 0:2, :, :].rearrange("p q k w -> p (q k w)").bitcast(I32)
        stage = [sb(f"stage{b}", [P, KEYS, TCH], F32) for b in range(2)]
        turned, iota_done, cols_done, steps = sem("picks_turned"), sem("iota128_done"), sem("cols_done"), sem("hot_steps")
        hots_ready, quad_full, quad_free = sem("hots_ready"), sem("quad_full"), sem("quad_free")
        stage_full = sem("stage_full")
        block = ctx.enter_context(nc.Block())

        def early_tiles(four, b):
            at = START + sum(EARLY_OF_CHUNK[:b])
            return [(four, K, c) for c in range(at, at + EARLY_OF_CHUNK[b])]

        @block.gpsimd
        def _(pool):
            pool.iota(iota_i, pattern=[[1, KEYS], [0, 4]], base=0, channel_multiplier=0)\
                .then_inc(iota_done, 1)
            with pool.Fori(0, CH // FOUR) as four:
                for b in range(FOUR):
                    for tile in early_tiles(four, b):
                        early.vector(pool, tile)

        @block.vector
        def _(dve):
            dve.wait_ge(iota_done, 1)
            dve.tensor_copy(iota[:, :, :].rearrange("p k f -> p (k f)"), iota_i).then_inc(cols_done, 1)
            for n, dst in enumerate((i1T, i2T, gT_hi)):
                dve.wait_ge(turned, n + 1)
                dve.tensor_scalar(dst[:, :], psum[n][:, :], GATE_SCALE if n == 2 else 1.0, None,
                                  ALU.mult).then_inc(cols_done, 1)
            dve.wait_ge(cols_done, 4)
            dve.scalar_tensor_tensor(out=gT_lo[:, :], in0=psum[2][:, :], scalar=GATE_SCALE, in1=gT_hi[:, :],
                                     op0=ALU.mult, op1=ALU.subtract).then_inc(cols_done, 1)
            dve.wait_ge(cols_done, 5)
            def rows(t0, src):
                return src[:, bass.ds(t0, TCH)].rearrange("p (q f) -> p q f", f=4).unsqueeze(2)\
                    .broadcast_to([P, QUADS, KEYS, 4])

            keys_row = iota[:, :, :].unsqueeze(1).broadcast_to([P, QUADS, KEYS, 4])
            with dve.Fori(0, CH // FOUR) as four:
                for b in range(FOUR):
                    chunk, h = four * FOUR + b, b % 2
                    t0, done = chunk * TCH, chunk * 4
                    dve.wait_ge(quad_full, (chunk + 1) * QUADS)
                    dve.tensor_tensor(hot1[h][:, :, :, :], rows(t0, i1T), keys_row, ALU.is_equal).then_inc(steps, 1)
                    dve.tensor_tensor(hot2[:, :, :, :], rows(t0, i2T), keys_row, ALU.is_equal).then_inc(steps, 1)
                    dve.wait_ge(steps, done + 2)
                    dve.tensor_tensor(hot2_hi[h][:, :, :, :], hot2[:, :, :, :], rows(t0, gT_hi),
                                      ALU.mult).then_inc(steps, 1)
                    dve.tensor_tensor(hot2_lo[h][:, :, :, :], hot2[:, :, :, :], rows(t0, gT_lo),
                                      ALU.mult).then_inc(steps, 1)
                    dve.wait_ge(steps, done + 4)
                    dve.sem_inc(hots_ready, 1)

        @block.tensor
        def _(pe):
            for n, src in enumerate(picks):
                for tb in range(TB):
                    last = pe.transpose(psum[n][:, tb * P:(tb + 1) * P], src[:, tb, :], ident[:, :])
                last.then_inc(turned, 1)
            pe.sem_inc(quad_full, 2 * QUADS)
            with pe.Fori(0, CH // FOUR) as four:
                for b in range(FOUR):
                    for tile in early_tiles(four, b):
                        early.tensor(pe, tile)
                    chunk, h = four * FOUR + b, b % 2
                    pe.wait_ge(hots_ready, chunk + 1)
                    for q in range(QUADS):
                        bank = psum[q % BANKS]
                        pe.wait_ge(quad_free, chunk * QUADS + q + 1)
                        for f in range(4):
                            out = bank[:, f * KEYS:(f + 1) * KEYS]
                            pe.matmul(out, hot1[h][:, q, :, f], hot2_hi[h][:, q, :, f], start=True, stop=False)
                            last = pe.matmul(out, hot1[h][:, q, :, f], hot2_lo[h][:, q, :, f], start=False, stop=True)
                        last.then_inc(quad_full, 1)

        @block.scalar
        def _(act):
            act.preload_act_table(ACT.Gelu)
            act.sem_inc(quad_free, BANKS)
            act.sem_inc(stored[0], 16)
            act.sem_inc(stored[1], 16)
            with act.Fori(0, CH // FOUR) as four:
                for b in range(FOUR):
                    for tile in early_tiles(four, b):
                        early.scalar(act, tile)
                    chunk, h = four * FOUR + b, b % 2
                    act.wait_ge(stored[h], four * (FOUR // 2 * 16) + (b // 2 + 1) * 16)
                    for q in range(QUADS):
                        act.wait_ge(quad_full, (chunk + 2) * QUADS + q + 1)
                        act.activation(stage[h][:, :, 4 * q:4 * q + 4].rearrange("p k f -> p f k"),
                                       psum[q % BANKS][:, :].rearrange("p (f k) -> p f k", f=4), ACT.Copy,
                                       scale=1.0 / GATE_SCALE).then_inc(quad_free, 1)
                    act.wait_ge(quad_free, (chunk + 1) * QUADS + BANKS)
                    act.sem_inc(stage_full, 1)

        @block.sync
        def _(sp):
            with sp.Fori(0, CH // FOUR) as four:
                for b in range(FOUR):
                    for tile in early_tiles(four, b):
                        early.sync(sp, tile)
                    chunk, h = four * FOUR + b, b % 2
                    sp.wait_ge(stage_full, chunk + 1)
                    sp.dma_start(gates_dram[bass.ds(chunk, 1), :, :, :].rearrange("o p k t -> (o p) k t"),
                                 stage[h][:, :, :]).then_inc(stored[h], 16)


def evaluate_experts(nc, sem, psum, res, spare, first, early, stored, peer_v, gates_dram, next_hT):
    G = GROUP
    RING = 2 * G
    OUTS = TB * D // BANK
    Y_BANKS = 4
    TBL = SEQ // TCH
    PRELOADED, PRESPLIT = 3, 1
    with ExitStack() as ctx:
        def sb(name, shape, dt=F32):
            return ctx.enter_context(nc.sbuf_tensor(name, shape, dt))

        v_raw = [spare[:, i, :] for i in range(2)]
        gelu_early = [spare[:, 2 + i // 2, i % 2 * SEQ:(i % 2 + 1) * SEQ] for i in range(G)]
        v_hi = [sb(f"v_hi{i}", [P, D], F32R) for i in range(RING)]
        v_lo = [sb(f"v_lo{i}", [P, D], F32R) for i in range(RING)]
        a_hi = [sb(f"a_hi{i}", [P, SEQ], F32R) for i in range(RING)]
        a_lo = [sb(f"a_lo{i}", [P, SEQ], F32R) for i in range(RING)]
        gates = [sb(f"gates{i}", [P, TBL, G, TCH]) for i in range(2)]
        v_in, g_in, early_in = ([sem(f"{n}_in{i}") for i in range(many)]
                                for n, many in (("v", 2), ("gate", 2), ("early", G)))
        v_hi_done, v_lo_done = sem("v_hi_done"), sem("v_lo_done")
        gated, a_hi_done, a_lo_done = sem("gated"), sem("a_hi_done"), sem("a_lo_done")
        y_full, y_added = sem("y_full"), sem("y_added")
        block = ctx.enter_context(nc.Block())

        def count(m, c, per=1):
            return m * (RING * per) + c * per if c or not isinstance(m, int) or m else 0

        def reached(eng, semaphore, value):
            if not isinstance(value, int) or value > 0:
                eng.wait_ge(semaphore, value)

        def late(c):
            return c % RING < G

        def tile_of(m, c):
            return m, G, c // RING * G + (EARLY + c % RING if late(c) else c % RING - G)

        def v_landed(m, c):
            return m * (RING // 2 * 16) + (c // 2 + 1) * 16

        def once_landed(m, c):
            return m * 16 + (c // RING + 1) * 16

        def activations(c):
            return first.out[c % 2][:, :] if late(c) else gelu_early[c % G]

        @block.sync
        def _(sp):
            def load_v(m, c):
                reached(sp, v_lo_done, count(m, c - 1))
                sp.dma_start(v_raw[c % 2], peer_v[bass.ds(first.number(tile_of(m, c)), 1), :, :]
                             .rearrange("o p d -> (o p) d")).then_inc(v_in[c % 2], 16)

            def load_gates(m, c):
                reached(sp, gated, count(m, c - G))
                sp.dma_start(gates[c // G % 2][:, :, :, :], gates_dram[:, :, bass.ds(first.number(tile_of(m, c)), G), :]
                             .rearrange("b p k t -> p b k t")).then_inc(g_in[c // G % 2], 16)

            def load(m, c):
                if late(c) and c > PRELOADED:
                    first.load(sp, tile_of(m, c))
                if c % G == 0:
                    load_gates(m, c)
                load_v(m, c)
                if not late(c):
                    reached(sp, a_lo_done, count(m, c - RING + 1))
                    sp.dma_start(gelu_early[c % G], early.dram[bass.ds(first.number(tile_of(m, c)), 1), :, :]
                                 .rearrange("o p t -> (o p) t")).then_inc(early_in[c % G], 16)

            for c in range(G):
                load_v(0, c)
                if c == 1:
                    first.load(sp, tile_of(0, PRELOADED))
            for b in range(2):
                early.wait_stored(sp, b)
                sp.wait_ge(stored[b], SEQ // TCH // 2 * 16 + 16)
            load_gates(0, 0)
            for c in range(G, RING):
                load(0, c)
            with sp.Fori(0, TILES // RING - 1) as ring:
                for c in range(RING):
                    load(ring, RING + c)

        def slots(eng, front, back):
            with eng.Fori(0, TILES // RING - 1) as ring:
                for c in range(RING, 2 * RING):
                    if late(c):
                        front(ring, c)
                    back(ring, c - 1)
            back(0, TILES - 1)

        @block.scalar
        def _(act):
            def front(m, c):
                first.split_hi(act, tile_of(m, c))

            def split_v(m, c):
                r = c % RING
                if r % G == 0:
                    reached(act, y_full, count(m, c - RING + G, OUTS // G))
                act.wait_ge(v_in[c % 2], v_landed(m, c))
                act.activation(v_hi[r][:, :], v_raw[c % 2], ACT.Copy).then_inc(v_hi_done, 1)

            def back(m, c, first_group=False):
                r = c % RING
                if not first_group:
                    split_v(m, c)
                if late(c) and not (first_group and c < 2):
                    reached(act, a_lo_done, count(m, c - 1 if r >= 2 else c - 1 - G))
                    first.gelu(act, tile_of(m, c))
                act.wait_ge(gated, count(m, c + 1))
                act.activation(a_hi[r][:, :], activations(c), ACT.Copy).then_inc(a_hi_done, 1)

            act.preload_act_table(ACT.Gelu)
            for c in range(PRESPLIT, G):
                front(0, c)
                for v in ((0, 1), (2,), (3,))[c - PRESPLIT]:
                    split_v(0, v)
                if c <= 2:
                    early.wait_stored(act, c - 1)
                    first.gelu(act, tile_of(0, c - 1))
            for c in range(RING - 1):
                back(0, c, first_group=c < G)
            slots(act, front, back)
            act.wait_ge(y_added, TILES * OUTS // G - OUTS // 2)
            next_hT.roots(act, 0)

        @block.vector
        def _(dve):
            def add_output(m, c, n):
                dve.wait_ge(y_full, count(m, c // G * G - G, OUTS // G) + (n + 1))
                at = res[:, n // 2, n % 2 * BANK:(n % 2 + 1) * BANK]
                dve.tensor_tensor(at, psum[n % Y_BANKS][:, :], at, ALU.add).then_inc(y_added, 1)

            def front(m, c):
                first.split_lo(dve, tile_of(m, c))

            def split_v(m, c):
                r = c % RING
                dve.wait_ge(v_hi_done, count(m, c + 1))
                dve.tensor_tensor(v_lo[r][:, :], v_raw[c % 2], v_hi[r][:, :].bitcast(F32),
                                  ALU.subtract).then_inc(v_lo_done, 1)

            def back(m, c, first_group=False):
                r = c % RING
                if not first_group:
                    split_v(m, c)
                if late(c):
                    dve.wait_ge(first.gelu_done, first.number(tile_of(m, c)) + 3)
                else:
                    dve.wait_ge(early_in[c % G], once_landed(m, c))
                if c % G == 0:
                    dve.wait_ge(g_in[c // G % 2], once_landed(m, c))
                a = activations(c)
                by_block = a.rearrange("p (b t) -> p b t", b=TBL)
                dve.tensor_tensor(by_block, by_block, gates[c // G % 2][:, :, c % G, :], ALU.mult).then_inc(gated, 1)
                dve.wait_ge(a_hi_done, count(m, c + 1))
                dve.tensor_tensor(a_lo[r][:, :], a, a_hi[r][:, :].bitcast(F32),
                                  ALU.subtract).then_inc(a_lo_done, 1)
                if c >= G:
                    for n in range(2 * (r % G), 2 * (r % G) + 2):
                        add_output(m, c, n)

            for c in range(PRESPLIT, G):
                front(0, c)
                for v in ((0, 1), (2,), (3,))[c - PRESPLIT]:
                    split_v(0, v)
            for c in range(RING - 1):
                back(0, c, first_group=c < G)
            slots(dve, front, back)
            for n in range(OUTS):
                add_output(0, TILES, n)
                if n == OUTS // 2:
                    next_hT.means(dve, 0)
                if n == OUTS // 2 + 1:
                    next_hT.scale(dve, 0)

        @block.tensor
        def _(pe):
            def output(m, c, n):
                r = c % RING
                if n == 0:
                    pe.wait_ge(v_lo_done, count(m, c + G))
                    pe.wait_ge(a_lo_done, count(m, c + G))
                reached(pe, y_added, count(m, c, OUTS // G) + (n + 1 - Y_BANKS))
                t, d = slice(n // 2 * P, (n // 2 + 1) * P), slice(n % 2 * BANK, (n % 2 + 1) * BANK)
                split_product(pe, psum[n % Y_BANKS][:, :],
                              [((a_hi[r + i][:, t], a_lo[r + i][:, t]), (v_hi[r + i][:, d], v_lo[r + i][:, d]))
                               for i in range(G)]).then_inc(y_full, 1)

            def slot(m, c):
                if late(c):
                    first.product(pe, tile_of(m, c))
                if c >= G:
                    for n in range(2 * (c % G), 2 * (c % G) + 2):
                        output(m, c // G * G - G, n)

            for c in range(RING):
                slot(0, c)
            with pe.Fori(0, TILES // RING - 1) as ring:
                for c in range(RING, 2 * RING):
                    slot(ring, c)
            for n in range(OUTS):
                output(0, TILES - G, n)


def add_embedding(nc, sem, psum, res, hT, p_t, w_gate, w_ple, out):
    PC = PLE // P
    with ExitStack() as ctx:
        def sb(name, shape, dt=F32):
            return ctx.enter_context(nc.sbuf_tensor(name, shape, dt))

        hT_hi, hT_lo = hT.hT_hi, hT.hT_lo
        p_raw, p_hi, p_lo = sb("p_raw", [P, PC, SEQ]), sb("p_hi", [P, PC, SEQ], F32R), sb("p_lo", [P, PC, SEQ], F32R)
        e_raw, e_hi, e_lo = sb("e_raw", [P, PC, D]), sb("e_hi", [P, PC, D], F32R), sb("e_lo", [P, PC, D], F32R)
        g_raw = [sb(f"g_raw{i}", [P, KC, PW]) for i in range(PANELS)]
        g_hi = [sb(f"g_hi{i}", [P, KC, PW], F32R) for i in range(PANELS)]
        g_lo = [sb(f"g_lo{i}", [P, KC, PW], F32R) for i in range(PANELS)]
        gates = list(zip(g_raw, g_hi, g_lo))
        splits = gates[:1] + [(p_raw, p_hi, p_lo), (e_raw, e_hi, e_lo)] + gates[1:]
        sources = [w_gate[0], p_t, w_ple] + [w_gate[i] for i in range(1, PANELS)]
        EMBEDDING = 3
        sig = [sb(f"sig{i}", [P, 2, PW]) for i in range(4)]
        loaded = [sem(f"ple_loaded{i}") for i in range(len(splits))]
        hi_done, lo_done, emb_full, gate_full, sig_done, mult_done, sum_done, stored = (
            sem("ple_hi"), sem("ple_lo"), sem("emb_full"), sem("gate_full"), sem("sig_done"), sem("mult_done"),
            sem("sum_done"), sem("out_stored"))
        units = [(i, half) for i in range(PANELS) for half in range(TB // 2)]
        block = ctx.enter_context(nc.Block())

        def place(n):
            i, half = units[n]
            return res[:, 2 * half:2 * half + 2, i * PW:(i + 1) * PW]

        def halves(bank):
            return bank[:, :].rearrange("p (t d) -> p t d", t=2)

        @block.sync
        def _(sp):
            for n, (raw, _, _) in enumerate(splits):
                sp.dma_start(raw[:, :, :], sources[n]).then_inc(loaded[n], 16)
            for n, (i, half) in enumerate(units):
                sp.wait_ge(sum_done, n + 1)
                sp.dma_start(out[2 * half * P:(2 * half + 2) * P, i * PW:(i + 1) * PW].rearrange("(t p) d -> p t d", p=P),
                             place(n)).then_inc(stored, 16)
            sp.wait_ge(stored, 16 * len(units))

        @block.scalar
        def _(act):
            def split(n):
                raw, hi, _ = splits[n]
                act.wait_ge(loaded[n], 16)
                act.activation(hi[:, :, :], raw[:, :, :], ACT.Copy).then_inc(hi_done, 1)

            hT.roots(act, 1)
            split(0)
            hT.scalar(act)
            for n in range(1, EMBEDDING + 1):
                split(n)
            for n in range(len(units)):
                if n % 2 == 0 and EMBEDDING + 1 + n // 2 < len(splits):
                    split(EMBEDDING + 1 + n // 2)
                act.wait_ge(gate_full, n + 1)
                if n >= 4:
                    act.wait_ge(sum_done, n - 3)
                act.activation(sig[n % 4][:, :, :], halves(psum[n % 4]), ACT.Sigmoid).then_inc(sig_done, 1)

        @block.vector
        def _(dve):
            def split(n):
                raw, hi, lo = splits[n]
                dve.wait_ge(hi_done, n + 1)
                dve.tensor_tensor(lo[:, :, :], raw[:, :, :], hi[:, :, :].bitcast(F32), ALU.subtract)\
                   .then_inc(lo_done, 1)

            hT.means(dve, 1)
            hT.scale(dve, 1)
            split(0)
            hT.vector(dve)
            for n in range(1, EMBEDDING + 1):
                split(n)
            for n in range(len(units)):
                if n % 2 == 0 and EMBEDDING + 1 + n // 2 < len(splits):
                    split(EMBEDDING + 1 + n // 2)
                dve.wait_ge(sig_done, n + 1)
                dve.wait_ge(emb_full, n + 1)
                dve.tensor_tensor(sig[n % 4][:, :, :], halves(psum[4 + n % 4]), sig[n % 4][:, :, :], ALU.mult)\
                   .then_inc(mult_done, 1)
                dve.wait_ge(mult_done, n + 1)
                dve.tensor_tensor(place(n), place(n), sig[n % 4][:, :, :], ALU.add).then_inc(sum_done, 1)

        @block.tensor
        def _(pe):
            def embedding(n):
                i, half = units[n]
                if n >= 4:
                    pe.wait_ge(mult_done, n - 3)
                for t in range(2):
                    rows = slice((2 * half + t) * P, (2 * half + t + 1) * P)
                    last = split_product(pe, psum[4 + n % 4][:, t * PW:(t + 1) * PW],
                                         [((p_hi[:, c, rows], p_lo[:, c, rows]),
                                           (e_hi[:, c, i * PW:(i + 1) * PW], e_lo[:, c, i * PW:(i + 1) * PW]))
                                          for c in range(PC)])
                last.then_inc(emb_full, 1)

            def gate(n):
                i, half = units[n]
                pe.wait_ge(lo_done, EMBEDDING + i if i else 1)
                if n >= 4:
                    pe.wait_ge(mult_done, n - 3)
                for t in range(2):
                    rows = slice((2 * half + t) * P, (2 * half + t + 1) * P)
                    last = split_product(pe, psum[n % 4][:, t * PW:(t + 1) * PW],
                                         [((hT_hi[:, c, rows], hT_lo[:, c, rows]), (g_hi[i][:, c, :], g_lo[i][:, c, :]))
                                          for c in range(KC)], made=(hT.lo_done, 0) if (n, t) == (0, 0) else None)
                last.then_inc(gate_full, 1)

            hT.tensor(pe)
            AHEAD = 2
            for n in range(AHEAD):
                gate(n)
            pe.wait_ge(lo_done, EMBEDDING)
            for n in range(len(units)):
                embedding(n)
                if n + AHEAD < len(units):
                    gate(n + AHEAD)


def kernel(x, p, g_mix, w_in, q_norm, k_norm, sinks, w_out, g_ffn,
           peer_w_query, peer_sub_keys, peer_u, peer_v, g_ple, w_ple_gate, w_ple_proj):
    import numpy as np
    import concourse.bacc as bacc
    from concourse.bass_utils import run_bass_kernel_spmd

    def panels(w, chunks, n, width):
        return np.asarray(w).reshape(chunks, P, n, width).transpose(2, 1, 0, 3)

    def half_panels(w):
        w = np.asarray(w).reshape(2, KC // 2, P, PANELS, PW).transpose(0, 3, 2, 1, 4)
        return w[::-1].reshape(2 * PANELS, P, KC // 2, PW)

    def column(g):
        return np.asarray(g).reshape(KC, P).T

    heads = np.arange(RH)
    gamma = 1.0 - np.exp2(-5.0 - heads)
    idx = np.arange(P)
    rel = idx[None, :] - idx[:, None]
    decay = np.where(rel[:, None, :] >= 0, gamma[None, :, None] ** np.maximum(rel, 0)[:, None, :], 0.0) * HD ** -0.5
    wq = np.repeat(gamma[:, None] ** (idx + 1)[None, :], HD, axis=0).reshape(RH // 2, P, P).transpose(1, 0, 2)
    wk = gamma[None, :] ** (P - 1 - idx)[:, None] * HD ** -0.5
    chunk = np.repeat(gamma ** P, HD).reshape(RH // 2, P).T
    half = HD // 2
    freqs = (np.float32(10000.0) ** (-np.arange(half, dtype=np.float32) / np.float32(half))).astype(np.float32)
    ang = np.arange(SEQ, dtype=np.float32)[:, None] * freqs[None, :]
    cos, sin = (f(ang).reshape(TB, P, half).transpose(1, 0, 2) for f in (np.cos, np.sin))
    back = idx[:, None] + P - np.arange(2 * P)[None, :]
    mask = np.where((back >= 0) & (back < P), 0.0, -1.0e30)

    arrays = {
        "x": np.asarray(x)[0], "p_t": np.asarray(p)[0, 0].T.reshape(PLE // P, P, SEQ).transpose(1, 0, 2),
        "g_mix": column(g_mix), "w_in": panels(np.roll(np.asarray(w_in), IN_W - SQ, axis=-1), KC, WIN_PANELS + RET_PANELS, PW),
        "q_norm": np.tile(np.asarray(q_norm)[0], 2)[:, None], "k_norm": np.tile(np.asarray(k_norm)[0], 2)[:, None],
        "sinks": np.broadcast_to(np.asarray(sinks)[0], (P, QH)), "w_out": half_panels(w_out),
        "g_ffn": column(g_ffn), "w_query": panels(peer_w_query, KC, 2 * PANELS, PW),
        "keys_t": np.asarray(peer_sub_keys)[0].transpose(2, 0, 1),
        "peer_u": np.asarray(peer_u)[0].reshape(KEYS, KEYS, KC, P).transpose(1, 3, 2, 0),
        "peer_v": np.asarray(peer_v)[0].reshape(KEYS, KEYS, D).transpose(1, 0, 2),
        "g_ple": column(g_ple), "w_gate": panels(w_ple_gate, KC, PANELS, PW),
        "w_ple": np.asarray(w_ple_proj).reshape(PLE // P, P, D).transpose(1, 0, 2),
        "ident_c": np.eye(P, dtype=np.float32),
        "cos_c": cos, "sin_c": sin, "decay_c": decay[:, [0, 2, 4, 6, 1, 3, 5, 7]].astype(np.float32), "wq_c": wq.astype(np.float32),
        "wk_c": wk.astype(np.float32), "chunk_c": chunk.astype(np.float32), "mask_c": mask.astype(np.float32),
    }
    arrays = {n: np.ascontiguousarray(a) for n, a in arrays.items()}
    nc = bacc.Bacc("TRN2", target_bir_lowering=False, num_devices=1)
    args = {n: nc.dram_tensor(n, a.shape, mybir.dt.from_np(a.dtype), kind="ExternalInput").ap()
            for n, a in arrays.items()}
    out = nc.dram_tensor("out", (SEQ, D), F32, kind="ExternalOutput").ap()
    hybrid_layer(nc, out=out, **args)
    r = run_bass_kernel_spmd(nc, [arrays], core_ids=[0])
    return np.asarray(r.results[0]["out"]).reshape(1, SEQ, D)
```
